# Optimizing a Trainium2 kernel written in Bass

```python
import math
import jax, jax.numpy as jnp
from jax import lax
import numpy as np

D_MODEL = 1024
BATCH = 1
SEQ = 512
DEPTH = 1

EPS = 1e-6
POOL_WINDOWS = (2, 4, 8, 16)
POOL_GROUPS = 4
POOL_WIDTH = D_MODEL // 2
POOL_GROUP_DIM = POOL_WIDTH // POOL_GROUPS
DN_HEADS = 8
DN_HEAD_DIM = 128
DN_WIDTH = DN_HEADS * DN_HEAD_DIM
CONV_WIDTH = 4
CHUNK = 64
PEER_HEADS = 8
N_KEYS = 128
N_EXPERTS = N_KEYS * N_KEYS
PEER_TOPK = 16
PEER_HALF = 128
PEER_QUERY_DIM = 2 * PEER_HALF
PEER_BLOCK = 64
SPLIT_POINTS = (
    POOL_WIDTH,
    POOL_WIDTH + 3 * DN_WIDTH,
    POOL_WIDTH + 4 * DN_WIDTH,
    POOL_WIDTH + 4 * DN_WIDTH + DN_HEADS,
    POOL_WIDTH + 4 * DN_WIDTH + 2 * DN_HEADS,
    POOL_WIDTH + 4 * DN_WIDTH + 2 * DN_HEADS + D_MODEL,
)
IN_COLS = POOL_WIDTH + 4 * DN_WIDTH + 2 * DN_HEADS + 2 * D_MODEL


def rmsnorm(x, w):
    xf = x.astype(jnp.float32)
    y = xf * lax.rsqrt(jnp.mean(xf * xf, axis=-1, keepdims=True) + EPS)
    return (y * w.astype(jnp.float32)).astype(x.dtype)

def l2norm(x):
    return x * lax.rsqrt(jnp.sum(x * x, axis=-1, keepdims=True) + EPS)

def pool_mixer(xa, pool_w, pool_scale):
    b, s, _ = xa.shape
    xf = xa.astype(jnp.float32)
    csum = jnp.cumsum(xf, axis=1)
    count = jnp.arange(1, s + 1, dtype=jnp.float32)[None, :, None]
    groups = []
    for g, win in enumerate(POOL_WINDOWS):
        sl = slice(g * POOL_GROUP_DIM, (g + 1) * POOL_GROUP_DIM)
        c = csum[..., sl]
        c_lag = jnp.pad(c, ((0, 0), (win, 0), (0, 0)))[:, :s]
        mean = (c - c_lag) / jnp.minimum(count, float(win))
        groups.append(mean - xf[..., sl])
    pooled = jnp.stack(groups, axis=2)
    y = jnp.einsum("bsgc,gcd->bsgd", pooled, pool_w.astype(jnp.float32))
    y = y.reshape(b, s, POOL_WIDTH) * pool_scale.astype(jnp.float32)
    return y.astype(xa.dtype)

def causal_dwconv(x, w):
    s = x.shape[1]
    k = w.shape[0]
    xp = jnp.pad(x, ((0, 0), (k - 1, 0), (0, 0)))
    y = xp[:, 0:s] * w[0]
    for j in range(1, k):
        y = y + xp[:, j:j + s] * w[j]
    return y

def gated_delta_rule(q, k, v, g, beta):
    b, h, s, dk = q.shape
    dv = v.shape[-1]
    nc = s // CHUNK
    q = q * (dk ** -0.5)
    k_beta = k * beta[..., None]
    v_beta = v * beta[..., None]

    def chunks(t):
        return t.reshape(b, h, nc, CHUNK, t.shape[-1])

    q, k, k_beta, v_beta = chunks(q), chunks(k), chunks(k_beta), chunks(v_beta)
    gc = jnp.cumsum(g.reshape(b, h, nc, CHUNK), axis=-1)
    tril = jnp.tril(jnp.ones((CHUNK, CHUNK), dtype=bool))
    strict = jnp.tril(jnp.ones((CHUNK, CHUNK), dtype=bool), -1)
    diff = gc[..., :, None] - gc[..., None, :]
    decay = jnp.where(tril, jnp.exp(jnp.where(tril, diff, 0.0)), 0.0)
    lower = jnp.where(strict, jnp.einsum("bhnid,bhnjd->bhnij", k_beta, k) * decay, 0.0)
    eye = jnp.eye(CHUNK, dtype=jnp.float32)
    t_inv = lax.linalg.triangular_solve(eye + lower, jnp.broadcast_to(eye, lower.shape),
                                        left_side=True, lower=True, unit_diagonal=True)
    u = jnp.einsum("bhnij,bhnjd->bhnid", t_inv, v_beta)
    w = jnp.einsum("bhnij,bhnjd->bhnid", t_inv, k_beta * jnp.exp(gc)[..., None])
    attn = jnp.where(tril, jnp.einsum("bhnid,bhnjd->bhnij", q, k) * decay, 0.0)

    def step(state, inp):
        q_i, k_i, u_i, w_i, a_i, g_i = inp
        v_new = u_i - jnp.einsum("bhcd,bhde->bhce", w_i, state)
        o = (jnp.einsum("bhcd,bhde->bhce", q_i * jnp.exp(g_i)[..., None], state)
             + jnp.einsum("bhij,bhje->bhie", a_i, v_new))
        g_last = g_i[..., -1]
        k_dec = k_i * jnp.exp(g_last[..., None] - g_i)[..., None]
        state = state * jnp.exp(g_last)[..., None, None] + jnp.einsum("bhcd,bhce->bhde", k_dec, v_new)
        return state, o

    xs = tuple(jnp.moveaxis(t, 2, 0) for t in (q, k, u, w, attn, gc))
    state0 = jnp.zeros((b, h, dk, dv), dtype=jnp.float32)
    _, o = lax.scan(step, state0, xs)
    return jnp.moveaxis(o, 0, 2).reshape(b, h, s, dv)

def deltanet_branch(qkv, z, beta_logit, a_logit, conv_w, a_log, dt_bias, dn_norm_w):
    b, s, _ = qkv.shape
    out_dtype = qkv.dtype
    f32 = jnp.float32
    qkv = jax.nn.silu(causal_dwconv(qkv.astype(f32), conv_w.astype(f32)))
    q, k, v = jnp.split(qkv, 3, axis=-1)

    def heads(t):
        return t.reshape(b, s, DN_HEADS, DN_HEAD_DIM).transpose(0, 2, 1, 3)

    q = l2norm(heads(q))
    k = l2norm(heads(k))
    v = heads(v)
    beta = jax.nn.sigmoid(beta_logit.astype(f32)).transpose(0, 2, 1)
    g = (-jnp.exp(a_log.astype(f32))
         * jax.nn.softplus(a_logit.astype(f32) + dt_bias.astype(f32))).transpose(0, 2, 1)
    o = gated_delta_rule(q, k, v, g, beta).transpose(0, 2, 1, 3)
    zf = z.astype(f32).reshape(b, s, DN_HEADS, DN_HEAD_DIM)
    o = rmsnorm(o, dn_norm_w) * jax.nn.silu(zf)
    return o.reshape(b, s, DN_WIDTH).astype(out_dtype)

def peer_ffn(x, w_query, keys_1, keys_2, expert_down, expert_up):
    b, s, d = x.shape
    f32 = jnp.float32
    q = (x @ w_query).astype(f32).reshape(b, s, PEER_HEADS, 2, PEER_HALF)
    s1 = jnp.einsum("bshc,hkc->bshk", q[..., 0, :], keys_1.astype(f32))
    s2 = jnp.einsum("bshc,hkc->bshk", q[..., 1, :], keys_2.astype(f32))
    v1, i1 = lax.top_k(s1, PEER_TOPK)
    v2, i2 = lax.top_k(s2, PEER_TOPK)
    cand_score = (v1[..., :, None] + v2[..., None, :]).reshape(b, s, PEER_HEADS, PEER_TOPK * PEER_TOPK)
    cand_idx = (i1[..., :, None] * N_KEYS + i2[..., None, :]).reshape(b, s, PEER_HEADS, PEER_TOPK * PEER_TOPK)
    top_score, pos = lax.top_k(cand_score, PEER_TOPK)
    experts = jnp.take_along_axis(cand_idx, pos, axis=-1)
    gates = jax.nn.softmax(top_score, axis=-1)

    nb = s // PEER_BLOCK
    xb = x.reshape(b, nb, PEER_BLOCK, d).transpose(1, 0, 2, 3)
    eb = experts.reshape(b, nb, PEER_BLOCK, PEER_HEADS, PEER_TOPK).transpose(1, 0, 2, 3, 4)
    gb = gates.reshape(b, nb, PEER_BLOCK, PEER_HEADS, PEER_TOPK).transpose(1, 0, 2, 3, 4)

    def block(args):
        xi, ei, gi = args
        u = jnp.take(expert_down, ei, axis=0)
        act = jax.nn.gelu(jnp.einsum("btd,bthkd->bthk", xi, u).astype(f32), approximate=False)
        vv = jnp.take(expert_up, ei, axis=0)
        return jnp.einsum("bthk,bthkd->btd", (gi * act).astype(x.dtype), vv)

    y = lax.map(block, (xb, eb, gb))
    return y.transpose(1, 0, 2, 3).reshape(b, s, d)

def first_inputs(seed: int = 0) -> dict:
    key = jax.random.key(seed)
    ks = jax.random.split(key, 20)
    f32 = jnp.float32

    def nrm(k, shape, scale):
        return scale * jax.random.normal(k, shape, f32)

    def gain(k, shape):
        return 1.0 + 0.05 * jax.random.normal(k, shape, f32)

    dt = jnp.exp(jax.random.uniform(ks[7], (DEPTH, DN_HEADS), f32, math.log(1e-3), math.log(1e-1)))
    dt_bias = dt + jnp.log(-jnp.expm1(-dt))
    a_log = jnp.log(jax.random.uniform(ks[8], (DEPTH, DN_HEADS), f32, 1.0, 16.0))
    return {
        "x": jax.random.normal(ks[0], (BATCH, SEQ, D_MODEL), f32),
        "mix_norm_w": gain(ks[1], (DEPTH, D_MODEL)),
        "w_in": nrm(ks[2], (DEPTH, D_MODEL, IN_COLS), D_MODEL ** -0.5),
        "pool_w": nrm(ks[3], (DEPTH, POOL_GROUPS, POOL_GROUP_DIM, POOL_GROUP_DIM), POOL_GROUP_DIM ** -0.5),
        "pool_scale": 1.0 + 0.1 * jax.random.normal(ks[4], (DEPTH, POOL_WIDTH), f32),
        "conv_w": nrm(ks[5], (DEPTH, CONV_WIDTH, 3 * DN_WIDTH), CONV_WIDTH ** -0.5),
        "a_log": a_log,
        "dt_bias": dt_bias,
        "dn_norm_w": gain(ks[6], (DEPTH, DN_HEAD_DIM)),
        "w_pool_up": nrm(ks[9], (DEPTH, POOL_WIDTH, D_MODEL), POOL_WIDTH ** -0.5),
        "w_dn_up": nrm(ks[10], (DEPTH, DN_WIDTH, D_MODEL), DN_WIDTH ** -0.5),
        "w_mix_out": nrm(ks[11], (DEPTH, D_MODEL, D_MODEL), D_MODEL ** -0.5),
        "ffn_norm_w": gain(ks[12], (DEPTH, D_MODEL)),
        "peer_w_query": nrm(ks[13], (DEPTH, D_MODEL, PEER_HEADS * PEER_QUERY_DIM), D_MODEL ** -0.5),
        "peer_keys_1": nrm(ks[14], (DEPTH, PEER_HEADS, N_KEYS, PEER_HALF), PEER_HALF ** -0.5),
        "peer_keys_2": nrm(ks[15], (DEPTH, PEER_HEADS, N_KEYS, PEER_HALF), PEER_HALF ** -0.5),
        "peer_down": nrm(ks[16], (DEPTH, N_EXPERTS, D_MODEL), D_MODEL ** -0.5),
        "peer_up": nrm(ks[17], (DEPTH, N_EXPERTS, D_MODEL), PEER_HEADS ** -0.5),
        "final_norm_w": gain(ks[18], (D_MODEL,)),
    }

def first_block(x, mix_norm_w, w_in, pool_w, pool_scale, conv_w, a_log, dt_bias, dn_norm_w,
              w_pool_up, w_dn_up, w_mix_out, ffn_norm_w, peer_w_query, peer_keys_1,
              peer_keys_2, peer_down, peer_up, final_norm_w):
    h = x
    for l in range(DEPTH):
        xn = rmsnorm(h, mix_norm_w[l])
        proj = xn @ w_in[l]
        xa, qkv, z, beta_logit, a_logit, gate_a, gate_b = jnp.split(proj, SPLIT_POINTS, axis=-1)
        y_a = pool_mixer(xa, pool_w[l], pool_scale[l]) @ w_pool_up[l]
        y_b = deltanet_branch(qkv, z, beta_logit, a_logit, conv_w[l], a_log[l], dt_bias[l],
                              dn_norm_w[l]) @ w_dn_up[l]
        merged = jax.nn.sigmoid(gate_a) * y_a + jax.nn.sigmoid(gate_b) * y_b
        h = h + merged @ w_mix_out[l]
        h = h + peer_ffn(rmsnorm(h, ffn_norm_w[l]), peer_w_query[l], peer_keys_1[l],
                         peer_keys_2[l], peer_down[l], peer_up[l])
    return rmsnorm(h, final_norm_w)


HEAD_DIM = 64
NSA_HEADS = 8
NSA_KV_HEADS = 2
SWA_HEADS = 8
SWA_KV_HEADS = 2
CMP_BLOCK = 32
CMP_STRIDE = 16
CMP_HIDDEN = 256
SLC_BLOCK = 64
N_SELECT = 16
NSA_WINDOW = 512
SWA_WINDOW = 128
Q_BLOCK = 128
RMS_EPS = 1e-6
NEG = -1e30
BIG = 1e30
NSA_WIDTH = NSA_HEADS * HEAD_DIM
SWA_WIDTH = SWA_HEADS * HEAD_DIM
KV_NSA = NSA_KV_HEADS * HEAD_DIM
KV_SWA = SWA_KV_HEADS * HEAD_DIM
SPLIT_SIZES = (NSA_WIDTH, 2 * KV_NSA, 2 * KV_NSA, 2 * KV_NSA, 3 * NSA_HEADS, NSA_WIDTH,
               SWA_WIDTH, 2 * KV_SWA, SWA_WIDTH, 2 * D_MODEL)
D_IN = sum(SPLIT_SIZES)


def split_points():
    pts, acc = [], 0
    for s in SPLIT_SIZES[:-1]:
        acc += s
        pts.append(acc)
    return pts

def alibi_slopes(n, n_kv):
    s = 2.0 ** (-8.0 * (np.arange(n) + 1) / n)
    return jnp.asarray(s, dtype=jnp.float32).reshape(n_kv, n // n_kv)

def rms_norm(x, g):
    xf = x.astype(jnp.float32)
    y = xf * lax.rsqrt(jnp.mean(xf * xf, axis=-1, keepdims=True) + RMS_EPS)
    return (y * g.astype(jnp.float32)).astype(x.dtype)

def q_heads(t, n_kv, r):
    B, S, _ = t.shape
    return t.reshape(B, S, n_kv, r, HEAD_DIM).transpose(0, 2, 3, 1, 4)

def kv_heads(t, n_kv):
    B, S, _ = t.shape
    return t.reshape(B, S, n_kv, HEAD_DIM).transpose(0, 2, 1, 3)

def merge_heads(o):
    B, G, r, S, dh = o.shape
    return o.transpose(0, 3, 1, 2, 4).reshape(B, S, G * r * dh)

def banded_attention(q, k, v, slopes, window, sinks=None):
    B, G, r, S, dh = q.shape
    nprev = window // Q_BLOCK
    nqb = S // Q_BLOCK
    lk = (nprev + 1) * Q_BLOCK
    pad = nprev * Q_BLOCK
    kp = jnp.pad(k, ((0, 0), (0, 0), (pad, 0), (0, 0)))
    vp = jnp.pad(v, ((0, 0), (0, 0), (pad, 0), (0, 0)))
    idx = jnp.arange(nqb)[:, None] * Q_BLOCK + jnp.arange(lk)[None, :]
    kb = kp[:, :, idx].astype(jnp.float32)
    vb = vp[:, :, idx].astype(jnp.float32)
    qb = q.reshape(B, G, r, nqb, Q_BLOCK, dh).astype(jnp.float32)
    s = jnp.einsum('bgrnqd,bgnkd->bgrnqk', qb, kb) * (dh ** -0.5)
    qpos = jnp.arange(nqb)[:, None] * Q_BLOCK + jnp.arange(Q_BLOCK)[None, :]
    kpos = idx - pad
    dist = qpos[:, :, None] - kpos[:, None, :]
    valid = (dist >= 0) & (dist < window) & (kpos[:, None, :] >= 0)
    s = s - slopes[None, :, :, None, None, None] * dist.astype(jnp.float32)
    s = jnp.where(valid, s, NEG)
    if sinks is not None:
        sink = jnp.broadcast_to(sinks.astype(jnp.float32).reshape(1, G, r, 1, 1, 1), s.shape[:-1] + (1,))
        p = jax.nn.softmax(jnp.concatenate([s, sink], axis=-1), axis=-1)[..., :-1]
    else:
        p = jax.nn.softmax(s, axis=-1)
    o = jnp.einsum('bgrnqk,bgnkd->bgrnqd', p, vb)
    return o.reshape(B, G, r, S, dh).astype(q.dtype)

def compress_blocks(t, pe, w1, w2):
    B, G, S, dh = t.shape
    nc = (S - CMP_BLOCK) // CMP_STRIDE + 1
    idx = jnp.arange(nc)[:, None] * CMP_STRIDE + jnp.arange(CMP_BLOCK)[None, :]
    blk = t[:, :, idx] + pe
    flat = blk.reshape(B, G, nc, CMP_BLOCK * dh)
    return jax.nn.silu(flat @ w1) @ w2

def compressed_attention(q, kc, vc, slopes):
    B, G, r, S, dh = q.shape
    nc = kc.shape[2]
    s = jnp.einsum('bgrqd,bgcd->bgrqc', q.astype(jnp.float32), kc.astype(jnp.float32)) * (dh ** -0.5)
    end = jnp.arange(nc) * CMP_STRIDE + CMP_BLOCK - 1
    dist = jnp.arange(S)[:, None] - end[None, :]
    valid = dist >= 0
    s = s - slopes[None, :, :, None, None] * dist.astype(jnp.float32)
    s = jnp.where(valid, s, NEG)
    p = jax.nn.softmax(s, axis=-1) * jnp.any(valid, axis=-1)[:, None].astype(jnp.float32)
    o = jnp.einsum('bgrqc,bgcd->bgrqd', p, vc.astype(jnp.float32))
    return o.astype(q.dtype), p

def select_blocks(p_cmp):
    p = p_cmp.sum(axis=2)
    S, nc = p.shape[2], p.shape[3]
    nsb = S // SLC_BLOCK
    ratio = SLC_BLOCK // CMP_STRIDE
    span = CMP_BLOCK // CMP_STRIDE
    offs = (jnp.arange(ratio)[:, None] + jnp.arange(span)[None, :]).reshape(-1)
    cidx = ratio * jnp.arange(nsb)[:, None] - offs[None, :]
    ok = (cidx >= 0) & (cidx < nc)
    imp = jnp.where(ok, p[..., jnp.clip(cidx, 0, nc - 1)], 0.0).sum(axis=-1)
    cur = jnp.arange(S) // SLC_BLOCK
    j = jnp.arange(nsb)
    causal = j[None, :] <= cur[:, None]
    forced = (j[None, :] == 0) | (j[None, :] == cur[:, None]) | (j[None, :] == cur[:, None] - 1)
    score = jnp.where(causal & forced, BIG, jnp.where(causal, imp, NEG))
    _, idx = lax.top_k(score, min(N_SELECT, nsb))
    return idx

def selected_attention(q, k, v, blk_idx, slopes):
    B, G, r, S, dh = q.shape
    nsb = S // SLC_BLOCK
    n_sel = blk_idx.shape[-1]
    nqc = S // Q_BLOCK
    kb = k.reshape(B, G, nsb, SLC_BLOCK, dh)
    vb = v.reshape(B, G, nsb, SLC_BLOCK, dh)
    qc = q.reshape(B, G, r, nqc, Q_BLOCK, dh).transpose(3, 0, 1, 2, 4, 5)
    ic = blk_idx.reshape(B, G, nqc, Q_BLOCK, n_sel).transpose(2, 0, 1, 3, 4)
    qpos = jnp.arange(S).reshape(nqc, Q_BLOCK)
    gather = jax.vmap(jax.vmap(lambda blocks, ix: blocks[ix]))

    def one_block(args):
        q_i, ix, qp = args
        k_sel = gather(kb, ix).astype(jnp.float32)
        v_sel = gather(vb, ix).astype(jnp.float32)
        kpos = ix[..., None] * SLC_BLOCK + jnp.arange(SLC_BLOCK)
        dist = (qp[None, None, :, None, None] - kpos)[:, :, None]
        s = jnp.einsum('bgrqd,bgqnkd->bgrqnk', q_i.astype(jnp.float32), k_sel) * (dh ** -0.5)
        s = s - slopes[None, :, :, None, None, None] * dist.astype(jnp.float32)
        s = jnp.where(dist >= 0, s, NEG).reshape(B, G, r, Q_BLOCK, n_sel * SLC_BLOCK)
        p = jax.nn.softmax(s, axis=-1)
        return jnp.einsum('bgrqk,bgqkd->bgrqd', p, v_sel.reshape(B, G, Q_BLOCK, n_sel * SLC_BLOCK, dh))

    o = lax.map(one_block, (qc, ic, qpos))
    return o.transpose(1, 2, 3, 0, 4, 5).reshape(B, G, r, S, dh).astype(q.dtype)

def second_inputs(seed: int = 0) -> dict:
    key = jax.random.key(seed)
    ks = jax.random.split(key, 20)
    D, L, dh = D_MODEL, DEPTH, HEAD_DIM
    nrm = lambda k, shape, fan: jax.random.normal(k, shape, jnp.float32) * (fan ** -0.5)
    return {
        'x': jax.random.normal(ks[0], (BATCH, SEQ, D), jnp.float32),
        'c': jax.random.normal(ks[1], (BATCH, D), jnp.float32),
        'w_ada': nrm(ks[2], (L, D, 3 * D), D) * 0.5,
        'b_ada': 0.01 * jax.random.normal(ks[3], (L, 3 * D), jnp.float32),
        'g_pre': 1.0 + 0.05 * jax.random.normal(ks[4], (L, D), jnp.float32),
        'g_post': 1.0 + 0.05 * jax.random.normal(ks[5], (L, D), jnp.float32),
        'w_in': nrm(ks[6], (L, D, D_IN), D),
        'pe_cmp_k': 0.02 * jax.random.normal(ks[7], (L, CMP_BLOCK, dh), jnp.float32),
        'pe_cmp_v': 0.02 * jax.random.normal(ks[8], (L, CMP_BLOCK, dh), jnp.float32),
        'w_cmp_k1': nrm(ks[9], (L, CMP_BLOCK * dh, CMP_HIDDEN), CMP_BLOCK * dh),
        'w_cmp_k2': nrm(ks[10], (L, CMP_HIDDEN, dh), CMP_HIDDEN),
        'w_cmp_v1': nrm(ks[11], (L, CMP_BLOCK * dh, CMP_HIDDEN), CMP_BLOCK * dh),
        'w_cmp_v2': nrm(ks[12], (L, CMP_HIDDEN, dh), CMP_HIDDEN),
        'w_o_nsa': nrm(ks[13], (L, NSA_WIDTH, D), NSA_WIDTH),
        'w_o_swa': nrm(ks[14], (L, SWA_WIDTH, D), SWA_WIDTH),
        'w_out': nrm(ks[15], (L, D, D), D),
        'sinks': jax.random.normal(ks[16], (L, SWA_HEADS), jnp.float32),
    }

def second_block(x, c, w_ada, b_ada, g_pre, g_post, w_in, pe_cmp_k, pe_cmp_v, w_cmp_k1, w_cmp_k2,
              w_cmp_v1, w_cmp_v2, w_o_nsa, w_o_swa, w_out, sinks):
    B, S, D = x.shape
    ra = NSA_HEADS // NSA_KV_HEADS
    rb = SWA_HEADS // SWA_KV_HEADS
    slopes_a = alibi_slopes(NSA_HEADS, NSA_KV_HEADS)
    slopes_b = alibi_slopes(SWA_HEADS, SWA_KV_HEADS)
    pts = split_points()
    for l in range(DEPTH):
        mod = c @ w_ada[l] + b_ada[l]
        shift, scale, gate = jnp.split(mod, 3, axis=-1)
        h = rms_norm(x, g_pre[l]) * (1.0 + scale[:, None, :]) + shift[:, None, :]
        proj = h @ w_in[l]
        q_a, kv_c, kv_s, kv_w, g_nsa, z_a, q_b, kv_b, z_b, merge = jnp.split(proj, pts, axis=-1)

        qa = q_heads(q_a, NSA_KV_HEADS, ra)
        kc_raw, vc_raw = jnp.split(kv_c, 2, axis=-1)
        ks_, vs_ = jnp.split(kv_s, 2, axis=-1)
        kw_, vw_ = jnp.split(kv_w, 2, axis=-1)
        kc = compress_blocks(kv_heads(kc_raw, NSA_KV_HEADS), pe_cmp_k[l], w_cmp_k1[l], w_cmp_k2[l])
        vc = compress_blocks(kv_heads(vc_raw, NSA_KV_HEADS), pe_cmp_v[l], w_cmp_v1[l], w_cmp_v2[l])
        o_cmp, p_cmp = compressed_attention(qa, kc, vc, slopes_a)
        blk_idx = select_blocks(p_cmp)
        o_slc = selected_attention(qa, kv_heads(ks_, NSA_KV_HEADS), kv_heads(vs_, NSA_KV_HEADS), blk_idx, slopes_a)
        o_win = banded_attention(qa, kv_heads(kw_, NSA_KV_HEADS), kv_heads(vw_, NSA_KV_HEADS), slopes_a, NSA_WINDOW)
        gts = jax.nn.sigmoid(g_nsa.reshape(B, S, 3, NSA_KV_HEADS, ra)).transpose(2, 0, 3, 4, 1)[..., None]
        o_a = gts[0] * o_cmp + gts[1] * o_slc + gts[2] * o_win
        y_a = (merge_heads(o_a) * jax.nn.silu(z_a)) @ w_o_nsa[l]

        qb = q_heads(q_b, SWA_KV_HEADS, rb)
        kb_, vb_ = jnp.split(kv_b, 2, axis=-1)
        o_b = banded_attention(qb, kv_heads(kb_, SWA_KV_HEADS), kv_heads(vb_, SWA_KV_HEADS), slopes_b,
                               SWA_WINDOW, sinks=sinks[l])
        y_b = (merge_heads(o_b) * jax.nn.silu(z_b)) @ w_o_swa[l]

        m_a, m_b = jnp.split(merge, 2, axis=-1)
        y = (jax.nn.sigmoid(m_a) * y_a + jax.nn.sigmoid(m_b) * y_b) @ w_out[l]
        x = x + gate[:, None, :] * rms_norm(y, g_post[l])
    return x


def setup_inputs(seed=0):
    out = dict(first_inputs(seed))
    for name, value in second_inputs(seed + 1).items():
        if name != "x":
            out[name + "_2"] = value
    return out


def reference(
    x, mix_norm_w, w_in, pool_w, pool_scale, conv_w, a_log, dt_bias, dn_norm_w, w_pool_up,
    w_dn_up, w_mix_out, ffn_norm_w, peer_w_query, peer_keys_1, peer_keys_2, peer_down, peer_up,
    final_norm_w, c_2, w_ada_2, b_ada_2, g_pre_2, g_post_2, w_in_2, pe_cmp_k_2, pe_cmp_v_2,
    w_cmp_k1_2, w_cmp_k2_2, w_cmp_v1_2, w_cmp_v2_2, w_o_nsa_2, w_o_swa_2, w_out_2, sinks_2,
):
    x = first_block(
        x, mix_norm_w, w_in, pool_w, pool_scale, conv_w, a_log, dt_bias, dn_norm_w, w_pool_up,
        w_dn_up, w_mix_out, ffn_norm_w, peer_w_query, peer_keys_1, peer_keys_2, peer_down,
        peer_up, final_norm_w,
    )
    return second_block(
        x, c_2, w_ada_2, b_ada_2, g_pre_2, g_post_2, w_in_2, pe_cmp_k_2, pe_cmp_v_2, w_cmp_k1_2,
        w_cmp_k2_2, w_cmp_v1_2, w_cmp_v2_2, w_o_nsa_2, w_o_swa_2, w_out_2, sinks_2,
    )


_drawn_inputs = setup_inputs


def setup_inputs(seed=0):
    import zlib

    import numpy as np

    out = dict(_drawn_inputs(seed))
    spreads = {}
    factors = {'b_ada_2': 4.03, 'g_post_2': 2.67, 'pe_cmp_k_2': 64.0, 'pe_cmp_v_2': 8.0}
    for name, (base, spread) in spreads.items():
        noise = np.random.default_rng([zlib.crc32(name.encode()), seed]).standard_normal(out[name].shape)
        drawn = base * np.exp(spread * noise) if base else spread * noise
        out[name] = __import__('jax').numpy.asarray(drawn.astype(out[name].dtype))
    for name, factor in factors.items():
        out[name] = (out[name] * factor).astype(out[name].dtype)
    return out
```

```python
import numpy as np
import concourse.bass as bass
from concourse import mybir
from contextlib import ExitStack

D = 1024
S = 512
P = 128
KT = D // P
TT = S // P
HEADS = 8
HD = 128
TOPK = 16
RING = 8
EPS = 1e-6
EXPERTS_A = 128
GROUP = 4
BLOCK_T = 64
NC_CMP = 31
NSA_SCALE = 0.125
LEVELS = 7

CONST = {}
_at = 0
for _n, _w in (("ident", P), ("ones", P), ("upper", P), ("iota", P), ("strict", P), ("block", LEVELS * P),
               ("alibi", S), ("window", 2 * P), ("cmp", TT * NC_CMP), ("seen", TT), ("first", 64), ("eps", 2)):
    CONST[_n] = (_at, _w)
    _at += _w
N_CONST = _at

PARAM = {}
_at = 0
for _n, _w in (("mix_norm_w", KT), ("conv_w", 96), ("pool_scale", 4), ("a_log", 8), ("dt_bias", 8),
               ("dn_norm_w", 1), ("ffn_norm_w", KT), ("final_norm_w", KT), ("c", KT), ("b_ada", 24),
               ("g_pre", KT), ("g_post", KT), ("sinks", 8), ("pe_k", 16), ("pe_v", 16), ("pool_w", 512),
               ("w_ba", KT * 16), ("w_cmp_k2", 128), ("w_cmp_v2", 128)):
    PARAM[_n] = (_at, _w)
    _at += _w
N_PARAM = _at

STREAM = {}
_at = 0
for _n, _w in (("w_in", 52), ("pool_up", 4), ("dn_up", 8), ("mix_out", 8), ("query", 16),
               ("experts", 256), ("ada", 24), ("w_in_2", 37), ("v_tok", 4), ("cmp_k1", 4), ("cmp_v1", 4),
               ("o_nsa", 4), ("o_swa", 4), ("w_out", 8)):
    STREAM[_n] = _at
    _at += _w
N_STREAM = _at


class Steps:

    def __init__(self, sem, names):
        self.sem, self.names = sem, names

    def done(self, rnd, name):
        return rnd * len(self.names) + self.names.index(name) + 1


def program(nc, x_in, stream, params_in, consts_in, keys_in, out):
    f32, u32 = mybir.dt.float32, mybir.dt.uint32
    ALU, ACT, AX = mybir.AluOpType, mybir.ActivationFunctionType, mybir.AxisListType
    ds = bass.ds
    gate_dram = nc.dram_tensor("gate_matrix", [S // BLOCK_T, P, EXPERTS_A, BLOCK_T], f32).ap()

    with ExitStack() as ctx:
        def sb(name, cols, dt=f32):
            return ctx.enter_context(nc.sbuf_tensor(name, [P, cols], dt))

        def sem(name):
            return ctx.enter_context(nc.semaphore(name))

        consts = sb("consts", N_CONST)
        params = sb("params", N_PARAM)
        acts = sb("acts", 2 * KT * S)
        ring = sb("ring", RING * 1024)[:, :].rearrange("p (s n) -> p s n", s=RING)
        RS = sb("rstd", S)
        small = sb("small", 1024)
        work = sb("work", 31600)
        ps = ctx.enter_context(nc.psum_tensor("ps", [P, 8, 512], f32))

        def const(name):
            a, w = CONST[name]
            return consts[:, a:a + w]

        def param(name):
            a, w = PARAM[name]
            return params[:, a:a + w]

        ident, ones, upper, iota = (const(n) for n in ("ident", "ones", "upper", "iota"))

        def view(base, at, *dims):
            n = int(np.prod(dims))
            assert at + n <= base.shape[1], (at, dims)
            v = base[:, at:at + n]
            if len(dims) == 1:
                return v
            names = "abcd"[:len(dims)]
            return v.rearrange(f"p ({' '.join(names)}) -> p {' '.join(names)}", **dict(zip(names, dims)))

        def over(ap, axis, n):
            v = ap.unsqueeze(axis)
            shape = list(v.shape)
            shape[axis] = n
            return v.broadcast_to(shape)

        XT = view(acts, 0, KT, S)
        XN = view(acts, KT * S, KT, S)

        class Region:

            def __init__(self, base, at=0):
                self.base, self.at = base, at

            def take(self, *dims):
                v = view(self.base, self.at, *dims)
                self.at += int(np.prod(dims))
                return v

        sm = Region(small)
        w32 = sm.take(KT)
        ea, beta, a_in, sp_a, sp_b = sm.take(8), sm.take(TT, 8), sm.take(TT, 8), sm.take(TT, 8), sm.take(TT, 8)
        g_log, gc, egc, nbeg = sm.take(TT, 8), sm.take(TT, 8), sm.take(TT, 8), sm.take(TT, 8)
        mod, g_eff = sm.take(24), sm.take(KT)
        mx, nm, den, fac = sm.take(2, TT), sm.take(2, TT), sm.take(2, TT), sm.take(2, TT)
        esink, gn = sm.take(2, TT), sm.take(TT, 24)
        KC, VC = sm.take(64), sm.take(2, 64)
        zero_exp, zero_v, zero_w, RS16 = sm.take(8), sm.take(8), sm.take(8), sm.take(16)

        r1 = Region(work)
        QKV, Z, GT = r1.take(24, S), r1.take(KT, S), r1.take(16, S)
        SIDE = r1.at
        XA, pool_tmp = r1.take(4, 16 + S), r1.take(2, 16 + S)
        RAW, CONV = r1.take(2, 3 + S), r1.take(2, S)

        class Slot:

            def __init__(self, region):
                t = region.take
                self.sq, self.ed, self.et, self.df = t(2, S), t(TT, HD), t(TT, HD), t(TT, HD)
                self.lk, self.t, self.tt, self.vb = t(TT, HD), t(TT, HD), t(TT, HD), t(TT, HD)
                self.kt, self.state, self.r, self.vn = t(TT, HD), t(HD), t(HD), t(HD)
                self.egl, self.edl, self.oss, self.ors = t(TT), t(TT), t(TT), t(TT)
                self.gu = self.sq[:, 0, :].rearrange("p (c t) -> p c t", c=TT)
                self.x = self.sq[:, 1, :].rearrange("p (c t) -> p c t", c=TT)

        slots = [Slot(Region(acts)), Slot(Region(work, SIDE))]

        r2 = Region(work)
        QP, keys = r2.take(16, S), r2.take(16, P)
        SC, SC2, CAND, CAND2 = r2.take(2, TT, P), r2.take(TT, P), r2.take(TT, 256), r2.take(TT, 256)
        CAND_FLAT = CAND.rearrange("p c n -> p (c n)")
        V1, I1, I1F = r2.take(TT, 16, TOPK), r2.take(TT, 16, TOPK), r2.take(TT, 16, TOPK)
        TOP, POS, PF = r2.take(TT, 8, TOPK), r2.take(TT, 8, TOPK), r2.take(2, TT, 8, TOPK)
        SEL, EQ = r2.take(2, TT, 128), r2.take(2, 2048)
        GSUM = r2.take(TT, 8)
        PU = SC2
        TR = Region(work, 31600 - 1536)
        I1T, I2T, GTT = TR.take(S), TR.take(S), TR.take(S)
        r3 = Region(work)
        ONE_A, ONE_B = r3.take(16, P), r3.take(16, P)
        GB = r3.take(2, EXPERTS_A, BLOCK_T)
        r4 = Region(work)
        GG, W, GE = r4.take(2, 8, GROUP, BLOCK_T), r4.take(2, GROUP, S), r4.take(2, S)
        assert max(r2.at, r3.at) <= 31600 - 1536

        r5 = Region(work)
        QA, ZZ, GT2, KD, VT = r5.take(8, S), r5.take(8, S), r5.take(16, S), r5.take(3, 2, S), r5.take(TT, 384)
        at2 = r5.at
        KK, XC, CB, HID = r5.take(5, S), r5.take(2, 2, S), r5.take(2, 16, 62), r5.take(2, 2, 62)
        r6 = Region(work, at2)
        SS, PT, DG = r6.take(2, TT, S), r6.take(2, TT, S), r6.take(2, TT, P)

        w_loaded = [sem(f"w_loaded_{s}") for s in range(RING)]
        tile_done = sem("tile_done")
        bank_free = [sem(f"bank_free_{b}") for b in range(4)]
        x_loaded, par_loaded, keys_loaded = sem("x_loaded"), sem("par_loaded"), sem("keys_loaded")
        v_chain, a_chain, g_chain = sem("v_chain"), sem("a_chain"), sem("g_chain")
        rs_out = sem("rs_out")
        norm_sq, norm_ss, norm_done = sem("norm_sq"), sem("norm_ss"), sem("norm_done")
        pads, conv_part, conv_done, silu_done = sem("pads"), sem("conv_part"), sem("conv_done"), sem("silu_done")
        pool_ready, pooly_done, yt_ready = sem("pool_ready"), sem("pooly_done"), sem("yt_ready")
        ba_done, ba_v, ba_a, gc_done, gc_ready = sem("ba_done"), sem("ba_v"), sem("ba_a"), sem("gc_done"), sem("gc_ready")
        T_STEPS = ["sumsq", "turn", "gram", "decay", "lt", "t1"]
        A_STEPS = ["sq", "root", "ktok", "e", "eg", "lts"]
        V_STEPS = ["norm", "vb", "gu", "diff", "l", "at", "tt", "t"]
        for l in range(1, LEVELS):
            T_STEPS += [f"x{l}", f"tx{l}"]
            A_STEPS += [f"x{l}"]
            V_STEPS += [f"u{l}"]
        for c in range(TT):
            T_STEPS += [f"pq{c}"] * (c > 0) + [f"v{c}", f"os{c}"]
            A_STEPS += [f"vn{c}"]
            V_STEPS += [f"r{c}"] * (c > 0) + [f"s{c}"] * (c < TT - 1) + [f"o{c}"]
        dT = [Steps(sem(f"delta_pe_{p}"), T_STEPS + ["turn_o"]) for p in range(2)]
        dA = [Steps(sem(f"delta_act_{p}"), A_STEPS + ["oroot"]) for p in range(2)]
        dV = [Steps(sem(f"delta_dve_{p}"), V_STEPS + ["dg", "fin"]) for p in range(2)]
        dG = [Steps(sem(f"delta_pool_{p}"), ["edm", "etm", "kdec"] + [f"lk{l}" for l in range(LEVELS)])
              for p in range(2)]
        gated, merged, mixed = sem("gated"), sem("merged"), sem("mixed")
        qp_ready, sc_done, sc_ready, topk_done, cand_ready = (sem(n) for n in (
            "qp_ready", "sc_done", "sc_ready", "topk_done", "cand_ready"))
        cand_used, eq_ready, eq_mul, sel_ready = sem("cand_used"), sem("eq_ready"), sem("eq_mul"), sem("sel_ready")
        i1f_ready = sem("i1f_ready")
        gd_ready, ge_ready, gate_ready = sem("gd_ready"), sem("ge_ready"), sem("gate_ready")
        turned, turned_read = sem("turned"), sem("turned_read")
        onehot, token_mm, gate_out = sem("onehot"), sem("token_mm"), sem("gate_out")
        gate_written = [sem(f"gate_written_{p}") for p in range(2)]
        gate_loaded = [sem(f"gate_loaded_{p}") for p in range(2)]
        gelu_done, w_done, y_done, acc_done = sem("gelu_done"), sem("w_done"), sem("y_done"), sem("acc_done")
        mod_ready = sem("mod_ready")
        k_ready, dup_done, xc_ready, cb_ready = sem("k_ready"), sem("dup_done"), sem("xc_ready"), sem("cb_ready")
        v_ready, hid_ready, kv_done, kc_ready = sem("v_ready"), sem("hid_ready"), sem("kv_done"), sem("kc_ready")
        proj_ready = sem("proj_ready")
        at_scored, at_scaled, at_exp, at_diag = sem("at_scored"), sem("at_scaled"), sem("at_exp"), sem("at_diag")
        at_turned, at_copied, at_out, o_ready = sem("at_turned"), sem("at_copied"), sem("at_out"), sem("o_ready")
        yy_ready, out_ready, out_written = sem("yy_ready"), sem("out_ready"), sem("out_written")

        UNITS = [(kind, h) for h in range(8) for kind in ("cmp", "slc", "win")] + [("swa", h) for h in range(8)]

        def turns(kind):
            if kind == "cmp":
                return [(0, range(TT))]
            if kind == "swa":
                return [(k, range(k, min(k + 2, TT))) for k in range(TT)]
            return [(k, range(k, TT)) for k in range(TT)]

        CHUNKS = [0]
        for kind, _ in UNITS:
            CHUNKS.append(CHUNKS[-1] + len(turns(kind)))
        O_USE = {h: i for i, h in enumerate(range(0, 16, 2))}

        def key_cols(kind, i):
            if kind == "cmp":
                return NC_CMP, 0
            if kind == "swa":
                return (2 * P, (i - 1) * P) if i else (P, 0)
            return (i + 1) * P, 0

        block = ctx.enter_context(nc.Block())

        @block.sync
        def _(sp):
            for s in range(RING):
                sp.dma_start(ring[:, s, :], stream[s, :, :]).then_inc(w_loaded[s], 16)
            loops = (N_STREAM - RING) // RING
            with sp.Fori(0, loops) as i:
                for s in range(RING):
                    sp.wait_ge(tile_done, i * RING + (s + 1))
                    sp.dma_start(ring[:, s, :], stream[ds(i * RING + (RING + s), 1), :, :]
                                 .rearrange("o p n -> p (o n)")).then_inc(w_loaded[s], 16)
            for n in range(RING * (loops + 1), N_STREAM):
                sp.wait_ge(tile_done, n - RING + 1)
                sp.dma_start(ring[:, n % RING, :], stream[n, :, :]).then_inc(w_loaded[n % RING], 16)

        @block.gpsimd
        def _(pool):
            g_ = nc.gpsimd
            count = [0]

            def link(ins):
                count[0] += 1
                ins.then_inc(g_chain, 1)
                pool.wait_ge(g_chain, count[0])

            pool.wait_ge(pads, 1)
            pool.wait_ge(par_loaded, 32)
            first = const("first").rearrange("p (g n) -> p g n", g=4)
            for g in range(4):
                pool.wait_ge(bank_free[g], 1)
                src = XA[:, g, :]
                for x in range(g + 1):
                    dst = pool_tmp[:, x % 2, :]
                    link(g_.tensor_tensor(dst[:, 16:], src[:, 16:], src[:, 16 - 2 ** x:16 + S - 2 ** x], ALU.add))
                    src = dst
                link(g_.tensor_tensor(RS16, src[:, 16:32], first[:, g, :], ALU.mult))
                link(g_.tensor_tensor(RS16, RS16, XA[:, g, 16:32], ALU.subtract))
                link(g_.tensor_scalar(src[:, 16:], src[:, 16:], 1.0 / 2 ** (g + 1), None, ALU.mult))
                link(g_.tensor_tensor(XA[:, g, 16:], src[:, 16:], XA[:, g, 16:], ALU.subtract))
                link(g_.tensor_copy(XA[:, g, 16:32], RS16))
            g_.memset(RS16, 0.0).then_inc(pool_ready, 1)

            own = [0, 0]
            for r in range(HEADS // 2):
                def each(fn, steps=1):
                    for p in range(2):
                        if own[p]:
                            pool.wait_ge(dG[p].sem, own[p])
                        fn(p, 2 * r + p, slots[p])
                        own[p] += steps

                def edm(p, h, s):
                    pool.wait_ge(dA[p].sem, dA[p].done(r, "e"))
                    link(g_.tensor_tensor(s.ed, s.ed, over(const("strict"), 1, TT), ALU.mult))
                    g_.tensor_tensor(s.ed, s.ed, over(beta[:, :, h], 2, P), ALU.mult).then_inc(dG[p].sem, 1)

                def etm(p, h, s):
                    g_.tensor_tensor(s.et, s.et, over(upper, 1, TT), ALU.mult).then_inc(dG[p].sem, 1)
                    pool.wait_ge(dA[p].sem, dA[p].done(r, "eg"))
                    g_.tensor_tensor(s.kt, s.kt, over(s.edl, 2, HD), ALU.mult).then_inc(dG[p].sem, 1)

                each(edm)
                each(etm, 2)
                for l in range(LEVELS):
                    def lk(p, h, s):
                        if l == 0:
                            pool.wait_ge(dA[p].sem, dA[p].done(r, "lts"))
                            if r:
                                pool.wait_ge(dT[p].sem, dT[p].done(r - 1, "turn_o"))
                        elif l == 1:
                            pool.wait_ge(dV[p].sem, dV[p].done(r, "tt"))
                        else:
                            pool.wait_ge(dT[p].sem, dT[p].done(r, f"x{l - 1}"))
                        m = const("block")[:, l * P:(l + 1) * P]
                        g_.tensor_tensor(s.lk, s.df, over(m, 1, TT), ALU.mult).then_inc(dG[p].sem, 1)
                    each(lk)

            for d in range(KT):
                pool.wait_ge(bank_free[d % 4], (60 + d) // 4 + 1)
                last = g_.tensor_tensor(XN[:, d, :], GT[:, d, :], GT[:, 8 + d, :], ALU.add)
            last.then_inc(merged, 1)
            for h in range(8):
                pool.wait_ge(topk_done, 2 * h + 2)
                if h:
                    pool.wait_ge(cand_used, h)
                for c in range(TT):
                    last = g_.tensor_tensor(CAND[:, c, :].rearrange("p (a b) -> p a b", a=16),
                                            over(V1[:, c, 2 * h, :], 2, 16), over(V1[:, c, 2 * h + 1, :], 1, 16), ALU.add)
                last.then_inc(cand_ready, 1)
            pool.wait_ge(i1f_ready, 1)
            for x in range(8):
                c, z = divmod(x, 2)
                pool.wait_ge(eq_ready, x + 1)
                e = EQ[:, x % 2, :].rearrange("p (h k j) -> p h k j", h=8, k=16)
                idx = I1F[:, c, :, :].rearrange("p (h z) j -> p h z j", z=2)[:, :, z, :]
                g_.tensor_tensor(e, e, over(idx, 2, 16), ALU.mult).then_inc(eq_mul, 1)

            def load(g, par):
                pool.dma_start(GG[:, par, :, :, :].rearrange("p c e t -> p c (e t)"),
                               gate_dram[:, :, ds(g * GROUP, GROUP), :].rearrange("c p e t -> p c (e t)"))\
                    .then_inc(gate_loaded[par], 16)

            for par in range(2):
                pool.wait_ge(gate_written[par], 16 * (S // BLOCK_T // 2) + 16)
            load(0, 0)
            load(1, 1)
            with pool.Fori(0, 15) as i:
                pool.wait_ge(w_done, i * 8 + 4)
                load(i * 2 + 2, 0)
                pool.wait_ge(w_done, i * 8 + 8)
                load(i * 2 + 3, 1)

            for m in range(124, 129):
                pool.wait_ge(bank_free[m % 4], m // 4 + 1)
            for g in range(2):
                src = KK[g * 64:(g + 1) * 64, :, :]
                pool.dma_start(XC[0:64, :, g, :], src[:, 0:2, :]).then_inc(xc_ready, 16)
                pool.dma_start(XC[64:128, :, g, 0:S - 1], src[:, 0:2, 1:S]).then_inc(xc_ready, 16)
            for g in range(2):
                src = KK[g * 64:(g + 1) * 64, :, :]
                for half in range(2):
                    pool.dma_start(KD[half * 64:(half + 1) * 64, :, g, :], src[:, 2:5, :]).then_inc(dup_done, 16)
            for d in range(KT):
                pool.wait_ge(bank_free[(137 + d) % 4], (137 + d) // 4 + 1)
                last = g_.tensor_tensor(XN[:, d, :], GT2[:, d, :], GT2[:, 8 + d, :], ALU.add)
            last.then_inc(merged, 1)
            pool.wait_ge(dup_done, 64)

        @block.scalar
        def _(act):
            def link(ins):
                a_count[0] += 1
                ins.then_inc(a_chain, 1)
                act.wait_ge(a_chain, a_count[0])

            a_count = [0]

            def take(m, dst, func, i=None, per=8):
                return nc.scalar.activation(dst, ps[:, m % 4, :], func)

            def square(j, src):
                nc.scalar.activation(view(acts, KT * S, KT * S), src, ACT.Square).then_inc(norm_sq, 1)

            def root(j):
                act.wait_ge(norm_ss, j + 1)
                nc.scalar.activation(RS[:, :], ps[:, 7, :], ACT.Sqrt, bias=const("eps")[:, 1:2]).then_inc(rs_out, 1)

            act.dma_start(view(acts, 0, KT * S), x_in).then_inc(x_loaded, 16)
            act.dma_start(params[:, :], params_in).then_inc(par_loaded, 16)
            act.dma_start(consts[:, :], consts_in).then_inc(par_loaded, 16)
            act.wait_ge(x_loaded, 16)
            square(0, view(acts, 0, KT * S))
            act.wait_ge(par_loaded, 32)
            root(0)
            nc.scalar.activation(ea, param("a_log"), ACT.Exp).then_inc(silu_done, 2)
            for m in range(4):
                act.wait_ge(tile_done, m + 1)
                take(m, XA[:, m, 16:], ACT.Copy).then_inc(bank_free[m % 4], 1)
            with act.Fori(0, 3) as i:
                for u in range(8):
                    act.wait_ge(tile_done, i * 8 + (5 + u))
                    act.wait_ge(conv_done, i * 8 + (u + 1))
                    take(4 + u, RAW[:, u % 2, 3:], ACT.Copy).then_inc(bank_free[u % 4], 1)
                    act.wait_ge(conv_done, i * 8 + (u + 3))
                    nc.scalar.activation(QKV[:, ds(i * 8 + u, 1), :].rearrange("p o t -> p (o t)"),
                                         CONV[:, u % 2, :], ACT.Silu).then_inc(silu_done, 1)
            for u in range(8):
                act.wait_ge(tile_done, 29 + u)
                take(28 + u, Z[:, u, :], ACT.Silu).then_inc(bank_free[u % 4], 1)
            with act.Fori(0, 2) as i:
                for u in range(8):
                    act.wait_ge(tile_done, i * 8 + (37 + u))
                    take(36 + u, GT[:, ds(i * 8 + u, 1), :].rearrange("p o t -> p (o t)"), ACT.Sigmoid)\
                        .then_inc(bank_free[u % 4], 1)
            for g in range(4):
                act.wait_ge(pooly_done, g + 1)
                nc.scalar.activation(XA[:, g, 16:], ps[:, 4 + g, :], ACT.Copy,
                                     scale=param("pool_scale")[:, g:g + 1]).then_inc(yt_ready, 1)
            act.wait_ge(ba_v, 1)
            logits = ps[:, 4, 0:64].rearrange("p (c n) -> p c n", c=TT)
            nc.scalar.activation(beta, logits[:, :, 0:8], ACT.Sigmoid).then_inc(ba_a, 1)
            act.wait_ge(ba_v, 1)
            link(nc.scalar.activation(sp_a, sp_a, ACT.Exp, scale=-1.0))
            nc.scalar.activation(sp_b, sp_a, ACT.Ln, bias=1.0).then_inc(ba_a, 1)
            act.wait_ge(ba_v, 3)
            nc.scalar.activation(egc, gc, ACT.Exp).then_inc(ba_a, 1)

            act.wait_ge(silu_done, 26)
            act.wait_ge(tile_done, 56)
            own = [0, 0]
            for r in range(HEADS // 2):
                def each(fn, steps=1):
                    for p in range(2):
                        if own[p]:
                            act.wait_ge(dA[p].sem, own[p])
                        fn(p, 2 * r + p, slots[p], 4 * p)
                        own[p] += steps

                def four(v):
                    return v.rearrange("p c t -> p (c t)")

                def sq(p, h, s, b):
                    nc.scalar.activation(s.sq[:, 0, :], QKV[:, h, :], ACT.Square)
                    nc.scalar.activation(s.sq[:, 1, :], QKV[:, 8 + h, :], ACT.Square).then_inc(dA[p].sem, 1)

                def root_qk(p, h, s, b):
                    act.wait_ge(dT[p].sem, dT[p].done(r, "sumsq"))
                    nc.scalar.activation(s.sq, ps[:, b:b + 2, :], ACT.Sqrt, bias=const("eps")[:, 0:1])\
                        .then_inc(dA[p].sem, 1)

                def ktok(p, h, s, b):
                    act.wait_ge(dT[p].sem, dT[p].done(r, "turn"))
                    nc.scalar.activation(four(s.kt), ps[:, b, :], ACT.Copy).then_inc(dA[p].sem, 1)

                def e(p, h, s, b):
                    act.wait_ge(dV[p].sem, dV[p].done(r, "diff"))
                    nc.scalar.activation(s.ed, s.ed, ACT.Exp, scale=-1.0)
                    nc.scalar.activation(s.et, s.et, ACT.Exp).then_inc(dA[p].sem, 1)
                    gl = ps[:, b, :].rearrange("p (c t) -> p c t", c=TT)[:, :, P - 1]
                    nc.scalar.activation(s.egl, gl, ACT.Exp)
                    nc.scalar.activation(s.edl, s.df[:, :, P - 1], ACT.Exp).then_inc(dA[p].sem, 1)

                def lts(p, h, s, b):
                    act.wait_ge(dT[p].sem, dT[p].done(r, "lt"))
                    nc.scalar.activation(four(s.df), ps[:, b + 1, :], ACT.Copy).then_inc(dA[p].sem, 1)

                for fn in (sq, root_qk, ktok):
                    each(fn)
                each(e, 2)
                each(lts)
                for l in range(1, LEVELS):
                    def x(p, h, s, b):
                        act.wait_ge(dT[p].sem, dT[p].done(r, f"x{l}"))
                        nc.scalar.activation(four(s.x), ps[:, b, :], ACT.Copy).then_inc(dA[p].sem, 1)
                    each(x)
                for c in range(TT):
                    def vn(p, h, s, b):
                        act.wait_ge(dT[p].sem, dT[p].done(r, f"v{c}"))
                        nc.scalar.activation(s.vn, ps[:, b + 1, 0:P], ACT.Copy).then_inc(dA[p].sem, 1)
                    each(vn)

                def osq(p, h, s, b):
                    act.wait_ge(dV[p].sem, dV[p].done(r, f"o{TT - 1}"))
                    for c in range(TT):
                        last = nc.scalar.activation(s.x[:, c, :], s.t[:, c, :], ACT.Square,
                                                    accum_out=s.oss[:, c:c + 1])
                    link(last)
                    nc.scalar.activation(s.ors, s.oss, ACT.Sqrt, scale=1.0 / HD, bias=const("eps")[:, 0:1])\
                        .then_inc(dA[p].sem, 1)
                each(osq)

            for p in range(2):
                act.wait_ge(dV[p].sem, dV[p].done(3, "fin"))
            act.dma_start(view(acts, 0, KT * S), x_in).then_inc(x_loaded, 16)
            act.dma_start(keys.rearrange("p a b -> p (a b)"), keys_in).then_inc(keys_loaded, 16)
            for b in range(4):
                act.wait_ge(bank_free[b], 19)
            square(1, view(acts, 0, KT * S))
            root(1)
            for hz in range(17):
                if hz < 16:
                    act.wait_ge(tile_done, STREAM["query"] + hz + 1)
                    take(76 + hz, QP[:, hz, :], ACT.Copy).then_inc(bank_free[hz % 4], 1)
                if hz:
                    q = hz - 1
                    act.wait_ge(sc_done, q + 1)
                    if q >= 2:
                        act.wait_ge(topk_done, q - 1)
                    nc.scalar.activation(SC[:, q % 2, :, :].rearrange("p c t -> p (c t)"), ps[:, 4 + q % 4, :],
                                         ACT.Copy).then_inc(sc_ready, 1)
            act.wait_ge(gd_ready, 1)
            nc.scalar.activation(TOP.rearrange("p c h k -> p (c h k)"), view(CAND_FLAT, 0, 512), ACT.Exp)\
                .then_inc(ge_ready, 1)
            nc.scalar.activation(zero_exp[:, 0:1], ea[:, 0:1], ACT.Copy).then_inc(gate_out, 4)
            nc.scalar.activation(zero_exp[:, 1:2], ea[:, 0:1], ACT.Copy).then_inc(gate_written[0], 16)
            nc.scalar.activation(zero_exp[:, 2:3], ea[:, 0:1], ACT.Copy).then_inc(gate_written[1], 16)
            for n, dst in enumerate((I1T, I2T, GTT)):
                act.wait_ge(turned, n + 1)
                nc.scalar.activation(dst, ps[:, 4 + n, :], ACT.Copy).then_inc(turned_read, 1)
            with act.Fori(0, S // BLOCK_T // 2) as cc:
                for par in range(2):
                    act.wait_ge(gate_written[par], cc * 16 + 16)
                    with act.Fori(0, BLOCK_T // 16) as j:
                        for q in range(4):
                            act.wait_ge(token_mm, cc * (32 * 4) + j * 16 + (par * 64 + 4 * (q + 1) + 16))
                            nc.scalar.activation(
                                GB[:, par, :, ds(j * 16 + 4 * q, 4)],
                                ps[:, 4 + q, :].rearrange("p (t i) -> p i t", t=4), ACT.Copy)\
                                .then_inc(gate_out, 1)
                    act.wait_ge(gate_out, cc * 32 + (16 * (par + 1) + 4))
                    act.dma_start(gate_dram[ds(cc * 2 + par, 1), :, :, :].rearrange("o p i t -> p (o i t)"),
                                  GB[:, par, :, :].rearrange("p i t -> p (i t)")).then_inc(gate_written[par], 16)
            for par in range(2):
                act.wait_ge(gate_written[par], 16 * (S // BLOCK_T // 2) + 16)
            e0 = STREAM["experts"]

            def gelus(n, g4, i=None):
                for e in range(GROUP):
                    act.wait_ge(tile_done, (n + e + 1) if i is None else i * 16 + (n + e + 1))
                    if not (isinstance(g4, int) and g4 + e < 2):
                        act.wait_ge(w_done, g4 + (e - 1))
                    nc.scalar.activation(GE[:, e % 2, :], ps[:, e % 2, :], ACT.Gelu).then_inc(gelu_done, 1)

            gelus(e0, 0)
            with act.Fori(0, 15) as i:
                gelus(e0 + 4, i * 8 + 4, i)
                gelus(e0 + 12, i * 8 + 8, i)
            gelus(e0 + 244, 124)
            act.wait_ge(acc_done, 8 * 32 + 8)
            square(2, view(acts, 0, KT * S))
            root(2)
            act.wait_ge(norm_done, 3)
            square(3, view(acts, 0, KT * S))
            root(3)

            n0 = STREAM["w_in_2"]
            for u in range(16):
                act.wait_ge(tile_done, n0 + u + 1)
                take(92 + u, QA[:, u, :] if u < 8 else ZZ[:, u - 8, :], ACT.Copy if u < 8 else ACT.Silu)\
                    .then_inc(bank_free[u % 4], 1)
            with act.Fori(0, 2) as i:
                for u in range(8):
                    act.wait_ge(tile_done, i * 8 + (n0 + 17 + u))
                    take(108 + u, GT2[:, ds(i * 8 + u, 1), :].rearrange("p o t -> p (o t)"), ACT.Sigmoid)\
                        .then_inc(bank_free[u % 4], 1)
            for u in range(5):
                act.wait_ge(tile_done, n0 + 33 + u)
                take(124 + u, KK[:, u, :], ACT.Copy).then_inc(bank_free[u % 4], 1)
            act.wait_ge(tile_done, STREAM["v_tok"] + 4)
            for c in range(TT):
                nc.scalar.activation(VT[:, c, :], ps[:, 4 + c, 0:384], ACT.Copy)
                nc.scalar.activation(gn[:, c, :], ps[:, 4 + c, 384:408], ACT.Sigmoid).then_inc(v_ready, 1)
            for kv in range(2):
                act.wait_ge(tile_done, STREAM["cmp_k1" if kv == 0 else "cmp_v1"] + 4)
                for a in range(2):
                    last = nc.scalar.activation(HID[:, kv, a, :], ps[:, 4 + 2 * kv + a, 0:62], ACT.Silu)
                last.then_inc(hid_ready, 1)
            act.wait_ge(kv_done, 1)
            nc.scalar.activation(KC[:, 0:62], ps[:, 0, 0:62], ACT.Copy)
            nc.scalar.activation(VC[0:NC_CMP, :, :].rearrange("p g d -> p (g d)"), ps[0:NC_CMP, 1, 0:128], ACT.Copy)\
                .then_inc(kc_ready, 1)

            def exps(u):
                kind, h = UNITS[u]
                par = u % 2
                act.wait_ge(at_scaled, u + 1)
                if kind == "swa":
                    nc.scalar.activation(esink[:, par, :], nm[:, par, :], ACT.Exp, bias=param("sinks")[:, h:h + 1])
                for i in range(TT):
                    w, _ = key_cols(kind, i)
                    last = nc.scalar.activation(SS[:, par, i, 0:w], SS[:, par, i, 0:w], ACT.Exp,
                                                bias=nm[:, par, i:i + 1], scale=NSA_SCALE,
                                                accum_out=den[:, par, i:i + 1])
                last.then_inc(at_exp, 1)

            def copies(u):
                kind, h = UNITS[u]
                par = u % 2
                if u >= 2:
                    act.wait_ge(at_out, u - 1)
                for x, (kt, tiles) in enumerate(turns(kind)):
                    chunk = CHUNKS[u] + x
                    act.wait_ge(at_turned, chunk + 1)
                    m = NC_CMP if kind == "cmp" else P
                    a, b = tiles[0] * P, (tiles[-1] + 1) * P
                    nc.scalar.activation(PT[0:m, par, kt, a:b], ps[0:m, 4 + chunk % 2, a:b], ACT.Copy)\
                        .then_inc(at_copied, 1)

            exps(0)
            for u in range(len(UNITS)):
                if u + 1 < len(UNITS):
                    exps(u + 1)
                copies(u)
            for u in range(8):
                act.wait_ge(tile_done, STREAM["w_out"] + u + 1)
                take(145 + u, ZZ[:, u, :], ACT.Copy).then_inc(bank_free[(145 + u) % 4], 1)
            for u in range(4, 8):
                act.wait_ge(bank_free[(145 + u) % 4], (145 + u) // 4 + 1)
            square(4, ZZ.rearrange("p k t -> p (k t)"))
            root(4)
            act.wait_ge(out_ready, 1)
            act.dma_start(out, view(acts, 0, KT * S)).then_inc(out_written, 16)
            act.wait_ge(out_written, 16)

        @block.vector
        def _(dve):
            v = nc.vector
            count = [0]

            def link(ins):
                count[0] += 1
                ins.then_inc(v_chain, 1)
                dve.wait_ge(v_chain, count[0])

            def norm(j, src, dst, weight):
                link(v.tensor_scalar(w32, weight, float(np.sqrt(D)), None, ALU.mult))
                dve.wait_ge(rs_out, j + 1)
                link(v.reciprocal(RS[:, :], RS[:, :]))
                for k in range(KT):
                    last = v.scalar_tensor_tensor(dst[:, k, :], src[:, k, :], w32[:, k:k + 1], RS[:, :],
                                                  ALU.mult, ALU.mult)
                return last

            v.memset(XA[:, :, 0:16], 0.0)
            v.memset(pool_tmp[:, :, 0:16], 0.0).then_inc(pads, 1)
            v.memset(RAW[:, :, 0:3], 0.0).then_inc(conv_done, 2)
            v.memset(zero_v, 0.0).then_inc(token_mm, 16)
            v.memset(zero_w, 0.0).then_inc(acc_done, 8)
            dve.wait_ge(par_loaded, 32)
            dve.wait_ge(x_loaded, 16)
            dve.wait_ge(acc_done, 8)
            norm(0, XT, XN, param("mix_norm_w")).then_inc(norm_done, 1)
            with dve.Fori(0, 3) as i:
                for u in range(8):
                    raw, y = RAW[:, u % 2, :], CONV[:, u % 2, :]
                    dve.wait_ge(bank_free[u % 4], i * 2 + (u // 4 + 2))
                    dve.wait_ge(silu_done, i * 8 + (u + 1))
                    dve.wait_ge(conv_done, i * 8 + (u + 2))

                    def w(tap):
                        return param("conv_w")[:, ds(i * 32 + (u * 4 + tap), 1)]
                    v.tensor_scalar(y, raw[:, 3:3 + S], w(3), None, ALU.mult).then_inc(conv_part, 1)
                    for x in (2, 1, 0):
                        dve.wait_ge(conv_part, i * 24 + (3 * u + 3 - x))
                        v.scalar_tensor_tensor(y, raw[:, x:x + S], w(x), y, ALU.mult, ALU.add)\
                            .then_inc(conv_part if x else conv_done, 1)
            for d in range(KT):
                dve.wait_ge(tile_done, 53 + d // 2)
                v.tensor_tensor(GT[:, d, :], GT[:, d, :], ps[:, d % 4, :], ALU.mult).then_inc(bank_free[d % 4], 1)
            dve.wait_ge(ba_done, 1)
            logits = ps[:, 4, 0:64].rearrange("p (c n) -> p c n", c=TT)
            link(v.tensor_tensor(a_in, logits[:, :, 8:16], over(param("dt_bias"), 1, TT), ALU.add))
            v.scalar_tensor_tensor(sp_a, a_in, -1.0, a_in, ALU.mult, ALU.max).then_inc(ba_v, 1)
            dve.wait_ge(ba_a, 2)
            link(v.scalar_tensor_tensor(sp_b, a_in, 0.0, sp_b, ALU.max, ALU.add))
            v.scalar_tensor_tensor(g_log, sp_b, -1.0, over(ea, 1, TT), ALU.mult, ALU.mult).then_inc(ba_v, 1)
            dve.wait_ge(gc_done, 1)
            v.tensor_copy(gc.rearrange("p c h -> p (c h)"), ps[:, 5, 0:TT * 8]).then_inc(ba_v, 1)
            dve.wait_ge(ba_a, 3)
            v.scalar_tensor_tensor(nbeg, beta, -1.0, egc, ALU.mult, ALU.mult).then_inc(gc_ready, 1)
            dve.wait_ge(gc_ready, 1)

            own = [0, 0]
            for r in range(HEADS // 2):
                def each(fn, steps=1):
                    for p in range(2):
                        if own[p]:
                            dve.wait_ge(dV[p].sem, own[p])
                        fn(p, 2 * r + p, slots[p], 4 * p)
                        own[p] += steps

                def bank(b):
                    return ps[:, b, :].rearrange("p (c t) -> p c t", c=TT)

                def norm_qk(p, h, s, b):
                    dve.wait_ge(dA[p].sem, dA[p].done(r, "root"))
                    link(v.reciprocal(s.sq, s.sq))
                    v.scalar_tensor_tensor(QKV[:, h, :], QKV[:, h, :], HD ** -0.5, s.sq[:, 0, :], ALU.mult, ALU.mult)
                    v.tensor_tensor(QKV[:, 8 + h, :], QKV[:, 8 + h, :], s.sq[:, 1, :], ALU.mult)\
                        .then_inc(dV[p].sem, 1)

                def vb(p, h, s, b):
                    dve.wait_ge(dT[p].sem, dT[p].done(r, "turn"))
                    v.tensor_tensor(s.vb, bank(b + 1), over(beta[:, :, h], 2, HD), ALU.mult).then_inc(dV[p].sem, 1)
                    v.tensor_tensor(s.gu, over(upper, 1, TT), over(g_log[:, :, h], 2, P), ALU.mult)\
                        .then_inc(dV[p].sem, 1)

                def diff(p, h, s, b):
                    dve.wait_ge(dT[p].sem, dT[p].done(r, "decay"))
                    link(v.tensor_tensor(s.df, bank(b), over(gc[:, :, h], 2, P), ALU.subtract))
                    v.tensor_scalar(s.ed, s.df, 0.0, None, ALU.max)
                    v.tensor_scalar(s.et, s.df, 0.0, None, ALU.min).then_inc(dV[p].sem, 1)

                def lower(p, h, s, b):
                    dve.wait_ge(dT[p].sem, dT[p].done(r, "gram"))
                    dve.wait_ge(dG[p].sem, dG[p].done(r, "edm"))
                    v.tensor_tensor(s.ed, bank(b + 2), s.ed, ALU.mult).then_inc(dV[p].sem, 1)
                    dve.wait_ge(dG[p].sem, dG[p].done(r, "etm"))
                    v.tensor_tensor(s.et, bank(b + 3), s.et, ALU.mult).then_inc(dV[p].sem, 1)

                def level0(p, h, s, b):
                    dve.wait_ge(dG[p].sem, dG[p].done(r, "lk0"))
                    v.tensor_tensor(s.tt, over(ident, 1, TT), s.lk, ALU.subtract).then_inc(dV[p].sem, 1)

                def t1(p, h, s, b):
                    dve.wait_ge(dT[p].sem, dT[p].done(r, "t1"))
                    v.tensor_copy(s.t, bank(b)).then_inc(dV[p].sem, 1)

                for fn, steps in ((norm_qk, 1), (vb, 2), (diff, 1), (lower, 2), (level0, 1), (t1, 1)):
                    each(fn, steps)
                for l in range(1, LEVELS):
                    def up(p, h, s, b):
                        dve.wait_ge(dT[p].sem, dT[p].done(r, f"tx{l}"))
                        dve.wait_ge(dV[p].sem, dV[p].done(r, "t" if l == 1 else f"u{l - 1}"))
                        if l < LEVELS - 1:
                            v.tensor_tensor(s.t, s.t, bank(b + 2), ALU.subtract)
                        v.tensor_tensor(s.tt, s.tt, bank(b + 3), ALU.subtract).then_inc(dV[p].sem, 1)
                    each(up)
                for c in range(TT):
                    def r_(p, h, s, b):
                        dve.wait_ge(dT[p].sem, dT[p].done(r, f"pq{c}"))
                        v.scalar_tensor_tensor(s.r, ps[:, b, 0:P], nbeg[:, c, h:h + 1], s.vb[:, c, :],
                                               ALU.mult, ALU.add).then_inc(dV[p].sem, 1)

                    def so(p, h, s, b):
                        dve.wait_ge(dT[p].sem, dT[p].done(r, f"os{c}"))
                        o = ps[:, b + 1, P:2 * P]
                        if c == 0:
                            v.tensor_copy(s.state, ps[:, b + 1, 2 * P:3 * P]).then_inc(dV[p].sem, 1)
                            v.tensor_copy(s.t[:, c, :], o).then_inc(dV[p].sem, 1)
                            return
                        if c < TT - 1:
                            dve.wait_ge(dV[p].sem, dV[p].done(r, f"s{c - 1}"))
                            v.scalar_tensor_tensor(s.state, s.state, s.egl[:, c:c + 1], ps[:, b + 1, 2 * P:3 * P],
                                                   ALU.mult, ALU.add).then_inc(dV[p].sem, 1)
                        link(v.tensor_scalar(s.t[:, c, :], ps[:, b, P:2 * P], egc[:, c, h:h + 1], None, ALU.mult))
                        v.tensor_tensor(s.t[:, c, :], s.t[:, c, :], o, ALU.add).then_inc(dV[p].sem, 1)

                    if c:
                        each(r_)
                    each(so, 2 if c < TT - 1 else 1)

                def dg(p, h, s, b):
                    dve.wait_ge(dA[p].sem, dA[p].done(r, "oroot"))
                    link(v.reciprocal(s.ors, s.ors))
                    v.tensor_tensor(s.lk, over(ident, 1, TT), over(s.ors, 2, P), ALU.mult).then_inc(dV[p].sem, 1)

                def fin(p, h, s, b):
                    dve.wait_ge(dT[p].sem, dT[p].done(r, "turn_o"))
                    v.scalar_tensor_tensor(Z[:, h, :], ps[:, b + 2, :], param("dn_norm_w"), Z[:, h, :],
                                           ALU.mult, ALU.mult).then_inc(dV[p].sem, 1)
                each(dg)
                each(fin)

            for d in range(KT):
                dve.wait_ge(tile_done, STREAM["dn_up"] + d + 1)
                v.tensor_tensor(GT[:, 8 + d, :], GT[:, 8 + d, :], ps[:, d % 4, :], ALU.mult)\
                    .then_inc(bank_free[d % 4], 1)
            dve.wait_ge(x_loaded, 32)
            for d in range(KT):
                dve.wait_ge(tile_done, STREAM["mix_out"] + d + 1)
                v.tensor_tensor(XT[:, d, :], XT[:, d, :], ps[:, d % 4, :], ALU.add).then_inc(bank_free[d % 4], 1)
            for b in range(4):
                dve.wait_ge(bank_free[b], 19)
            norm(1, XT, XN, param("ffn_norm_w")).then_inc(norm_done, 1)

            i1u, posu = I1.bitcast(u32), POS.bitcast(u32)

            def top16(sources, spare, values, indices, sig):
                for c in range(TT):
                    last = v.max(values[c][:, 0:8], sources[c])
                link(last)
                for c in range(TT):
                    v.max_index(indices[c][:, 0:8], values[c][:, 0:8], sources[c])
                for c in range(TT):
                    last = v.match_replace(spare[c], values[c][:, 0:8], sources[c], -3.0e38)
                link(last)
                for c in range(TT):
                    last = v.max(values[c][:, 8:16], spare[c])
                link(last)
                for c in range(TT):
                    last = v.max_index(indices[c][:, 8:16], values[c][:, 8:16], spare[c])
                last.then_inc(sig, 1)

            def pick(h):
                dve.wait_ge(cand_ready, h + 1)
                top16([CAND[:, c, :] for c in range(TT)], [CAND2[:, c, :] for c in range(TT)],
                      [TOP[:, c, h, :] for c in range(TT)], [posu[:, c, h, :] for c in range(TT)], cand_used)

            for q in range(16):
                dve.wait_ge(sc_ready, q + 1)
                top16([SC[:, q % 2, c, :] for c in range(TT)], [SC2[:, c, :] for c in range(TT)],
                      [V1[:, c, q, :] for c in range(TT)], [i1u[:, c, q, :] for c in range(TT)], topk_done)
                if q % 2 == 0 and q:
                    pick(q // 2 - 1)
            pick(7)
            dve.wait_ge(cand_used, 8)
            dve.wait_ge(topk_done, 16)
            v.tensor_copy(I1F, i1u).then_inc(i1f_ready, 1)
            flat = posu.rearrange("p c h k -> p (c h k)")
            pu = PU.bitcast(u32).rearrange("p c h -> p (c h)")
            for z, (op, n) in enumerate(((ALU.logical_shift_right, 4), (ALU.bitwise_and, 15))):
                link(v.tensor_scalar(pu, flat, n, None, op))
                link(v.tensor_copy(PF[:, z, :, :, :].rearrange("p c h k -> p (c h k)"), pu))
            gtmp = view(CAND_FLAT, 0, TT, 8, TOPK)
            v.tensor_tensor(gtmp, TOP, TOP[:, :, :, 0:1].broadcast_to([P, TT, 8, TOPK]), ALU.subtract)\
                .then_inc(gd_ready, 1)

            def eq(x):
                c, z = divmod(x, 2)
                if x >= 2:
                    dve.wait_ge(sel_ready, x - 1)
                v.tensor_tensor(EQ[:, x % 2, :].rearrange("p (h k j) -> p h k j", h=8, k=16),
                                over(PF[:, z, c, :, :], 3, 16), over(over(iota[:, 0:16], 1, 16), 1, 8),
                                ALU.is_equal).then_inc(eq_ready, 1)

            eq(0)
            for x in range(8):
                if x < 7:
                    eq(x + 1)
                c, z = divmod(x, 2)
                dve.wait_ge(eq_mul, x + 1)
                v.tensor_reduce(SEL[:, z, c, :], EQ[:, x % 2, :].rearrange("p (n j) -> p n j", j=16),
                                AX.X, ALU.add).then_inc(sel_ready, 1)
            dve.wait_ge(ge_ready, 1)
            link(v.tensor_reduce(GSUM, TOP, AX.X, ALU.add))
            link(v.reciprocal(GSUM, GSUM))
            v.tensor_tensor(TOP, TOP, over(GSUM, 3, TOPK), ALU.mult).then_inc(gate_ready, 1)
            dve.wait_ge(turned_read, 3)
            with dve.Fori(0, S // 16) as j:
                for u in range(16):
                    dve.wait_ge(token_mm, j * 16 + (u + 1))
                    t = ds(j * 16 + u, 1)
                    v.tensor_scalar(ONE_A[:, u, :], iota, I1T[:, t], GTT[:, t], ALU.is_equal, ALU.mult)
                    v.tensor_scalar(ONE_B[:, u, :], iota, I2T[:, t], None, ALU.is_equal).then_inc(onehot, 1)

            e0 = STREAM["experts"]

            def weigh(g, g4, par, loads):
                dve.wait_ge(gate_loaded[par], loads)
                for e in range(GROUP):
                    dve.wait_ge(gelu_done, g4 + (e + 1))
                    v.tensor_tensor(W[:, par, e, :].rearrange("p (c t) -> p c t", t=BLOCK_T),
                                    GE[:, e % 2, :].rearrange("p (c t) -> p c t", t=BLOCK_T),
                                    GG[:, par, :, e, :], ALU.mult).then_inc(w_done, 1)

            def accumulate(n, g, i=None):
                for d in range(KT):
                    if d < KT - 1:
                        dve.wait_ge(y_done, g * 7 + (d + 1))
                    else:
                        dve.wait_ge(tile_done, (n + 4) if i is None else i * 16 + (n + 4))
                    dve.wait_ge(acc_done, g * 8 + (d + 1))
                    v.tensor_tensor(XT[:, d, :], XT[:, d, :], ps[:, 2 + d % 4, :], ALU.add).then_inc(acc_done, 1)

            for par in range(2):
                dve.wait_ge(gate_written[par], 16 * (S // BLOCK_T // 2) + 16)
            weigh(0, 0, 0, 16)
            with dve.Fori(0, 15) as i:
                weigh(None, i * 8 + 4, 1, i * 16 + 16)
                accumulate(e0 + 8, i * 2, i)
                weigh(None, i * 8 + 8, 0, i * 16 + 32)
                accumulate(e0 + 16, i * 2 + 1, i)
            weigh(31, 124, 1, 16 * 16)
            accumulate(e0 + 248, 30)
            accumulate(e0 + 252, 31)

            dve.wait_ge(tile_done, STREAM["ada"] + 24)
            link(v.tensor_tensor(mod, ps[:, 6, 0:24], param("b_ada"), ALU.add))
            link(v.scalar_tensor_tensor(g_eff, mod[:, 8:16], 1.0, param("g_pre"), ALU.add, ALU.mult))
            dve.wait_ge(acc_done, 8 * 32 + 8)
            norm(2, XT, XT, param("final_norm_w")).then_inc(norm_done, 1)
            dve.wait_ge(norm_done, 3)
            link(norm(3, XT, XN, g_eff))
            for k in range(KT):
                last = v.tensor_scalar(XN[:, k, :], XN[:, k, :], mod[:, k:k + 1], None, ALU.add)
            last.then_inc(norm_done, 1)

            dve.wait_ge(xc_ready, 64)
            for kv in range(2):
                for m in range(16):
                    last = v.tensor_scalar(CB[:, kv, m, :].rearrange("p (g n) -> p g n", g=2),
                                           XC[:, kv, :, 2 * m:2 * m + 16 * (NC_CMP - 1) + 1:16],
                                           param("pe_k" if kv == 0 else "pe_v")[:, m:m + 1], None, ALU.add)
                last.then_inc(cb_ready, 1)

            def scale(u):
                kind, h = UNITS[u]
                par = u % 2
                slope = 2.0 ** -(h + 1) / NSA_SCALE
                dve.wait_ge(at_scored, u + 1)
                if u >= 2:
                    dve.wait_ge(at_turned, CHUNKS[u - 1])
                for i in range(TT):
                    w, k0 = key_cols(kind, i)
                    if kind == "cmp":
                        bias = const("cmp")[:, i * NC_CMP:(i + 1) * NC_CMP]
                    elif kind == "swa":
                        bias = const("window")[:, 2 * P - w:2 * P]
                    else:
                        bias = const("alibi")[:, S - w:S]
                    last = v.scalar_tensor_tensor(SS[:, par, i, 0:w], bias, slope, ps[:, i, 0:w], ALU.mult, ALU.add)
                link(last)
                for i in range(TT):
                    w, _ = key_cols(kind, i)
                    last = v.tensor_reduce(mx[:, par, i:i + 1], SS[:, par, i, 0:w], AX.X, ALU.max)
                link(last)
                if kind == "swa":
                    link(v.tensor_scalar(mx[:, par, :], mx[:, par, :], NSA_SCALE, param("sinks")[:, h:h + 1],
                                         ALU.mult, ALU.max))
                    v.tensor_scalar(nm[:, par, :], mx[:, par, :], -1.0, None, ALU.mult).then_inc(at_scaled, 1)
                else:
                    v.tensor_scalar(nm[:, par, :], mx[:, par, :], -NSA_SCALE, None, ALU.mult).then_inc(at_scaled, 1)

            def diag(u):
                kind, h = UNITS[u]
                par = u % 2
                dve.wait_ge(at_exp, u + 1)
                if kind == "swa":
                    link(v.tensor_tensor(den[:, par, :], den[:, par, :], esink[:, par, :], ALU.add))
                link(v.reciprocal(fac[:, par, :], den[:, par, :]))
                if kind != "swa":
                    b = ("cmp", "slc", "win").index(kind) * 8 + h
                    link(v.tensor_tensor(fac[:, par, :], fac[:, par, :], gn[:, :, b], ALU.mult))
                if kind == "cmp":
                    link(v.tensor_tensor(fac[:, par, :], fac[:, par, :], const("seen"), ALU.mult))
                v.tensor_tensor(DG[:, par, :, :], over(ident, 1, TT), over(fac[:, par, :], 2, P), ALU.mult)\
                    .then_inc(at_diag, 1)

            def gate_out_tile(u):
                kind, h = UNITS[u]
                if h % 2 == 1 and kind in ("win", "swa"):
                    t = h // 2 + (4 if kind == "swa" else 0)
                    dve.wait_ge(at_out, u + 1)
                    v.tensor_tensor(QA[:, t, :], ps[:, 6 + t % 2, :], ZZ[:, t, :], ALU.mult).then_inc(o_ready, 1)

            dve.wait_ge(v_ready, 4)
            scale(0)
            for u in range(len(UNITS)):
                if u + 1 < len(UNITS):
                    scale(u + 1)
                diag(u)
                if u:
                    gate_out_tile(u - 1)
            gate_out_tile(len(UNITS) - 1)
            for d in range(16):
                n = STREAM["o_nsa"] + d // 2
                dve.wait_ge(tile_done, n + 1)
                v.tensor_tensor(GT2[:, d, :], GT2[:, d, :], ps[:, (129 + d) % 4, :], ALU.mult)\
                    .then_inc(bank_free[(129 + d) % 4], 1)
            norm(4, ZZ, ZZ, param("g_post")).then_inc(norm_done, 1)
            dve.wait_ge(norm_done, 5)
            for k in range(KT):
                last = v.scalar_tensor_tensor(XT[:, k, :], ZZ[:, k, :], mod[:, 16 + k:17 + k], XT[:, k, :],
                                              ALU.mult, ALU.add)
            last.then_inc(out_ready, 1)

        @block.tensor
        def _(pe):
            def mm(o, lhsT, rhs, start=True, stop=True):
                return nc.tensor.matmul(o, lhsT, rhs, start=start, stop=stop, skip_group_check=True)

            def weights(n, later=0):
                pe.wait_ge(w_loaded[n % RING], later * 16 + 16 * (n // RING + 1))
                return ring[:, n % RING, :]

            def project(n, m, x, i=None):
                w = weights(n, 0 if i is None else i)
                if m >= 4:
                    pe.wait_ge(bank_free[m % 4], m // 4 if i is None else i * 2 + m // 4)
                for k in range(KT):
                    last = mm(ps[:, m % 4, :], w[:, k * P:(k + 1) * P], x[:, k, :], k == 0, k == KT - 1)
                last.then_inc(tile_done, 1)

            def project_half(n, m, x):
                w = weights(n)
                for o in range(2):
                    pe.wait_ge(bank_free[(m + o) % 4], (m + o) // 4)
                    for k in range(4):
                        last = mm(ps[:, (m + o) % 4, :], w[:, o * 512 + k * P:o * 512 + (k + 1) * P],
                                  x[:, k, :], k == 0, k == 3)
                last.then_inc(tile_done, 1)

            def sum_squares(j, sq):
                pe.wait_ge(norm_sq, j + 1)
                for k in range(KT):
                    last = mm(ps[:, 7, :], ones, sq[:, k, :], k == 0, k == KT - 1)
                last.then_inc(norm_ss, 1)

            pe.wait_ge(par_loaded, 32)
            sum_squares(0, XN)
            pe.wait_ge(norm_done, 1)
            n0 = STREAM["w_in"]
            for m in range(4):
                project(n0 + m, m, XN)
            with pe.Fori(0, 3) as i:
                for u in range(8):
                    project(n0 + 4 + u, 4 + u, XN, i)
            for m in range(28, 36):
                project(n0 + m, m, XN)
            with pe.Fori(0, 2) as i:
                for u in range(8):
                    project(n0 + 36 + u, 36 + u, XN, i)
            pe.wait_ge(pool_ready, 1)
            for g in range(4):
                mm(ps[:, 4 + g, :], param("pool_w")[:, g * P:(g + 1) * P], XA[:, g, 16:]).then_inc(pooly_done, 1)
            pe.wait_ge(yt_ready, 4)
            for u in range(4):
                project_half(STREAM["pool_up"] + u, 52 + 2 * u, XA[:, :, 16:])
            for c in range(TT):
                for k in range(KT):
                    last = mm(ps[:, 4, c * 16:(c + 1) * 16], XN[:, k, c * P:(c + 1) * P],
                              param("w_ba")[:, k * 16:(k + 1) * 16], k == 0, k == KT - 1)
            last.then_inc(ba_done, 1)
            pe.wait_ge(ba_v, 2)
            mm(ps[:, 5, 0:TT * 8], upper, g_log.rearrange("p c h -> p (c h)")).then_inc(gc_done, 1)
            pe.wait_ge(gc_ready, 1)

            for r in range(HEADS // 2):
                def each(fn):
                    for p in range(2):
                        fn(p, 2 * r + p, slots[p], 4 * p)

                def sumsq(p, h, s, b):
                    pe.wait_ge(dA[p].sem, dA[p].done(r, "sq"))
                    mm(ps[:, b, :], ones, s.sq[:, 0, :])
                    mm(ps[:, b + 1, :], ones, s.sq[:, 1, :]).then_inc(dT[p].sem, 1)

                def four(bank, lhsT, rhs, is_transpose=False):
                    for c in range(TT):
                        last = mm(ps[:, bank, c * P:(c + 1) * P], lhsT(c), rhs(c))
                    return last

                def turn(p, h, s, b):
                    pe.wait_ge(dV[p].sem, dV[p].done(r, "norm"))
                    four(b, lambda c: QKV[:, 8 + h, c * P:(c + 1) * P], lambda c: ident)
                    four(b + 1, lambda c: QKV[:, 16 + h, c * P:(c + 1) * P], lambda c: ident)\
                        .then_inc(dT[p].sem, 1)
                    four(b + 2, lambda c: QKV[:, 8 + h, c * P:(c + 1) * P], lambda c: QKV[:, 8 + h, c * P:(c + 1) * P])
                    four(b + 3, lambda c: QKV[:, 8 + h, c * P:(c + 1) * P], lambda c: QKV[:, h, c * P:(c + 1) * P])\
                        .then_inc(dT[p].sem, 1)

                def decay(p, h, s, b):
                    pe.wait_ge(dV[p].sem, dV[p].done(r, "gu"))
                    pe.wait_ge(dA[p].sem, dA[p].done(r, "ktok"))
                    mm(ps[:, b, :], ones, s.gu.rearrange("p c t -> p (c t)")).then_inc(dT[p].sem, 1)

                def lt(p, h, s, b):
                    pe.wait_ge(dV[p].sem, dV[p].done(r, "l"))
                    four(b + 1, lambda c: s.ed[:, c, :], lambda c: ident).then_inc(dT[p].sem, 1)

                def t1(p, h, s, b):
                    pe.wait_ge(dV[p].sem, dV[p].done(r, "tt"))
                    pe.wait_ge(dA[p].sem, dA[p].done(r, "lts"))
                    four(b, lambda c: s.tt[:, c, :], lambda c: ident).then_inc(dT[p].sem, 1)

                for fn in (sumsq, turn, decay, lt, t1):
                    each(fn)
                for l in range(1, LEVELS):
                    def lx(p, h, s, b):
                        pe.wait_ge(dG[p].sem, dG[p].done(r, f"lk{l}"))
                        pe.wait_ge(dV[p].sem, dV[p].done(r, "t" if l == 1 else f"u{l - 1}"))
                        four(b, lambda c: s.lk[:, c, :], lambda c: s.t[:, c, :]).then_inc(dT[p].sem, 1)

                    def tx(p, h, s, b):
                        pe.wait_ge(dA[p].sem, dA[p].done(r, f"x{l}"))
                        if l < LEVELS - 1:
                            four(b + 2, lambda c: s.tt[:, c, :], lambda c: s.x[:, c, :])
                        four(b + 3, lambda c: s.x[:, c, :], lambda c: s.tt[:, c, :]).then_inc(dT[p].sem, 1)

                    each(lx)
                    each(tx)
                for c in range(TT):
                    def pq(p, h, s, b):
                        pe.wait_ge(dV[p].sem, dV[p].done(r, f"o{c - 1}"))
                        mm(ps[:, b, 0:P], QKV[:, 8 + h, c * P:(c + 1) * P], s.state)
                        mm(ps[:, b, P:2 * P], QKV[:, h, c * P:(c + 1) * P], s.state).then_inc(dT[p].sem, 1)

                    def vnew(p, h, s, b):
                        pe.wait_ge(dV[p].sem, dV[p].done(r, f"r{c}" if c else f"u{LEVELS - 1}"))
                        mm(ps[:, b + 1, 0:P], s.tt[:, c, :], s.r if c else s.vb[:, 0, :]).then_inc(dT[p].sem, 1)

                    def outs(p, h, s, b):
                        pe.wait_ge(dA[p].sem, dA[p].done(r, f"vn{c}"))
                        pe.wait_ge(dG[p].sem, dG[p].done(r, "kdec"))
                        last = mm(ps[:, b + 1, P:2 * P], s.et[:, c, :], s.vn)
                        if c < TT - 1:
                            last = mm(ps[:, b + 1, 2 * P:3 * P], s.kt[:, c, :], s.vn)
                        last.then_inc(dT[p].sem, 1)

                    for fn in ((pq,) if c else ()) + (vnew, outs):
                        each(fn)

                def turn_o(p, h, s, b):
                    pe.wait_ge(dV[p].sem, dV[p].done(r, "dg"))
                    four(b + 2, lambda c: s.t[:, c, :], lambda c: s.lk[:, c, :]).then_inc(dT[p].sem, 1)

                each(turn_o)

            for p in range(2):
                pe.wait_ge(dV[p].sem, dV[p].done(3, "fin"))
            for u in range(8):
                project(STREAM["dn_up"] + u, 60 + u, Z)
            pe.wait_ge(merged, 1)
            for u in range(8):
                project(STREAM["mix_out"] + u, 68 + u, XN)
            sum_squares(1, XN)
            pe.wait_ge(norm_done, 2)
            pe.wait_ge(keys_loaded, 16)
            for hz in range(17):
                if hz < 16:
                    project(STREAM["query"] + hz, 76 + hz, XN)
                if hz:
                    q = hz - 1
                    pe.wait_ge(bank_free[(76 + q) % 4], (76 + q) // 4 + 1)
                    if q >= 4:
                        pe.wait_ge(sc_ready, q - 3)
                    for c in range(TT):
                        last = mm(ps[:, 4 + q % 4, c * P:(c + 1) * P], QP[:, q, c * P:(c + 1) * P], keys[:, q, :])
                    last.then_inc(sc_done, 1)
            for z, bank in ((0, 4), (1, 5)):
                for c in range(TT):
                    pe.wait_ge(sel_ready, 8)
                    last = mm(ps[:, bank, c * P:(c + 1) * P], SEL[:, z, c, :], ident)
                last.then_inc(turned, 1)
            pe.wait_ge(gate_ready, 1)
            for c in range(TT):
                last = mm(ps[:, 6, c * P:(c + 1) * P], TOP[:, c, :, :].rearrange("p h k -> p (h k)"), ident)
            last.then_inc(turned, 1)
            pe.wait_ge(turned_read, 3)
            with pe.Fori(0, S // 16) as j:
                for u in range(16):
                    if u % 4 == 0:
                        pe.wait_ge(gate_out, j * 4 + (u // 4 + 1))
                    pe.wait_ge(onehot, j * 16 + (u + 1))
                    mm(ps[:, 4 + u // 4, (u % 4) * P:(u % 4 + 1) * P], ONE_B[:, u, :], ONE_A[:, u, :])\
                        .then_inc(token_mm, 1)
            e0 = STREAM["experts"]

            def hidden(n, gelu_before, i=None):
                for e in range(GROUP):
                    w = weights(n + e, 0 if i is None else i * 2)
                    if not (isinstance(gelu_before, int) and gelu_before + e < 2):
                        pe.wait_ge(gelu_done, gelu_before + (e - 1))
                    for k in range(KT):
                        last = mm(ps[:, e % 2, :], w[:, k * P:(k + 1) * P], XN[:, k, :], k == 0, k == KT - 1)
                    last.then_inc(tile_done, 1)

            def expert_out(n, g, par, i=None):
                ws = [weights(n + e, 0 if i is None else i * 2) for e in range(GROUP)]
                pe.wait_ge(w_done, g * 4 + 4)
                for d in range(KT):
                    pe.wait_ge(acc_done, g * 8 + (d + 5))
                    for e in range(GROUP):
                        last = mm(ps[:, 2 + d % 4, :], ws[e][:, d * P:(d + 1) * P], W[:, par, e, :],
                                  e == 0, e == GROUP - 1)
                        if d == KT - 1:
                            last.then_inc(tile_done, 1)
                    if d < KT - 1:
                        last.then_inc(y_done, 1)

            hidden(e0, 0)
            with pe.Fori(0, 15) as i:
                hidden(e0 + 4, i * 8 + 4, i)
                expert_out(e0 + 8, i * 2, 0, i)
                hidden(e0 + 12, i * 8 + 8, i)
                expert_out(e0 + 16, i * 2 + 1, 1, i)
            hidden(e0 + 244, 124)
            expert_out(e0 + 248, 30, 0)
            expert_out(e0 + 252, 31, 1)
            for u in range(24):
                w = weights(STREAM["ada"] + u)
                if u == 0:
                    pe.wait_ge(turned_read, 3)
                for k in range(KT):
                    last = mm(ps[:, 6, u:u + 1], w[:, k * P:(k + 1) * P], param("c")[:, k:k + 1], k == 0, k == KT - 1)
                last.then_inc(tile_done, 1)
            for j in (2, 3):
                sum_squares(j, XN)
            pe.wait_ge(norm_done, 4)
            n0 = STREAM["w_in_2"]
            for u in range(16):
                project(n0 + u, 92 + u, XN)
            with pe.Fori(0, 2) as i:
                for u in range(8):
                    project(n0 + 16 + u, 108 + u, XN, i)
            for u in range(5):
                project(n0 + 32 + u, 124 + u, XN)
            for j in range(4):
                w = weights(STREAM["v_tok"] + j)
                for c in range(TT):
                    for k in range(2):
                        last = mm(ps[:, 4 + c, 0:408], XN[:, 2 * j + k, c * P:(c + 1) * P],
                                  w[:, k * 512:k * 512 + 408], j == 0 and k == 0, j == 3 and k == 1)
                last.then_inc(tile_done, 1)
            for kv in range(2):
                pe.wait_ge(cb_ready, kv + 1)
                pe.wait_ge(v_ready, 4)
                for m in range(16):
                    w = weights(STREAM["cmp_k1" if kv == 0 else "cmp_v1"] + m // 4)
                    for a in range(2):
                        last = mm(ps[:, 4 + 2 * kv + a, 0:62], w[:, (m % 4) * 256 + a * P:(m % 4) * 256 + (a + 1) * P],
                                  CB[:, kv, m, :], m == 0, m == 15)
                    if m % 4 == 3:
                        last.then_inc(tile_done, 1)
            pe.wait_ge(hid_ready, 2)
            for b in range(4):
                pe.wait_ge(bank_free[b], (129 - b + 3) // 4)
            for half in range(2):
                for a in range(2):
                    mm(ps[half * 64:(half + 1) * 64, 0, 0:62], param("w_cmp_k2")[:, a * 64:(a + 1) * 64],
                       HID[:, 0, a, :], a == 0, a == 1)
            for g in range(2):
                for a in range(2):
                    last = mm(ps[0:NC_CMP, 1, g * 64:(g + 1) * 64], HID[:, 1, a, g * NC_CMP:(g + 1) * NC_CMP],
                              param("w_cmp_v2")[:, a * 64:(a + 1) * 64], a == 0, a == 1)
            last.then_inc(kv_done, 1)
            pe.wait_ge(kc_ready, 1)
            pe.wait_ge(dup_done, 64)

            def scores(u):
                kind, h = UNITS[u]
                if u:
                    pe.wait_ge(at_scaled, u)
                p0, t = 64 * (h % 2), h // 2 + (4 if kind == "swa" else 0)
                for i in range(TT):
                    q = QA[p0:p0 + 64, t, i * P:(i + 1) * P]
                    w, k0 = key_cols(kind, i)
                    if kind == "cmp":
                        k = KC[p0:p0 + 64, (h // 4) * NC_CMP:(h // 4 + 1) * NC_CMP]
                    else:
                        k = KD[p0:p0 + 64, ("slc", "win", "swa").index(kind), h // 4, k0:k0 + w]
                    last = mm(ps[:, i, 0:w], q, k)
                last.then_inc(at_scored, 1)

            def values(u):
                kind, h = UNITS[u]
                par, p0, t = u % 2, 64 * (h % 2), h // 2 + (4 if kind == "swa" else 0)
                pe.wait_ge(at_diag, u + 1)
                for x, (kt, tiles) in enumerate(turns(kind)):
                    chunk = CHUNKS[u] + x
                    if chunk >= 2:
                        pe.wait_ge(at_copied, chunk - 1)
                    for i in tiles:
                        w, k0 = key_cols(kind, i)
                        a = kt * P - k0
                        m = NC_CMP if kind == "cmp" else P
                        last = mm(ps[0:m, 4 + chunk % 2, i * P:(i + 1) * P], SS[:, par, i, a:a + m], DG[:, par, i, :])
                    last.then_inc(at_turned, 1)
                pe.wait_ge(at_copied, CHUNKS[u + 1])
                if h % 2 == 0 and kind in ("cmp", "swa") and t >= 2:
                    pe.wait_ge(o_ready, t - 1)
                o = ps[p0:p0 + 64, 6 + t % 2, :]
                if kind == "cmp":
                    last = mm(o, VC[0:NC_CMP, h // 4, :], PT[0:NC_CMP, par, 0, :], True, False)
                elif kind == "swa":
                    for i in range(TT):
                        for kt in range(max(0, i - 1), i + 1):
                            v = VT[:, kt, 256 + (h // 4) * 64:256 + (h // 4 + 1) * 64]
                            last = mm(o[:, i * P:(i + 1) * P], v, PT[:, par, kt, i * P:(i + 1) * P],
                                      kt == max(0, i - 1), kt == i)
                else:
                    b = 0 if kind == "slc" else 128
                    for kt in range(TT):
                        v = VT[:, kt, b + (h // 4) * 64:b + (h // 4 + 1) * 64]
                        last = mm(o[:, kt * P:], v, PT[:, par, kt, kt * P:], False, kind == "win" and kt == TT - 1)
                last.then_inc(at_out, 1)

            scores(0)
            for u in range(len(UNITS)):
                if u + 1 < len(UNITS):
                    scores(u + 1)
                values(u)
            pe.wait_ge(o_ready, 8)
            for u in range(4):
                project_half(STREAM["o_nsa"] + u, 129 + 2 * u, QA[:, 0:4, :])
            for u in range(4):
                project_half(STREAM["o_swa"] + u, 137 + 2 * u, QA[:, 4:8, :])
            pe.wait_ge(merged, 2)
            for u in range(8):
                project(STREAM["w_out"] + u, 145 + u, XN)
            sum_squares(4, XN)


def shape_constants():
    p, j = np.arange(P)[:, None], np.arange(P)[None, :]
    parts = {
        "ident": p == j,
        "ones": np.ones((P, P)),
        "upper": p <= j,
        "iota": np.broadcast_to(j, (P, P)),
        "strict": j < p,
        "block": np.concatenate([(j >> l & 1 == 1) & (p >> l & 1 == 0) & (j >> l + 1 == p >> l + 1)
                                 for l in range(LEVELS)], axis=1),
    }
    x = np.arange(S)[None, :]
    dist = p + S - P - x
    parts["alibi"] = np.where(dist >= 0, -dist, -1e30)
    dist = P + p - np.arange(2 * P)[None, :]
    parts["window"] = np.where((dist >= 0) & (dist < P), -dist, -1e30)
    t = np.arange(TT)[None, :, None] * P + p[:, :, None]
    dist = t - (np.arange(NC_CMP)[None, None, :] * 16 + 31)
    parts["cmp"] = np.where(dist >= 0, -dist, -1e30).reshape(P, -1)
    parts["seen"] = (t[:, :, 0] >= 31)
    n = np.arange(16)[None, :] + 1
    first = 1.0 / np.minimum(n, 2.0 ** (np.arange(4)[:, None] + 1))
    parts["eps"] = np.broadcast_to([[EPS, D * EPS]], (P, 2))
    parts["first"] = np.broadcast_to(first.reshape(1, 64), (P, 64))
    return np.concatenate([np.asarray(parts[k], np.float32) for k in CONST], axis=1)


def by_feature(v):
    return v.reshape(-1, P).T


def tiles(w):
    return w.reshape(KT, P, -1, P).transpose(2, 1, 0, 3).reshape(-1, P, 1024)


def half_tiles(w):
    return w.reshape(4, P, 8, P).transpose(2, 1, 0, 3).reshape(4, 2, P, 512).transpose(0, 2, 1, 3).reshape(4, P, 1024)


def lay_out(inputs):
    a = {k: np.asarray(v) for k, v in inputs.items()}
    one = {k: v[0] for k, v in a.items()}
    w, w2 = one["w_in"], one["w_in_2"]
    down = one["peer_down"].reshape(P, P, KT, P).transpose(0, 3, 2, 1).reshape(32, GROUP, P, 1024)
    up = one["peer_up"].reshape(32, GROUP, P, 1024)
    experts = [down[0]]
    for g in range(31):
        experts += [down[g + 1], up[g]]
    experts.append(up[31])
    v_tok = np.concatenate([w2[:, 896:1024], w2[:, 1152:1280], w2[:, 2456:2584], w2[:, 1280:1304],
                            np.zeros((1024, 104), np.float32)], axis=1)
    cmp_tiles = lambda m: m.reshape(4, 4, P, 256).transpose(0, 2, 1, 3).reshape(4, P, 1024)
    stream = np.concatenate([
        tiles(w[:, 0:4608]), tiles(w[:, 4624:6672]), half_tiles(one["w_pool_up"]), tiles(one["w_dn_up"]),
        tiles(one["w_mix_out"]), tiles(one["peer_w_query"]), *experts, tiles(one["w_ada_2"]),
        tiles(w2[:, 0:512]), tiles(w2[:, 1816:2328]), tiles(w2[:, 1304:1816]), tiles(w2[:, 2584:3096]),
        tiles(w2[:, 3096:5144]), tiles(w2[:, 512:768]), tiles(w2[:, 768:896]), tiles(w2[:, 1024:1152]),
        tiles(w2[:, 2328:2456]),
        v_tok.reshape(4, 2, P, 512).transpose(0, 2, 1, 3).reshape(4, P, 1024),
        cmp_tiles(one["w_cmp_k1_2"]), cmp_tiles(one["w_cmp_v1_2"]),
        half_tiles(one["w_o_nsa_2"]), half_tiles(one["w_o_swa_2"]), tiles(one["w_out_2"])])
    rows = lambda v: np.broadcast_to(v.reshape(1, -1), (P, v.size))
    params = {
        "mix_norm_w": by_feature(one["mix_norm_w"]),
        "conv_w": one["conv_w"].reshape(4, 24, P).transpose(2, 1, 0).reshape(P, 96),
        "pool_scale": by_feature(one["pool_scale"]),
        "a_log": rows(one["a_log"]), "dt_bias": rows(one["dt_bias"]),
        "dn_norm_w": one["dn_norm_w"].reshape(P, 1),
        "ffn_norm_w": by_feature(one["ffn_norm_w"]), "final_norm_w": by_feature(a["final_norm_w"]),
        "c": by_feature(one["c_2"]), "b_ada": by_feature(one["b_ada_2"]),
        "g_pre": by_feature(one["g_pre_2"]), "g_post": by_feature(one["g_post_2"]),
        "sinks": rows(one["sinks_2"]),
        "pe_k": one["pe_cmp_k_2"].reshape(16, P).T, "pe_v": one["pe_cmp_v_2"].reshape(16, P).T,
        "pool_w": one["pool_w"].transpose(1, 0, 2).reshape(P, 512),
        "w_ba": w[:, 4608:4624].reshape(KT, P, 16).transpose(1, 0, 2).reshape(P, 128),
        "w_cmp_k2": one["w_cmp_k2_2"].reshape(2, P, 64).transpose(1, 0, 2).reshape(P, 128),
        "w_cmp_v2": one["w_cmp_v2_2"].reshape(2, P, 64).transpose(1, 0, 2).reshape(P, 128),
    }
    both = np.stack([one["peer_keys_1"], one["peer_keys_2"]], axis=1)
    return {
        "x_in": one["x"].T.reshape(KT, P, S).transpose(1, 0, 2).reshape(P, KT * S),
        "stream": stream,
        "params": np.concatenate([params[k] for k in PARAM], axis=1),
        "consts": shape_constants(),
        "keys": both.transpose(3, 0, 1, 2).reshape(P, 2048),
    }


def kernel(**inputs):
    import concourse.bacc as bacc
    from concourse.bass_utils import run_bass_kernel_spmd

    nc = bacc.Bacc("TRN2", target_bir_lowering=False, num_devices=1)
    arrays = {k: np.ascontiguousarray(v) for k, v in lay_out(inputs).items()}
    aps = [nc.dram_tensor("dram_" + k, v.shape, mybir.dt.float32, kind="ExternalInput").ap() for k, v in arrays.items()]
    out = nc.dram_tensor("dram_out", [P, KT * S], mybir.dt.float32, kind="ExternalOutput").ap()
    program(nc, *aps, out)
    got = run_bass_kernel_spmd(nc, [{"dram_" + k: v for k, v in arrays.items()}], core_ids=[0]).results[0]["dram_out"]
    return got.reshape(P, KT, S).transpose(2, 1, 0).reshape(1, S, D)
```

```python
import numpy as np
import concourse.bass as bass
from concourse import mybir
from contextlib import ExitStack

D = 1024
S = 512
P = 128
KT = D // P
TT = S // P
HEADS = 8
HD = 128
TOPK = 16
RING = 8
EPS = 1e-6
EXPERTS_A = 128
GROUP = 4
BLOCK_T = 64
NC_CMP = 31
NSA_SCALE = 0.125
LEVELS = 7

CONST = {}
_at = 0
for _n, _w in (("ident", P), ("ones", P), ("upper", P), ("iota", P), ("strict", P), ("block", LEVELS * P),
               ("alibi", S), ("window", 2 * P), ("cmp", TT * NC_CMP), ("seen", TT), ("first", 64), ("eps", 2)):
    CONST[_n] = (_at, _w)
    _at += _w
N_CONST = _at

PARAM = {}
_at = 0
for _n, _w in (("mix_norm_w", KT), ("conv_w", 96), ("pool_scale", 4), ("a_log", 8), ("dt_bias", 8),
               ("dn_norm_w", 1), ("ffn_norm_w", KT), ("final_norm_w", KT), ("c", KT), ("b_ada", 24),
               ("g_pre", KT), ("g_post", KT), ("sinks", 8), ("pe_k", 16), ("pe_v", 16), ("pool_w", 512),
               ("w_ba", KT * 16), ("w_cmp_k2", 128), ("w_cmp_v2", 128)):
    PARAM[_n] = (_at, _w)
    _at += _w
N_PARAM = _at

STREAM = {}
_at = 0
for _n, _w in (("w_in", 52), ("pool_up", 4), ("dn_up", 8), ("mix_out", 8), ("query", 16),
               ("ada", 24), ("experts", 256), ("w_in_2", 37), ("v_tok", 4), ("cmp_k1", 4), ("cmp_v1", 4),
               ("o_nsa", 4), ("o_swa", 4), ("w_out", 8)):
    STREAM[_n] = _at
    _at += _w
N_STREAM = _at


class Steps:

    def __init__(self, sem, names):
        self.sem, self.names = sem, names

    def done(self, rnd, name):
        return rnd * len(self.names) + self.names.index(name) + 1


def program(nc, x_in, stream, params_in, consts_in, keys_in, out):
    f32, u32 = mybir.dt.float32, mybir.dt.uint32
    ALU, ACT, AX = mybir.AluOpType, mybir.ActivationFunctionType, mybir.AxisListType
    ds = bass.ds
    gate_dram = nc.dram_tensor("gate_matrix", [S // BLOCK_T, P, EXPERTS_A, BLOCK_T], f32).ap()

    with ExitStack() as ctx:
        def sb(name, cols, dt=f32):
            return ctx.enter_context(nc.sbuf_tensor(name, [P, cols], dt))

        def sem(name):
            return ctx.enter_context(nc.semaphore(name))

        consts = sb("consts", N_CONST)
        params = sb("params", N_PARAM)
        acts_at = -(-nc.sbuf_base // 32) * 32
        acts = sb("acts", 2 * KT * S)
        ring = sb("ring", RING * 1024)[:, :].rearrange("p (s n) -> p s n", s=RING)
        RS = sb("rstd", S)
        small = sb("small", 1024)
        work_at = -(-nc.sbuf_base // 32) * 32
        work = sb("work", 31600)
        ps = ctx.enter_context(nc.psum_tensor("ps", [P, 8, 512], f32))

        def const(name):
            a, w = CONST[name]
            return consts[:, a:a + w]

        def param(name):
            a, w = PARAM[name]
            return params[:, a:a + w]

        ident, ones, upper, iota = (const(n) for n in ("ident", "ones", "upper", "iota"))

        def view(base, at, *dims):
            n = int(np.prod(dims))
            assert at + n <= base.shape[1], (at, dims)
            v = base[:, at:at + n]
            if len(dims) == 1:
                return v
            names = "abcd"[:len(dims)]
            return v.rearrange(f"p ({' '.join(names)}) -> p {' '.join(names)}", **dict(zip(names, dims)))

        def over(ap, axis, n):
            v = ap.unsqueeze(axis)
            shape = list(v.shape)
            shape[axis] = n
            return v.broadcast_to(shape)

        XT = view(acts, 0, KT, S)
        XN = view(acts, KT * S, KT, S)

        class Region:

            def __init__(self, base, at=0):
                self.base, self.at = base, at

            def take(self, *dims):
                v = view(self.base, self.at, *dims)
                self.at += int(np.prod(dims))
                return v

        sm = Region(small)
        w32 = sm.take(KT)
        ea, beta, a_in, sp_a, sp_b = sm.take(8), sm.take(TT, 8), sm.take(TT, 8), sm.take(TT, 8), sm.take(TT, 8)
        g_log, gc, egc, nbeg = sm.take(TT, 8), sm.take(TT, 8), sm.take(TT, 8), sm.take(TT, 8)
        mod, g_eff = sm.take(24), sm.take(KT)
        mx, nm, den, fac = sm.take(3, TT), sm.take(3, TT), sm.take(3, TT), sm.take(3, TT)
        esink, gn = sm.take(3, TT), sm.take(TT, 24)
        KC, VC = sm.take(64), sm.take(2, 64)
        zero_exp, zero_v, zero_w, rtok, RS16 = sm.take(8), sm.take(8), sm.take(8), sm.take(TT), sm.take(16)

        r1 = Region(work)
        QKV, Z, GT = r1.take(24, S), r1.take(KT, S), r1.take(16, S)
        SIDE = r1.at
        XA, pool_tmp = r1.take(4, 16 + S), r1.take(2, 16 + S)
        RAW, CONV = r1.take(2, 3 + S), r1.take(2, S)

        class Slot:

            def __init__(self, region):
                t = region.take
                self.sq, self.ed, self.et, self.df = t(2, S), t(TT, HD), t(TT, HD), t(TT, HD)
                self.lk, self.t, self.tt, self.vb = t(TT, HD), t(TT, HD), t(TT, HD), t(TT, HD)
                self.kt, self.state, self.r, self.vn = t(TT, HD), t(HD), t(HD), t(HD)
                self.rqk = t(8)
                self.egl, self.edl, self.oss, self.ors = t(TT), t(TT), t(TT), t(TT)
                self.gu = self.sq[:, 0, :].rearrange("p (c t) -> p c t", c=TT)
                self.x = self.sq[:, 1, :].rearrange("p (c t) -> p c t", c=TT)

        slots = [Slot(Region(acts)), Slot(Region(work, SIDE))]

        r2 = Region(work)
        QP, keys = r2.take(16, S), r2.take(16, P)
        SC, SC2, CAND, CAND2 = r2.take(2, TT, P), r2.take(TT, P), r2.take(TT, 256), r2.take(TT, 256)
        CAND_FLAT = CAND.rearrange("p c n -> p (c n)")
        V1, I1, I1F = r2.take(TT, 16, TOPK), r2.take(TT, 16, TOPK), r2.take(TT, 16, TOPK)
        TOP, POS, PF = r2.take(TT, 8, TOPK), r2.take(TT, 8, TOPK), r2.take(2, TT, 8, TOPK)
        SEL, EQ = r2.take(2, TT, 128), r2.take(2, 2048)
        GSUM = r2.take(TT, 8)
        PU = SC2
        TR = Region(work, 31600 - 1536)
        I1T, I2T, GTT = TR.take(S), TR.take(S), TR.take(S)
        r3 = Region(work)
        ONE_A, ONE_B = r3.take(16, P), r3.take(16, P)
        GB = r3.take(2, EXPERTS_A, BLOCK_T)
        def split_at(name, base, at, *dims):
            t = nc.alloc_sbuf_tensor_at(name, [P, int(np.prod(dims))], mybir.dt.float32r, offset=base + 4 * at)
            return view(t, 0, *dims)

        UH, UL = split_at("up_hi", work_at, 0, GROUP, 1024), split_at("up_lo", work_at, 4096, GROUP, 1024)
        WH, WL = (split_at("act_hi", work_at, 8192, 2, GROUP, S), split_at("act_lo", work_at, 12288, 2, GROUP, S))
        GG = view(work, 16384, 2, 8, GROUP, BLOCK_T)
        XH, XL = split_at("x_hi", work_at, 20480, KT, S), split_at("x_lo", work_at, 24576, KT, S)
        GE = view(work, 28672, 2, S)
        DH, DL = split_at("down_hi", acts_at, KT * S, 2, 1024), split_at("down_lo", acts_at, KT * S + 2048, 2, 1024)
        assert max(r2.at, r3.at) <= 31600 - 1536

        r5 = Region(work)
        QA, ZZ, GT2, KD, VT = r5.take(8, S), r5.take(8, S), r5.take(16, S), r5.take(3, 2, S), r5.take(TT, 384)
        at2 = r5.at
        KK, XC, CB, HID = r5.take(5, S), r5.take(2, 2, S), r5.take(2, 16, 62), r5.take(2, 2, 62)
        r6 = Region(work, at2)
        SS, PT = r6.take(3, TT, S), view(acts, KT * S, 2, TT, S)

        w_loaded = [sem(f"w_loaded_{s}") for s in range(RING)]
        tile_done = sem("tile_done")
        bank_free = [sem(f"bank_free_{b}") for b in range(4)]
        x_loaded, par_loaded, keys_loaded = sem("x_loaded"), sem("par_loaded"), sem("keys_loaded")
        v_chain, a_chain, g_chain = sem("v_chain"), sem("a_chain"), sem("g_chain")
        rs_out = sem("rs_out")
        norm_diag, norm_bc = sem("norm_diag"), sem("norm_bc")
        norm_sq, norm_ss, norm_done = sem("norm_sq"), sem("norm_ss"), sem("norm_done")
        pads, conv_part, conv_done, silu_done = sem("pads"), sem("conv_part"), sem("conv_done"), sem("silu_done")
        pool_ready, pooly_done, yt_ready = sem("pool_ready"), sem("pooly_done"), sem("yt_ready")
        ba_done, ba_v, ba_a, gc_done, gc_ready = sem("ba_done"), sem("ba_v"), sem("ba_a"), sem("gc_done"), sem("gc_ready")
        T_STEPS = ["sumsq", "spread", "turn", "gram", "decay", "lt", "t1"]
        A_STEPS = ["sq", "root", "ktok", "e", "eg", "lts"]
        V_STEPS = ["rd", "norm", "vb", "gu", "diff", "l", "at", "tt", "t"]
        for l in range(1, LEVELS):
            T_STEPS += [f"x{l}", f"tx{l}"]
            A_STEPS += [f"x{l}"]
            V_STEPS += [f"u{l}"]
        for c in range(TT):
            T_STEPS += [f"pq{c}"] * (c > 0) + [f"v{c}", f"os{c}"]
            A_STEPS += [f"vn{c}"]
            V_STEPS += [f"r{c}"] * (c > 0) + [f"s{c}"] * (c < TT - 1) + [f"o{c}"]
        dT = [Steps(sem(f"delta_pe_{p}"), T_STEPS + ["turn_o"]) for p in range(2)]
        dA = [Steps(sem(f"delta_act_{p}"), A_STEPS + ["oroot"]) for p in range(2)]
        dV = [Steps(sem(f"delta_dve_{p}"), V_STEPS + ["dg", "fin"]) for p in range(2)]
        dG = [Steps(sem(f"delta_pool_{p}"), ["edm", "etm", "kdec"] + [f"lk{l}" for l in range(LEVELS)])
              for p in range(2)]
        gated, merged, mixed = sem("gated"), sem("merged"), sem("mixed")
        qp_ready, sc_done, sc_ready, topk_done, cand_ready = (sem(n) for n in (
            "qp_ready", "sc_done", "sc_ready", "topk_done", "cand_ready"))
        cand_used, eq_ready, eq_mul, sel_ready = sem("cand_used"), sem("eq_ready"), sem("eq_mul"), sem("sel_ready")
        i1f_ready = sem("i1f_ready")
        gd_ready, ge_ready, gate_ready = sem("gd_ready"), sem("ge_ready"), sem("gate_ready")
        turned, turned_read = sem("turned"), sem("turned_read")
        onehot_a, onehot_b, gated_a = sem("onehot_a"), sem("onehot_b"), sem("gated_a")
        token_mm, gate_out = sem("token_mm"), sem("gate_out")
        gate_written = [sem(f"gate_written_{p}") for p in range(2)]
        gate_loaded = [sem(f"gate_loaded_{p}") for p in range(2)]
        gelu_done, w_done, y_done, acc_done = sem("gelu_done"), sem("w_done"), sem("y_done"), sem("acc_done")
        x_hi, x_lo, split_hi, split_lo, prod_done = (sem(n) for n in ("x_hi", "x_lo", "split_hi", "split_lo", "prod_done"))
        w_hi = sem("w_hi")
        k_ready, dup_done, xc_ready, cb_ready = sem("k_ready"), sem("dup_done"), sem("xc_ready"), sem("cb_ready")
        v_ready, hid_ready, kv_done, kc_ready = sem("v_ready"), sem("hid_ready"), sem("kv_done"), sem("kc_ready")
        proj_ready = sem("proj_ready")
        at_scored, at_scaled, at_exp, at_fac = sem("at_scored"), sem("at_scaled"), sem("at_exp"), sem("at_fac")
        at_read, at_weighted = sem("at_read"), sem("at_weighted")
        at_turned, at_copied, at_out, o_ready = sem("at_turned"), sem("at_copied"), sem("at_out"), sem("o_ready")
        yy_ready, out_ready, out_written = sem("yy_ready"), sem("out_ready"), sem("out_written")

        UNITS = [(kind, h) for h in range(8) for kind in ("cmp", "slc", "win")] + [("swa", h) for h in range(8)]

        def turns(kind):
            if kind == "cmp":
                return [(0, range(TT))]
            if kind == "swa":
                return [(k, range(k, min(k + 2, TT))) for k in range(TT)]
            return [(k, range(k, TT)) for k in range(TT)]

        CHUNKS = [0]
        for kind, _ in UNITS:
            CHUNKS.append(CHUNKS[-1] + len(turns(kind)))
        O_USE = {h: i for i, h in enumerate(range(0, 16, 2))}

        def key_cols(kind, i):
            if kind == "cmp":
                return NC_CMP, 0
            if kind == "swa":
                return (2 * P, (i - 1) * P) if i else (P, 0)
            return (i + 1) * P, 0

        SPLIT_U, SPLIT_D = (6, 8, 10, 11), (4, 5, 7, 9)

        def nth(base, later):
            return base[0] if later is None else later * base[1] + base[0]

        def pair_side(v, level, side):
            return v.rearrange("p (a s n) -> p a s n", s=2, n=2 ** level)[:, :, side, :]

        block = ctx.enter_context(nc.Block())

        @block.sync
        def _(sp):
            for s in range(RING):
                sp.dma_start(ring[:, s, :], stream[s, :, :]).then_inc(w_loaded[s], 16)
            loops = (N_STREAM - RING) // RING
            with sp.Fori(0, loops) as i:
                for s in range(RING):
                    sp.wait_ge(tile_done, i * RING + (s + 1))
                    sp.dma_start(ring[:, s, :], stream[ds(i * RING + (RING + s), 1), :, :]
                                 .rearrange("o p n -> p (o n)")).then_inc(w_loaded[s], 16)
            for n in range(RING * (loops + 1), N_STREAM):
                sp.wait_ge(tile_done, n - RING + 1)
                sp.dma_start(ring[:, n % RING, :], stream[n, :, :]).then_inc(w_loaded[n % RING], 16)

        @block.gpsimd
        def _(pool):
            g_ = nc.gpsimd
            count = [0]

            def link(ins):
                count[0] += 1
                ins.then_inc(g_chain, 1)
                pool.wait_ge(g_chain, count[0])

            pool.wait_ge(pads, 1)
            pool.wait_ge(par_loaded, 32)
            first = const("first").rearrange("p (g n) -> p g n", g=4)
            for g in range(4):
                pool.wait_ge(bank_free[g], 1)
                src = XA[:, g, :]
                for x in range(g + 1):
                    dst = pool_tmp[:, x % 2, :]
                    link(g_.tensor_tensor(dst[:, 16:], src[:, 16:], src[:, 16 - 2 ** x:16 + S - 2 ** x], ALU.add))
                    src = dst
                link(g_.tensor_tensor(RS16, src[:, 16:32], first[:, g, :], ALU.mult))
                link(g_.tensor_tensor(RS16, RS16, XA[:, g, 16:32], ALU.subtract))
                link(g_.tensor_scalar(src[:, 16:], src[:, 16:], 1.0 / 2 ** (g + 1), None, ALU.mult))
                link(g_.tensor_tensor(XA[:, g, 16:], src[:, 16:], XA[:, g, 16:], ALU.subtract))
                link(g_.tensor_copy(XA[:, g, 16:32], RS16))
            g_.memset(RS16, 0.0).then_inc(pool_ready, 1)

            own = [0, 0]
            for r in range(HEADS // 2):
                def each(fn, steps=1):
                    for p in range(2):
                        if own[p]:
                            pool.wait_ge(dG[p].sem, own[p])
                        fn(p, 2 * r + p, slots[p])
                        own[p] += steps

                def edm(p, h, s):
                    pool.wait_ge(dA[p].sem, dA[p].done(r, "e"))
                    link(g_.tensor_tensor(s.ed, s.ed, over(const("strict"), 1, TT), ALU.mult))
                    g_.tensor_tensor(s.ed, s.ed, over(beta[:, :, h], 2, P), ALU.mult).then_inc(dG[p].sem, 1)

                def etm(p, h, s):
                    g_.tensor_tensor(s.et, s.et, over(upper, 1, TT), ALU.mult).then_inc(dG[p].sem, 1)
                    pool.wait_ge(dA[p].sem, dA[p].done(r, "eg"))
                    g_.tensor_tensor(s.kt, s.kt, over(s.edl, 2, HD), ALU.mult).then_inc(dG[p].sem, 1)

                each(edm)
                each(etm, 2)
                for l in range(LEVELS):
                    def lk(p, h, s):
                        if l == 0:
                            pool.wait_ge(dA[p].sem, dA[p].done(r, "lts"))
                            if r:
                                pool.wait_ge(dT[p].sem, dT[p].done(r - 1, "turn_o"))
                        elif l == 1:
                            pool.wait_ge(dV[p].sem, dV[p].done(r, "tt"))
                        else:
                            pool.wait_ge(dT[p].sem, dT[p].done(r, f"x{l - 1}"))
                        m = const("block")[:, l * P:(l + 1) * P]
                        g_.tensor_tensor(s.lk, s.df, over(m, 1, TT), ALU.mult).then_inc(dG[p].sem, 1)
                    each(lk)

            for d in range(KT):
                pool.wait_ge(bank_free[d % 4], (60 + d) // 4 + 1)
                last = g_.tensor_tensor(XN[:, d, :], GT[:, d, :], GT[:, 8 + d, :], ALU.add)
            last.then_inc(merged, 1)
            for h in range(8):
                pool.wait_ge(topk_done, 2 * h + 2)
                if h:
                    pool.wait_ge(cand_used, h)
                for c in range(TT):
                    last = g_.tensor_tensor(CAND[:, c, :].rearrange("p (a b) -> p a b", a=16),
                                            over(V1[:, c, 2 * h, :], 2, 16), over(V1[:, c, 2 * h + 1, :], 1, 16), ALU.add)
                last.then_inc(cand_ready, 1)
            pool.wait_ge(i1f_ready, 1)
            for x in range(8):
                c, z = divmod(x, 2)
                pool.wait_ge(eq_ready, x + 1)
                e = EQ[:, x % 2, :].rearrange("p (h k j) -> p h k j", h=8, k=16)
                idx = I1F[:, c, :, :].rearrange("p (h z) j -> p h z j", z=2)[:, :, z, :]
                g_.tensor_tensor(e, e, over(idx, 2, 16), ALU.mult).then_inc(eq_mul, 1)

            with pool.Fori(0, S // 16) as j:
                for u in range(0, 16, 4):
                    pool.wait_ge(onehot_a, j * 4 + (u // 4 + 1))
                    rows = ONE_A[:, u:u + 4, :]
                    g_.tensor_tensor(rows, rows, over(GTT[:, ds(j * 16 + u, 4)], 2, P), ALU.mult)\
                        .then_inc(gated_a, 1)

            def load(g, par):
                pool.dma_start(GG[:, par, :, :, :].rearrange("p c e t -> p c (e t)"),
                               gate_dram[:, :, ds(g * GROUP, GROUP), :].rearrange("c p e t -> p c (e t)"))\
                    .then_inc(gate_loaded[par], 16)

            for par in range(2):
                pool.wait_ge(gate_written[par], 16 * (S // BLOCK_T // 2) + 16)
            load(0, 0)
            load(1, 1)
            with pool.Fori(0, 15) as i:
                pool.wait_ge(w_done, i * 8 + 4)
                load(i * 2 + 2, 0)
                pool.wait_ge(w_done, i * 8 + 8)
                load(i * 2 + 3, 1)

            for m in range(124, 129):
                pool.wait_ge(bank_free[m % 4], m // 4 + 1)
            for g in range(2):
                src = KK[g * 64:(g + 1) * 64, :, :]
                pool.dma_start(XC[0:64, :, g, :], src[:, 0:2, :]).then_inc(xc_ready, 16)
                pool.dma_start(XC[64:128, :, g, 0:S - 1], src[:, 0:2, 1:S]).then_inc(xc_ready, 16)
            for g in range(2):
                src = KK[g * 64:(g + 1) * 64, :, :]
                for half in range(2):
                    pool.dma_start(KD[half * 64:(half + 1) * 64, :, g, :], src[:, 2:5, :]).then_inc(dup_done, 16)
            for u, (kind, h) in enumerate(UNITS):
                pool.wait_ge(at_fac, u + 1)
                for i in range(TT):
                    p_ = SS[:, u % 3, i, 0:key_cols(kind, i)[0]]
                    last = g_.tensor_scalar(p_, p_, fac[:, u % 3, i:i + 1], None, ALU.mult)
                last.then_inc(at_weighted, 1)
            for d in range(KT):
                pool.wait_ge(bank_free[(137 + d) % 4], (137 + d) // 4 + 1)
                last = g_.tensor_tensor(XN[:, d, :], GT2[:, d, :], GT2[:, 8 + d, :], ALU.add)
            last.then_inc(merged, 1)
            pool.wait_ge(dup_done, 64)

        @block.scalar
        def _(act):
            def link(ins):
                a_count[0] += 1
                ins.then_inc(a_chain, 1)
                act.wait_ge(a_chain, a_count[0])

            a_count = [0]

            def take(m, dst, func, i=None, per=8):
                return nc.scalar.activation(dst, ps[:, m % 4, :], func)

            def square(j, src):
                nc.scalar.activation(view(acts, KT * S, KT * S), src, ACT.Square).then_inc(norm_sq, 1)

            def root(j):
                act.wait_ge(norm_ss, j + 1)
                nc.scalar.activation(rtok, ps[:, 7, 0:TT], ACT.Sqrt, bias=const("eps")[:, 1:2]).then_inc(rs_out, 1)

            act.dma_start(view(acts, 0, KT * S), x_in).then_inc(x_loaded, 16)
            act.dma_start(params[:, :], params_in).then_inc(par_loaded, 16)
            act.dma_start(consts[:, :], consts_in).then_inc(par_loaded, 16)
            act.wait_ge(x_loaded, 16)
            square(0, view(acts, 0, KT * S))
            act.wait_ge(par_loaded, 32)
            root(0)
            nc.scalar.activation(ea, param("a_log"), ACT.Exp).then_inc(silu_done, 2)
            for m in range(4):
                act.wait_ge(tile_done, m + 1)
                take(m, XA[:, m, 16:], ACT.Copy).then_inc(bank_free[m % 4], 1)
            with act.Fori(0, 3) as i:
                for u in range(8):
                    act.wait_ge(tile_done, i * 8 + (5 + u))
                    act.wait_ge(conv_done, i * 8 + (u + 1))
                    take(4 + u, RAW[:, u % 2, 3:], ACT.Copy).then_inc(bank_free[u % 4], 1)
                    act.wait_ge(conv_done, i * 8 + (u + 3))
                    nc.scalar.activation(QKV[:, ds(i * 8 + u, 1), :].rearrange("p o t -> p (o t)"),
                                         CONV[:, u % 2, :], ACT.Silu).then_inc(silu_done, 1)
            for u in range(8):
                act.wait_ge(tile_done, 29 + u)
                take(28 + u, Z[:, u, :], ACT.Silu).then_inc(bank_free[u % 4], 1)
            with act.Fori(0, 2) as i:
                for u in range(8):
                    act.wait_ge(tile_done, i * 8 + (37 + u))
                    take(36 + u, GT[:, ds(i * 8 + u, 1), :].rearrange("p o t -> p (o t)"), ACT.Sigmoid)\
                        .then_inc(bank_free[u % 4], 1)
            for g in range(4):
                act.wait_ge(pooly_done, g + 1)
                nc.scalar.activation(XA[:, g, 16:], ps[:, 4 + g, :], ACT.Copy,
                                     scale=param("pool_scale")[:, g:g + 1]).then_inc(yt_ready, 1)
            act.wait_ge(ba_v, 1)
            logits = ps[:, 4, 0:64].rearrange("p (c n) -> p c n", c=TT)
            nc.scalar.activation(beta, logits[:, :, 0:8], ACT.Sigmoid).then_inc(ba_a, 1)
            act.wait_ge(ba_v, 1)
            link(nc.scalar.activation(sp_a, sp_a, ACT.Exp, scale=-1.0))
            nc.scalar.activation(sp_b, sp_a, ACT.Ln, bias=1.0).then_inc(ba_a, 1)
            act.wait_ge(ba_v, 3)
            nc.scalar.activation(egc, gc, ACT.Exp).then_inc(ba_a, 1)

            act.wait_ge(silu_done, 26)
            act.wait_ge(tile_done, 56)
            own = [0, 0]
            for r in range(HEADS // 2):
                def each(fn, steps=1):
                    for p in range(2):
                        if own[p]:
                            act.wait_ge(dA[p].sem, own[p])
                        fn(p, 2 * r + p, slots[p], 4 * p)
                        own[p] += steps

                def four(v):
                    return v.rearrange("p c t -> p (c t)")

                def sq(p, h, s, b):
                    nc.scalar.activation(s.sq[:, 0, :], QKV[:, h, :], ACT.Square)
                    nc.scalar.activation(s.sq[:, 1, :], QKV[:, 8 + h, :], ACT.Square).then_inc(dA[p].sem, 1)

                def root_qk(p, h, s, b):
                    act.wait_ge(dT[p].sem, dT[p].done(r, "sumsq"))
                    nc.scalar.activation(s.rqk, ps[:, b, 0:8], ACT.Sqrt, bias=const("eps")[:, 0:1])\
                        .then_inc(dA[p].sem, 1)

                def ktok(p, h, s, b):
                    act.wait_ge(dT[p].sem, dT[p].done(r, "turn"))
                    nc.scalar.activation(four(s.kt), ps[:, b, :], ACT.Copy).then_inc(dA[p].sem, 1)

                def e(p, h, s, b):
                    act.wait_ge(dV[p].sem, dV[p].done(r, "diff"))
                    nc.scalar.activation(s.ed, s.ed, ACT.Exp, scale=-1.0)
                    nc.scalar.activation(s.et, s.et, ACT.Exp).then_inc(dA[p].sem, 1)
                    gl = ps[:, b, :].rearrange("p (c t) -> p c t", c=TT)[:, :, P - 1]
                    nc.scalar.activation(s.egl, gl, ACT.Exp)
                    nc.scalar.activation(s.edl, s.df[:, :, P - 1], ACT.Exp).then_inc(dA[p].sem, 1)

                def lts(p, h, s, b):
                    act.wait_ge(dT[p].sem, dT[p].done(r, "lt"))
                    nc.scalar.activation(four(s.df), ps[:, b + 1, :], ACT.Copy).then_inc(dA[p].sem, 1)

                for fn in (sq, root_qk, ktok):
                    each(fn)
                each(e, 2)
                each(lts)
                for l in range(1, LEVELS):
                    def x(p, h, s, b):
                        act.wait_ge(dT[p].sem, dT[p].done(r, f"x{l}"))
                        nc.scalar.activation(four(s.x), ps[:, b, :], ACT.Copy).then_inc(dA[p].sem, 1)
                    each(x)
                for c in range(TT):
                    def vn(p, h, s, b):
                        act.wait_ge(dT[p].sem, dT[p].done(r, f"v{c}"))
                        nc.scalar.activation(s.vn, ps[:, b + 1, 0:P], ACT.Copy).then_inc(dA[p].sem, 1)
                    each(vn)

                def osq(p, h, s, b):
                    act.wait_ge(dV[p].sem, dV[p].done(r, f"o{TT - 1}"))
                    for c in range(TT):
                        last = nc.scalar.activation(s.x[:, c, :], s.t[:, c, :], ACT.Square,
                                                    accum_out=s.oss[:, c:c + 1])
                    link(last)
                    nc.scalar.activation(s.ors, s.oss, ACT.Sqrt, scale=1.0 / HD, bias=const("eps")[:, 0:1])\
                        .then_inc(dA[p].sem, 1)
                each(osq)

            for p in range(2):
                act.wait_ge(dV[p].sem, dV[p].done(3, "fin"))
            act.dma_start(view(acts, 0, KT * S), x_in).then_inc(x_loaded, 16)
            act.dma_start(keys.rearrange("p a b -> p (a b)"), keys_in).then_inc(keys_loaded, 16)
            for b in range(4):
                act.wait_ge(bank_free[b], 19)
            square(1, view(acts, 0, KT * S))
            root(1)
            for hz in range(17):
                if hz < 16:
                    act.wait_ge(tile_done, STREAM["query"] + hz + 1)
                    take(76 + hz, QP[:, hz, :], ACT.Copy).then_inc(bank_free[hz % 4], 1)
                if hz:
                    q = hz - 1
                    act.wait_ge(sc_done, q + 1)
                    if q >= 2:
                        act.wait_ge(topk_done, q - 1)
                    nc.scalar.activation(SC[:, q % 2, :, :].rearrange("p c t -> p (c t)"), ps[:, 4 + q % 4, :],
                                         ACT.Copy).then_inc(sc_ready, 1)
            act.wait_ge(gd_ready, 1)
            nc.scalar.activation(TOP.rearrange("p c h k -> p (c h k)"), view(CAND_FLAT, 0, 512), ACT.Exp)\
                .then_inc(ge_ready, 1)
            nc.scalar.activation(zero_exp[:, 0:1], ea[:, 0:1], ACT.Copy).then_inc(gate_out, 4)
            nc.scalar.activation(zero_exp[:, 1:2], ea[:, 0:1], ACT.Copy).then_inc(gate_written[0], 16)
            nc.scalar.activation(zero_exp[:, 2:3], ea[:, 0:1], ACT.Copy).then_inc(gate_written[1], 16)
            for n, dst in enumerate((I1T, I2T, GTT)):
                act.wait_ge(turned, n + 1)
                nc.scalar.activation(dst, ps[:, 4 + n, :], ACT.Copy).then_inc(turned_read, 1)
            nc.scalar.activation(XH.rearrange("p k t -> p (k t)"), view(acts, KT * S, KT * S), ACT.Copy)\
                .then_inc(x_hi, 1)
            with act.Fori(0, S // BLOCK_T // 2) as cc:
                for par in range(2):
                    act.wait_ge(gate_written[par], cc * 16 + 16)
                    with act.Fori(0, BLOCK_T // 16) as j:
                        for q in range(4):
                            act.wait_ge(token_mm, cc * (32 * 4) + j * 16 + (par * 64 + 4 * (q + 1) + 16))
                            nc.scalar.activation(
                                GB[:, par, :, ds(j * 16 + 4 * q, 4)],
                                ps[:, 4 + q, :].rearrange("p (t i) -> p i t", t=4), ACT.Copy)\
                                .then_inc(gate_out, 1)
                    act.wait_ge(gate_out, cc * 32 + (16 * (par + 1) + 4))
                    act.dma_start(gate_dram[ds(cc * 2 + par, 1), :, :, :].rearrange("o p i t -> p (o i t)"),
                                  GB[:, par, :, :].rearrange("p i t -> p (i t)")).then_inc(gate_written[par], 16)
            for par in range(2):
                act.wait_ge(gate_written[par], 16 * (S // BLOCK_T // 2) + 16)
            e0 = STREAM["experts"]

            def high(n, dst, freed, i):
                act.wait_ge(w_loaded[n % RING], nth((16 * (n // RING + 1), 32), i))
                if freed is not None:
                    act.wait_ge(tile_done, nth((freed + 1, 16), i))
                nc.scalar.activation(dst, ring[:, n % RING, :], ACT.Copy).then_inc(split_hi, 1)

            def down_tile(g, e):
                return e0 + (e if g == 0 else 8 * g - 4 + e)

            def high_down(g, e, i=None):
                n = down_tile(g, e)
                freed = n - 2 if e >= 2 else (down_tile(g - 1, e + 2) if g else None)
                high(n, DH[:, e % 2, :], freed, i)

            def high_up(g, e, i=None):
                n = e0 + 8 * g + 8 + e if g < 31 else e0 + 252 + e
                high(n, UH[:, e, :], n - 8 if 0 < g < 31 else (n - 4 if g == 31 else None), i)

            def acts_of(g, e, i=None):
                act.wait_ge(tile_done, nth((down_tile(g, e) + 1, 16), i))
                if g or e >= 2:
                    act.wait_ge(w_done, nth((4 * g + e - 1, 8), i))
                nc.scalar.activation(GE[:, e % 2, :], ps[:, e % 2, :], ACT.Gelu).then_inc(gelu_done, 1)
                act.wait_ge(prod_done, nth((4 * g + e + 1, 8), i))
                nc.scalar.activation(WH[:, g % 2, e, :], GE[:, e % 2, :], ACT.Copy).then_inc(w_hi, 1)

            def step(g, i=None):
                for e in range(GROUP):
                    high_up(g, e, i)
                    if e < 2:
                        high_down(g + 1, e + 2, i)
                    acts_of(g + 1, e, i)
                if g < 30:
                    for e in range(2):
                        high_down(g + 2, e, i)

            for e in range(2):
                high_down(0, e)
            for e in range(GROUP):
                if e < 2:
                    high_down(0, e + 2)
                acts_of(0, e)
            for e in range(2):
                high_down(1, e)
            step(0)
            step(1)
            with act.Fori(1, 15) as i:
                for g in range(2, 4):
                    step(g, i - 1)
            step(30)
            for e in range(GROUP):
                high_up(31, e)
            act.wait_ge(acc_done, 8 * 32 + 8)
            square(2, view(acts, 0, KT * S))
            root(2)
            act.wait_ge(norm_done, 3)
            square(3, view(acts, 0, KT * S))
            root(3)

            n0 = STREAM["w_in_2"]
            for u in range(16):
                act.wait_ge(tile_done, n0 + u + 1)
                take(92 + u, QA[:, u, :] if u < 8 else ZZ[:, u - 8, :], ACT.Copy if u < 8 else ACT.Silu)\
                    .then_inc(bank_free[u % 4], 1)
            with act.Fori(0, 2) as i:
                for u in range(8):
                    act.wait_ge(tile_done, i * 8 + (n0 + 17 + u))
                    take(108 + u, GT2[:, ds(i * 8 + u, 1), :].rearrange("p o t -> p (o t)"), ACT.Sigmoid)\
                        .then_inc(bank_free[u % 4], 1)
            for u in range(5):
                act.wait_ge(tile_done, n0 + 33 + u)
                take(124 + u, KK[:, u, :], ACT.Copy).then_inc(bank_free[u % 4], 1)
            act.wait_ge(tile_done, STREAM["v_tok"] + 4)
            for c in range(TT):
                nc.scalar.activation(VT[:, c, :], ps[:, 4 + c, 0:384], ACT.Copy)
                nc.scalar.activation(gn[:, c, :], ps[:, 4 + c, 384:408], ACT.Sigmoid).then_inc(v_ready, 1)
            for kv in range(2):
                act.wait_ge(tile_done, STREAM["cmp_k1" if kv == 0 else "cmp_v1"] + 4)
                for a in range(2):
                    last = nc.scalar.activation(HID[:, kv, a, :], ps[:, 4 + 2 * kv + a, 0:62], ACT.Silu)
                last.then_inc(hid_ready, 1)
            act.wait_ge(kv_done, 1)
            nc.scalar.activation(KC[:, 0:62], ps[:, 0, 0:62], ACT.Copy)
            nc.scalar.activation(VC[0:NC_CMP, :, :].rearrange("p g d -> p (g d)"), ps[0:NC_CMP, 1, 0:128], ACT.Copy)\
                .then_inc(kc_ready, 1)

            def exps(u):
                kind, h = UNITS[u]
                par = u % 3
                act.wait_ge(at_scaled, u + 1)
                if kind == "swa":
                    nc.scalar.activation(esink[:, par, :], nm[:, par, :], ACT.Exp, bias=param("sinks")[:, h:h + 1])
                for i in range(TT):
                    w, _ = key_cols(kind, i)
                    last = nc.scalar.activation(SS[:, par, i, 0:w], SS[:, par, i, 0:w], ACT.Exp,
                                                bias=nm[:, par, i:i + 1], scale=NSA_SCALE,
                                                accum_out=den[:, par, i:i + 1])
                last.then_inc(at_exp, 1)

            def copies(u):
                kind, h = UNITS[u]
                par = u % 2
                if u >= 2:
                    act.wait_ge(at_out, u - 1)
                for x, (kt, tiles) in enumerate(turns(kind)):
                    chunk = CHUNKS[u] + x
                    act.wait_ge(at_turned, chunk + 1)
                    m = NC_CMP if kind == "cmp" else P
                    a, b = tiles[0] * P, (tiles[-1] + 1) * P
                    nc.scalar.activation(PT[0:m, par, kt, a:b], ps[0:m, 4 + chunk % 2, a:b], ACT.Copy)\
                        .then_inc(at_copied, 1)

            exps(0)
            exps(1)
            for u in range(len(UNITS)):
                copies(u)
                if u + 2 < len(UNITS):
                    exps(u + 2)
            for u in range(8):
                act.wait_ge(tile_done, STREAM["w_out"] + u + 1)
                take(145 + u, ZZ[:, u, :], ACT.Copy).then_inc(bank_free[(145 + u) % 4], 1)
            for u in range(4, 8):
                act.wait_ge(bank_free[(145 + u) % 4], (145 + u) // 4 + 1)
            square(4, ZZ.rearrange("p k t -> p (k t)"))
            root(4)
            act.wait_ge(out_ready, 1)
            act.dma_start(out, view(acts, 0, KT * S)).then_inc(out_written, 16)
            act.wait_ge(out_written, 16)

        @block.vector
        def _(dve):
            v = nc.vector
            count = [0]

            def link(ins):
                count[0] += 1
                ins.then_inc(v_chain, 1)
                dve.wait_ge(v_chain, count[0])

            def norm(j, src, dst, weight):
                link(v.tensor_scalar(w32, weight, float(np.sqrt(D)), None, ALU.mult))
                dve.wait_ge(rs_out, j + 1)
                link(v.reciprocal(rtok, rtok))
                v.tensor_tensor(RS[:, :].rearrange("p (c t) -> p c t", c=TT), over(ident, 1, TT), over(rtok, 2, P),
                                ALU.mult).then_inc(norm_diag, 1)
                dve.wait_ge(norm_bc, j + 1)
                for k in range(KT):
                    last = v.scalar_tensor_tensor(dst[:, k, :], src[:, k, :], w32[:, k:k + 1], ps[:, 7, :],
                                                  ALU.mult, ALU.mult)
                return last

            v.memset(XA[:, :, 0:16], 0.0)
            v.memset(pool_tmp[:, :, 0:16], 0.0).then_inc(pads, 1)
            v.memset(RAW[:, :, 0:3], 0.0).then_inc(conv_done, 2)
            v.memset(zero_v, 0.0).then_inc(token_mm, 16)
            v.memset(zero_w, 0.0).then_inc(acc_done, 8)
            dve.wait_ge(par_loaded, 32)
            dve.wait_ge(x_loaded, 16)
            dve.wait_ge(acc_done, 8)
            norm(0, XT, XN, param("mix_norm_w")).then_inc(norm_done, 1)
            with dve.Fori(0, 3) as i:
                for u in range(8):
                    raw, y = RAW[:, u % 2, :], CONV[:, u % 2, :]
                    dve.wait_ge(bank_free[u % 4], i * 2 + (u // 4 + 2))
                    dve.wait_ge(silu_done, i * 8 + (u + 1))
                    dve.wait_ge(conv_done, i * 8 + (u + 2))

                    def w(tap):
                        return param("conv_w")[:, ds(i * 32 + (u * 4 + tap), 1)]
                    v.tensor_scalar(y, raw[:, 3:3 + S], w(3), None, ALU.mult).then_inc(conv_part, 1)
                    for x in (2, 1, 0):
                        dve.wait_ge(conv_part, i * 24 + (3 * u + 3 - x))
                        v.scalar_tensor_tensor(y, raw[:, x:x + S], w(x), y, ALU.mult, ALU.add)\
                            .then_inc(conv_part if x else conv_done, 1)
            for d in range(KT):
                dve.wait_ge(tile_done, 53 + d // 2)
                v.tensor_tensor(GT[:, d, :], GT[:, d, :], ps[:, d % 4, :], ALU.mult).then_inc(bank_free[d % 4], 1)
            dve.wait_ge(ba_done, 1)
            logits = ps[:, 4, 0:64].rearrange("p (c n) -> p c n", c=TT)
            link(v.tensor_tensor(a_in, logits[:, :, 8:16], over(param("dt_bias"), 1, TT), ALU.add))
            v.scalar_tensor_tensor(sp_a, a_in, -1.0, a_in, ALU.mult, ALU.max).then_inc(ba_v, 1)
            dve.wait_ge(ba_a, 2)
            link(v.scalar_tensor_tensor(sp_b, a_in, 0.0, sp_b, ALU.max, ALU.add))
            v.scalar_tensor_tensor(g_log, sp_b, -1.0, over(ea, 1, TT), ALU.mult, ALU.mult).then_inc(ba_v, 1)
            dve.wait_ge(gc_done, 1)
            v.tensor_copy(gc.rearrange("p c h -> p (c h)"), ps[:, 5, 0:TT * 8]).then_inc(ba_v, 1)
            dve.wait_ge(ba_a, 3)
            v.scalar_tensor_tensor(nbeg, beta, -1.0, egc, ALU.mult, ALU.mult).then_inc(gc_ready, 1)
            dve.wait_ge(gc_ready, 1)

            own = [0, 0]
            for r in range(HEADS // 2):
                def each(fn, steps=1):
                    for p in range(2):
                        if own[p]:
                            dve.wait_ge(dV[p].sem, own[p])
                        fn(p, 2 * r + p, slots[p], 4 * p)
                        own[p] += steps

                def bank(b):
                    return ps[:, b, :].rearrange("p (c t) -> p c t", c=TT)

                def rd(p, h, s, b):
                    dve.wait_ge(dA[p].sem, dA[p].done(r, "root"))
                    link(v.reciprocal(s.rqk, s.rqk))
                    v.tensor_tensor(s.sq.rearrange("p a (c t) -> p (a c) t", c=TT), over(ident, 1, 8),
                                    over(s.rqk, 2, P), ALU.mult).then_inc(dV[p].sem, 1)

                def norm_qk(p, h, s, b):
                    dve.wait_ge(dT[p].sem, dT[p].done(r, "spread"))
                    v.scalar_tensor_tensor(QKV[:, h, :], QKV[:, h, :], HD ** -0.5, ps[:, b, :], ALU.mult, ALU.mult)
                    v.tensor_tensor(QKV[:, 8 + h, :], QKV[:, 8 + h, :], ps[:, b + 1, :], ALU.mult)\
                        .then_inc(dV[p].sem, 1)

                def vb(p, h, s, b):
                    dve.wait_ge(dT[p].sem, dT[p].done(r, "turn"))
                    v.tensor_tensor(s.vb, bank(b + 1), over(beta[:, :, h], 2, HD), ALU.mult).then_inc(dV[p].sem, 1)
                    v.tensor_tensor(s.gu, over(upper, 1, TT), over(g_log[:, :, h], 2, P), ALU.mult)\
                        .then_inc(dV[p].sem, 1)

                def diff(p, h, s, b):
                    dve.wait_ge(dT[p].sem, dT[p].done(r, "decay"))
                    link(v.tensor_tensor(s.df, bank(b), over(gc[:, :, h], 2, P), ALU.subtract))
                    v.tensor_scalar(s.ed, s.df, 0.0, None, ALU.max)
                    v.tensor_scalar(s.et, s.df, 0.0, None, ALU.min).then_inc(dV[p].sem, 1)

                def lower(p, h, s, b):
                    dve.wait_ge(dT[p].sem, dT[p].done(r, "gram"))
                    dve.wait_ge(dG[p].sem, dG[p].done(r, "edm"))
                    v.tensor_tensor(s.ed, bank(b + 2), s.ed, ALU.mult).then_inc(dV[p].sem, 1)
                    dve.wait_ge(dG[p].sem, dG[p].done(r, "etm"))
                    v.tensor_tensor(s.et, bank(b + 3), s.et, ALU.mult).then_inc(dV[p].sem, 1)

                def level0(p, h, s, b):
                    dve.wait_ge(dG[p].sem, dG[p].done(r, "lk0"))
                    v.tensor_tensor(s.tt, over(ident, 1, TT), s.lk, ALU.subtract).then_inc(dV[p].sem, 1)

                def t1(p, h, s, b):
                    dve.wait_ge(dT[p].sem, dT[p].done(r, "t1"))
                    v.tensor_copy(s.t, bank(b)).then_inc(dV[p].sem, 1)

                for fn, steps in ((rd, 1), (norm_qk, 1), (vb, 2), (diff, 1), (lower, 2), (level0, 1), (t1, 1)):
                    each(fn, steps)
                for l in range(1, LEVELS):
                    def up(p, h, s, b):
                        dve.wait_ge(dT[p].sem, dT[p].done(r, f"tx{l}"))
                        dve.wait_ge(dV[p].sem, dV[p].done(r, "t" if l == 1 else f"u{l - 1}"))
                        def less(x, side, pb):
                            o = pair_side(x, l, side)
                            return v.tensor_tensor(o, o, ps[:, pb, 0:256].rearrange("p (a n) -> p a n", n=2 ** l),
                                                   ALU.subtract)
                        if l < LEVELS - 1:
                            less(s.t.rearrange("p c t -> p (c t)"), 0, b + 2)
                        less(s.tt.rearrange("p c t -> p (c t)"), 1, b + 3).then_inc(dV[p].sem, 1)
                    each(up)
                for c in range(TT):
                    def r_(p, h, s, b):
                        dve.wait_ge(dT[p].sem, dT[p].done(r, f"pq{c}"))
                        v.scalar_tensor_tensor(s.r, ps[:, b, 0:P], nbeg[:, c, h:h + 1], s.vb[:, c, :],
                                               ALU.mult, ALU.add).then_inc(dV[p].sem, 1)

                    def so(p, h, s, b):
                        dve.wait_ge(dT[p].sem, dT[p].done(r, f"os{c}"))
                        o = ps[:, b + 1, P:2 * P]
                        if c == 0:
                            v.tensor_copy(s.state, ps[:, b + 1, 2 * P:3 * P]).then_inc(dV[p].sem, 1)
                            v.tensor_copy(s.t[:, c, :], o).then_inc(dV[p].sem, 1)
                            return
                        if c < TT - 1:
                            dve.wait_ge(dV[p].sem, dV[p].done(r, f"s{c - 1}"))
                            v.scalar_tensor_tensor(s.state, s.state, s.egl[:, c:c + 1], ps[:, b + 1, 2 * P:3 * P],
                                                   ALU.mult, ALU.add).then_inc(dV[p].sem, 1)
                        link(v.tensor_scalar(s.t[:, c, :], ps[:, b, P:2 * P], egc[:, c, h:h + 1], None, ALU.mult))
                        v.tensor_tensor(s.t[:, c, :], s.t[:, c, :], o, ALU.add).then_inc(dV[p].sem, 1)

                    if c:
                        each(r_)
                    each(so, 2 if c < TT - 1 else 1)

                def dg(p, h, s, b):
                    dve.wait_ge(dA[p].sem, dA[p].done(r, "oroot"))
                    link(v.reciprocal(s.ors, s.ors))
                    v.tensor_tensor(s.lk, over(ident, 1, TT), over(s.ors, 2, P), ALU.mult).then_inc(dV[p].sem, 1)

                def fin(p, h, s, b):
                    dve.wait_ge(dT[p].sem, dT[p].done(r, "turn_o"))
                    v.scalar_tensor_tensor(Z[:, h, :], ps[:, b + 2, :], param("dn_norm_w"), Z[:, h, :],
                                           ALU.mult, ALU.mult).then_inc(dV[p].sem, 1)
                each(dg)
                each(fin)

            for d in range(KT):
                dve.wait_ge(tile_done, STREAM["dn_up"] + d + 1)
                v.tensor_tensor(GT[:, 8 + d, :], GT[:, 8 + d, :], ps[:, d % 4, :], ALU.mult)\
                    .then_inc(bank_free[d % 4], 1)
            dve.wait_ge(x_loaded, 32)
            for d in range(KT):
                dve.wait_ge(tile_done, STREAM["mix_out"] + d + 1)
                v.tensor_tensor(XT[:, d, :], XT[:, d, :], ps[:, d % 4, :], ALU.add).then_inc(bank_free[d % 4], 1)
            for b in range(4):
                dve.wait_ge(bank_free[b], 19)
            norm(1, XT, XN, param("ffn_norm_w")).then_inc(norm_done, 1)

            i1u, posu = I1.bitcast(u32), POS.bitcast(u32)

            def top16(sources, spare, values, indices, sig):
                for c in range(TT):
                    last = v.max(values[c][:, 0:8], sources[c])
                link(last)
                for c in range(TT):
                    v.max_index(indices[c][:, 0:8], values[c][:, 0:8], sources[c])
                for c in range(TT):
                    last = v.match_replace(spare[c], values[c][:, 0:8], sources[c], -3.0e38)
                link(last)
                for c in range(TT):
                    last = v.max(values[c][:, 8:16], spare[c])
                link(last)
                for c in range(TT):
                    last = v.max_index(indices[c][:, 8:16], values[c][:, 8:16], spare[c])
                last.then_inc(sig, 1)

            def pick(h):
                dve.wait_ge(cand_ready, h + 1)
                top16([CAND[:, c, :] for c in range(TT)], [CAND2[:, c, :] for c in range(TT)],
                      [TOP[:, c, h, :] for c in range(TT)], [posu[:, c, h, :] for c in range(TT)], cand_used)

            for q in range(16):
                dve.wait_ge(sc_ready, q + 1)
                top16([SC[:, q % 2, c, :] for c in range(TT)], [SC2[:, c, :] for c in range(TT)],
                      [V1[:, c, q, :] for c in range(TT)], [i1u[:, c, q, :] for c in range(TT)], topk_done)
                if q % 2 == 0 and q:
                    pick(q // 2 - 1)
            pick(7)
            dve.wait_ge(cand_used, 8)
            dve.wait_ge(topk_done, 16)
            v.tensor_copy(I1F, i1u).then_inc(i1f_ready, 1)
            flat = posu.rearrange("p c h k -> p (c h k)")
            pu = PU.bitcast(u32).rearrange("p c h -> p (c h)")
            for z, (op, n) in enumerate(((ALU.logical_shift_right, 4), (ALU.bitwise_and, 15))):
                link(v.tensor_scalar(pu, flat, n, None, op))
                link(v.tensor_copy(PF[:, z, :, :, :].rearrange("p c h k -> p (c h k)"), pu))
            gtmp = view(CAND_FLAT, 0, TT, 8, TOPK)
            v.tensor_tensor(gtmp, TOP, TOP[:, :, :, 0:1].broadcast_to([P, TT, 8, TOPK]), ALU.subtract)\
                .then_inc(gd_ready, 1)

            def eq(x):
                c, z = divmod(x, 2)
                if x >= 2:
                    dve.wait_ge(sel_ready, x - 1)
                v.tensor_tensor(EQ[:, x % 2, :].rearrange("p (h k j) -> p h k j", h=8, k=16),
                                over(PF[:, z, c, :, :], 3, 16), over(over(iota[:, 0:16], 1, 16), 1, 8),
                                ALU.is_equal).then_inc(eq_ready, 1)

            eq(0)
            for x in range(8):
                if x < 7:
                    eq(x + 1)
                c, z = divmod(x, 2)
                dve.wait_ge(eq_mul, x + 1)
                v.tensor_reduce(SEL[:, z, c, :], EQ[:, x % 2, :].rearrange("p (n j) -> p n j", j=16),
                                AX.X, ALU.add).then_inc(sel_ready, 1)
            dve.wait_ge(tile_done, STREAM["ada"] + 24)
            link(v.tensor_tensor(mod, ps[:, 3, 0:24], param("b_ada"), ALU.add))
            link(v.scalar_tensor_tensor(g_eff, mod[:, 8:16], 1.0, param("g_pre"), ALU.add, ALU.mult))
            dve.wait_ge(ge_ready, 1)
            link(v.tensor_reduce(GSUM, TOP, AX.X, ALU.add))
            link(v.reciprocal(GSUM, GSUM))
            v.tensor_tensor(TOP, TOP, over(GSUM, 3, TOPK), ALU.mult).then_inc(gate_ready, 1)
            dve.wait_ge(x_hi, 1)
            v.tensor_tensor(XL, XN, XH.bitcast(f32), ALU.subtract).then_inc(x_lo, 1)
            dve.wait_ge(turned_read, 3)
            with dve.Fori(0, S // 16) as j:
                for u in range(0, 16, 4):
                    dve.wait_ge(token_mm, j * 16 + (u + 4))
                    for one, key, ready in ((ONE_A, I1T, onehot_a), (ONE_B, I2T, onehot_b)):
                        v.tensor_tensor(one[:, u:u + 4, :], over(iota, 1, 4), over(key[:, ds(j * 16 + u, 4)], 2, P),
                                        ALU.is_equal).then_inc(ready, 1)

            e0 = STREAM["experts"]

            def low(index, n, hi, lo, i):
                dve.wait_ge(split_hi, nth((index + 1, 16), i))
                v.tensor_tensor(lo, ring[:, n % RING, :], hi.bitcast(f32), ALU.subtract).then_inc(split_lo, 1)

            def low_down(g, e, i=None):
                n = e0 + (e if g == 0 else 8 * g - 4 + e)
                low(e if g == 0 else 8 * (g - 1) + SPLIT_D[e], n, DH[:, e % 2, :], DL[:, e % 2, :], i)

            def low_up(g, e, i=None):
                n = e0 + 8 * g + 8 + e if g < 31 else e0 + 252 + e
                low(8 * g + SPLIT_U[e] if g < 31 else 252 + e, n, UH[:, e, :], UL[:, e, :], i)

            def weigh(g, e, i=None):
                if e == 0:
                    dve.wait_ge(gate_loaded[g % 2], nth((16 * (g // 2 + 1), 16), i))
                dve.wait_ge(gelu_done, nth((4 * g + e + 1, 8), i))
                ge = GE[:, e % 2, :]
                v.tensor_tensor(ge.rearrange("p (c t) -> p c t", t=BLOCK_T), ge.rearrange("p (c t) -> p c t", t=BLOCK_T),
                                GG[:, g % 2, :, e, :], ALU.mult).then_inc(prod_done, 1)
                dve.wait_ge(w_hi, nth((4 * g + e + 1, 8), i))
                v.tensor_tensor(WL[:, g % 2, e, :], ge, WH[:, g % 2, e, :].bitcast(f32), ALU.subtract)\
                    .then_inc(w_done, 1)

            def accumulate(g, i=None):
                n = e0 + 8 * g + 8 if g < 31 else e0 + 252
                for d in range(KT):
                    if d < KT - 1:
                        dve.wait_ge(y_done, nth((7 * g + d + 1, 14), i))
                    else:
                        dve.wait_ge(tile_done, nth((n + 4, 16), i))
                    dve.wait_ge(acc_done, nth((8 * g + d + 1, 16), i))
                    v.tensor_tensor(XT[:, d, :], XT[:, d, :], ps[:, 2 + d % 4, :], ALU.add).then_inc(acc_done, 1)

            def step(g, i=None):
                for e in range(GROUP):
                    low_up(g, e, i)
                    if e < 2:
                        low_down(g + 1, e + 2, i)
                    weigh(g + 1, e, i)
                if g < 30:
                    for e in range(2):
                        low_down(g + 2, e, i)
                accumulate(g, i)

            for par in range(2):
                dve.wait_ge(gate_written[par], 16 * (S // BLOCK_T // 2) + 16)
            for e in range(2):
                low_down(0, e)
            for e in range(GROUP):
                if e < 2:
                    low_down(0, e + 2)
                weigh(0, e)
            for e in range(2):
                low_down(1, e)
            with dve.Fori(0, 15) as i:
                for g in range(2):
                    step(g, i)
            step(30)
            for e in range(GROUP):
                low_up(31, e)
            accumulate(31)

            dve.wait_ge(acc_done, 8 * 32 + 8)
            norm(2, XT, XT, param("final_norm_w")).then_inc(norm_done, 1)
            dve.wait_ge(norm_done, 3)
            link(norm(3, XT, XN, g_eff))
            for k in range(KT):
                last = v.tensor_scalar(XN[:, k, :], XN[:, k, :], mod[:, k:k + 1], None, ALU.add)
            last.then_inc(norm_done, 1)

            dve.wait_ge(xc_ready, 64)
            for kv in range(2):
                for m in range(16):
                    last = v.tensor_scalar(CB[:, kv, m, :].rearrange("p (g n) -> p g n", g=2),
                                           XC[:, kv, :, 2 * m:2 * m + 16 * (NC_CMP - 1) + 1:16],
                                           param("pe_k" if kv == 0 else "pe_v")[:, m:m + 1], None, ALU.add)
                last.then_inc(cb_ready, 1)

            def scale(u):
                kind, h = UNITS[u]
                par = u % 3
                slope = 2.0 ** -(h + 1) / NSA_SCALE
                dve.wait_ge(at_scored, u + 1)
                if u >= 3:
                    dve.wait_ge(at_turned, CHUNKS[u - 2])
                for i in range(TT):
                    w, k0 = key_cols(kind, i)
                    if kind == "cmp":
                        bias = const("cmp")[:, i * NC_CMP:(i + 1) * NC_CMP]
                    elif kind == "swa":
                        bias = const("window")[:, 2 * P - w:2 * P]
                    else:
                        bias = const("alibi")[:, S - w:S]
                    last = v.scalar_tensor_tensor(SS[:, par, i, 0:w], bias, slope, ps[:, i, 0:w], ALU.mult, ALU.add)
                last.then_inc(at_read, 1)
                dve.wait_ge(at_read, u + 1)
                for i in range(TT):
                    w, _ = key_cols(kind, i)
                    last = v.tensor_reduce(mx[:, par, i:i + 1], SS[:, par, i, 0:w], AX.X, ALU.max)
                link(last)
                if kind == "swa":
                    link(v.tensor_scalar(mx[:, par, :], mx[:, par, :], NSA_SCALE, param("sinks")[:, h:h + 1],
                                         ALU.mult, ALU.max))
                    v.tensor_scalar(nm[:, par, :], mx[:, par, :], -1.0, None, ALU.mult).then_inc(at_scaled, 1)
                else:
                    v.tensor_scalar(nm[:, par, :], mx[:, par, :], -NSA_SCALE, None, ALU.mult).then_inc(at_scaled, 1)

            def factors(u):
                kind, h = UNITS[u]
                par = u % 3
                dve.wait_ge(at_exp, u + 1)
                if kind == "swa":
                    link(v.tensor_tensor(den[:, par, :], den[:, par, :], esink[:, par, :], ALU.add))
                    v.reciprocal(fac[:, par, :], den[:, par, :]).then_inc(at_fac, 1)
                    return
                link(v.reciprocal(fac[:, par, :], den[:, par, :]))
                b = ("cmp", "slc", "win").index(kind) * 8 + h
                if kind == "cmp":
                    link(v.tensor_tensor(fac[:, par, :], fac[:, par, :], const("seen"), ALU.mult))
                v.tensor_tensor(fac[:, par, :], fac[:, par, :], gn[:, :, b], ALU.mult).then_inc(at_fac, 1)

            def gate_out_tile(u):
                kind, h = UNITS[u]
                if h % 2 == 1 and kind in ("win", "swa"):
                    t = h // 2 + (4 if kind == "swa" else 0)
                    dve.wait_ge(at_out, u + 1)
                    v.tensor_tensor(QA[:, t, :], ps[:, 6 + t % 2, :], ZZ[:, t, :], ALU.mult).then_inc(o_ready, 1)

            dve.wait_ge(v_ready, 4)
            scale(0)
            scale(1)
            factors(0)
            for u in range(len(UNITS)):
                if u + 2 < len(UNITS):
                    scale(u + 2)
                if u + 1 < len(UNITS):
                    factors(u + 1)
                if u >= 2:
                    gate_out_tile(u - 2)
            gate_out_tile(len(UNITS) - 2)
            gate_out_tile(len(UNITS) - 1)
            for d in range(16):
                n = STREAM["o_nsa"] + d // 2
                dve.wait_ge(tile_done, n + 1)
                v.tensor_tensor(GT2[:, d, :], GT2[:, d, :], ps[:, (129 + d) % 4, :], ALU.mult)\
                    .then_inc(bank_free[(129 + d) % 4], 1)
            norm(4, ZZ, ZZ, param("g_post")).then_inc(norm_done, 1)
            dve.wait_ge(norm_done, 5)
            for k in range(KT):
                last = v.scalar_tensor_tensor(XT[:, k, :], ZZ[:, k, :], mod[:, 16 + k:17 + k], XT[:, k, :],
                                              ALU.mult, ALU.add)
            last.then_inc(out_ready, 1)

        @block.tensor
        def _(pe):
            def mm(o, lhsT, rhs, start=True, stop=True):
                return nc.tensor.matmul(o, lhsT, rhs, start=start, stop=stop, skip_group_check=True)

            def weights(n, later=0):
                pe.wait_ge(w_loaded[n % RING], later * 16 + 16 * (n // RING + 1))
                return ring[:, n % RING, :]

            def project(n, m, x, i=None):
                w = weights(n, 0 if i is None else i)
                if m >= 4:
                    pe.wait_ge(bank_free[m % 4], m // 4 if i is None else i * 2 + m // 4)
                for k in range(KT):
                    last = mm(ps[:, m % 4, :], w[:, k * P:(k + 1) * P], x[:, k, :], k == 0, k == KT - 1)
                last.then_inc(tile_done, 1)

            def project_half(n, m, x):
                w = weights(n)
                for o in range(2):
                    pe.wait_ge(bank_free[(m + o) % 4], (m + o) // 4)
                    for k in range(4):
                        last = mm(ps[:, (m + o) % 4, :], w[:, o * 512 + k * P:o * 512 + (k + 1) * P],
                                  x[:, k, :], k == 0, k == 3)
                last.then_inc(tile_done, 1)

            def sum_squares(j, sq):
                pe.wait_ge(norm_sq, j + 1)
                for c in range(TT):
                    for k in range(KT):
                        last = mm(ps[:, 7, c:c + 1], sq[:, k, c * P:(c + 1) * P], ones[:, 0:1], k == 0, k == KT - 1)
                last.then_inc(norm_ss, 1)
                pe.wait_ge(norm_diag, j + 1)
                mm(ps[:, 7, :], ones, RS[:, :]).then_inc(norm_bc, 1)

            pe.wait_ge(par_loaded, 32)
            sum_squares(0, XN)
            pe.wait_ge(norm_done, 1)
            n0 = STREAM["w_in"]
            for m in range(4):
                project(n0 + m, m, XN)
            with pe.Fori(0, 3) as i:
                for u in range(8):
                    project(n0 + 4 + u, 4 + u, XN, i)
            for m in range(28, 36):
                project(n0 + m, m, XN)
            with pe.Fori(0, 2) as i:
                for u in range(8):
                    project(n0 + 36 + u, 36 + u, XN, i)
            pe.wait_ge(pool_ready, 1)
            for g in range(4):
                mm(ps[:, 4 + g, :], param("pool_w")[:, g * P:(g + 1) * P], XA[:, g, 16:]).then_inc(pooly_done, 1)
            pe.wait_ge(yt_ready, 4)
            for u in range(4):
                project_half(STREAM["pool_up"] + u, 52 + 2 * u, XA[:, :, 16:])
            for c in range(TT):
                for k in range(KT):
                    last = mm(ps[:, 4, c * 16:(c + 1) * 16], XN[:, k, c * P:(c + 1) * P],
                              param("w_ba")[:, k * 16:(k + 1) * 16], k == 0, k == KT - 1)
            last.then_inc(ba_done, 1)
            pe.wait_ge(ba_v, 2)
            mm(ps[:, 5, 0:TT * 8], upper, g_log.rearrange("p c h -> p (c h)")).then_inc(gc_done, 1)
            pe.wait_ge(gc_ready, 1)

            for r in range(HEADS // 2):
                def each(fn):
                    for p in range(2):
                        fn(p, 2 * r + p, slots[p], 4 * p)

                def sumsq(p, h, s, b):
                    pe.wait_ge(dA[p].sem, dA[p].done(r, "sq"))
                    for x in range(8):
                        last = mm(ps[:, b, x:x + 1], s.sq[:, x // 4, (x % 4) * P:(x % 4 + 1) * P], ones[:, 0:1])
                    last.then_inc(dT[p].sem, 1)

                def spread(p, h, s, b):
                    pe.wait_ge(dV[p].sem, dV[p].done(r, "rd"))
                    mm(ps[:, b, :], ones, s.sq[:, 0, :])
                    mm(ps[:, b + 1, :], ones, s.sq[:, 1, :]).then_inc(dT[p].sem, 1)

                def four(bank, lhsT, rhs=None):
                    for c in range(TT):
                        o = ps[:, bank, c * P:(c + 1) * P]
                        last = mm(o, lhsT(c), rhs(c)) if rhs else nc.tensor.transpose(o, lhsT(c), ident)
                    return last

                def turn(p, h, s, b):
                    pe.wait_ge(dV[p].sem, dV[p].done(r, "norm"))
                    four(b, lambda c: QKV[:, 8 + h, c * P:(c + 1) * P])
                    four(b + 1, lambda c: QKV[:, 16 + h, c * P:(c + 1) * P])\
                        .then_inc(dT[p].sem, 1)
                    four(b + 2, lambda c: QKV[:, 8 + h, c * P:(c + 1) * P], lambda c: QKV[:, 8 + h, c * P:(c + 1) * P])
                    four(b + 3, lambda c: QKV[:, 8 + h, c * P:(c + 1) * P], lambda c: QKV[:, h, c * P:(c + 1) * P])\
                        .then_inc(dT[p].sem, 1)

                def decay(p, h, s, b):
                    pe.wait_ge(dV[p].sem, dV[p].done(r, "gu"))
                    pe.wait_ge(dA[p].sem, dA[p].done(r, "ktok"))
                    mm(ps[:, b, :], ones, s.gu.rearrange("p c t -> p (c t)")).then_inc(dT[p].sem, 1)

                def lt(p, h, s, b):
                    pe.wait_ge(dV[p].sem, dV[p].done(r, "l"))
                    four(b + 1, lambda c: s.ed[:, c, :]).then_inc(dT[p].sem, 1)

                def t1(p, h, s, b):
                    pe.wait_ge(dV[p].sem, dV[p].done(r, "tt"))
                    pe.wait_ge(dA[p].sem, dA[p].done(r, "lts"))
                    four(b, lambda c: s.tt[:, c, :]).then_inc(dT[p].sem, 1)

                for fn in (sumsq, spread, turn, decay, lt, t1):
                    each(fn)
                for l in range(1, LEVELS):
                    def lx(p, h, s, b):
                        pe.wait_ge(dG[p].sem, dG[p].done(r, f"lk{l}"))
                        pe.wait_ge(dV[p].sem, dV[p].done(r, "t" if l == 1 else f"u{l - 1}"))
                        four(b, lambda c: s.lk[:, c, :], lambda c: s.t[:, c, :]).then_inc(dT[p].sem, 1)

                    def tx(p, h, s, b):
                        pe.wait_ge(dA[p].sem, dA[p].done(r, f"x{l}"))
                        for c in range(TT):
                            if l < LEVELS - 1:
                                mm(ps[:, b + 2, c * 64:(c + 1) * 64], s.tt[:, c, :], pair_side(s.x[:, c, :], l, 0))
                        for c in range(TT):
                            last = mm(ps[:, b + 3, c * 64:(c + 1) * 64], s.x[:, c, :], pair_side(s.tt[:, c, :], l, 1))
                        last.then_inc(dT[p].sem, 1)

                    each(lx)
                    each(tx)
                for c in range(TT):
                    def pq(p, h, s, b):
                        pe.wait_ge(dV[p].sem, dV[p].done(r, f"o{c - 1}"))
                        mm(ps[:, b, 0:P], QKV[:, 8 + h, c * P:(c + 1) * P], s.state)
                        mm(ps[:, b, P:2 * P], QKV[:, h, c * P:(c + 1) * P], s.state).then_inc(dT[p].sem, 1)

                    def vnew(p, h, s, b):
                        pe.wait_ge(dV[p].sem, dV[p].done(r, f"r{c}" if c else f"u{LEVELS - 1}"))
                        mm(ps[:, b + 1, 0:P], s.tt[:, c, :], s.r if c else s.vb[:, 0, :]).then_inc(dT[p].sem, 1)

                    def outs(p, h, s, b):
                        pe.wait_ge(dA[p].sem, dA[p].done(r, f"vn{c}"))
                        pe.wait_ge(dG[p].sem, dG[p].done(r, "kdec"))
                        last = mm(ps[:, b + 1, P:2 * P], s.et[:, c, :], s.vn)
                        if c < TT - 1:
                            last = mm(ps[:, b + 1, 2 * P:3 * P], s.kt[:, c, :], s.vn)
                        last.then_inc(dT[p].sem, 1)

                    for fn in ((pq,) if c else ()) + (vnew, outs):
                        each(fn)

                def turn_o(p, h, s, b):
                    pe.wait_ge(dV[p].sem, dV[p].done(r, "dg"))
                    four(b + 2, lambda c: s.t[:, c, :], lambda c: s.lk[:, c, :]).then_inc(dT[p].sem, 1)

                each(turn_o)

            for p in range(2):
                pe.wait_ge(dV[p].sem, dV[p].done(3, "fin"))
            for u in range(8):
                project(STREAM["dn_up"] + u, 60 + u, Z)
            pe.wait_ge(merged, 1)
            for u in range(8):
                project(STREAM["mix_out"] + u, 68 + u, XN)
            sum_squares(1, XN)
            pe.wait_ge(norm_done, 2)
            pe.wait_ge(keys_loaded, 16)
            for hz in range(17):
                if hz < 16:
                    project(STREAM["query"] + hz, 76 + hz, XN)
                if hz:
                    q = hz - 1
                    pe.wait_ge(bank_free[(76 + q) % 4], (76 + q) // 4 + 1)
                    if q >= 4:
                        pe.wait_ge(sc_ready, q - 3)
                    for c in range(TT):
                        last = mm(ps[:, 4 + q % 4, c * P:(c + 1) * P], QP[:, q, c * P:(c + 1) * P], keys[:, q, :])
                    last.then_inc(sc_done, 1)
            pe.wait_ge(bank_free[3], 23)
            for u in range(24):
                w = weights(STREAM["ada"] + u)
                for k in range(KT):
                    last = mm(ps[:, 3, u:u + 1], w[:, k * P:(k + 1) * P], param("c")[:, k:k + 1], k == 0, k == KT - 1)
                last.then_inc(tile_done, 1)
            for z, bank in ((0, 4), (1, 5)):
                for c in range(TT):
                    pe.wait_ge(sel_ready, 8)
                    last = nc.tensor.transpose(ps[:, bank, c * P:(c + 1) * P], SEL[:, z, c, :], ident)
                last.then_inc(turned, 1)
            pe.wait_ge(gate_ready, 1)
            for c in range(TT):
                last = nc.tensor.transpose(ps[:, 6, c * P:(c + 1) * P], TOP[:, c, :, :].rearrange("p h k -> p (h k)"), ident)
            last.then_inc(turned, 1)
            pe.wait_ge(turned_read, 3)
            with pe.Fori(0, S // 16) as j:
                for u in range(16):
                    if u % 4 == 0:
                        pe.wait_ge(gate_out, j * 4 + (u // 4 + 1))
                        pe.wait_ge(gated_a, j * 4 + (u // 4 + 1))
                        pe.wait_ge(onehot_b, j * 4 + (u // 4 + 1))
                    mm(ps[:, 4 + u // 4, (u % 4) * P:(u % 4 + 1) * P], ONE_B[:, u, :], ONE_A[:, u, :])\
                        .then_inc(token_mm, 1)
            pe.wait_ge(x_lo, 1)

            def three(o, wh, wl, xh, xl, first, last):
                mm(o, wh, xh, first, False)
                mm(o, wh, xl, False, False)
                return mm(o, wl, xh, False, last)

            def hidden(g, i=None):
                for e in range(GROUP):
                    pe.wait_ge(split_lo, nth((8 * (g - 1) + SPLIT_D[e] + 1 if g else e + 1, 16), i))
                    if g or e >= 2:
                        pe.wait_ge(gelu_done, nth((4 * g + e - 1, 8), i))
                    for k in range(KT):
                        ks = slice(k * P, (k + 1) * P)
                        last = three(ps[:, e % 2, :], DH[:, e % 2, ks], DL[:, e % 2, ks], XH[:, k, :], XL[:, k, :],
                                     k == 0, k == KT - 1)
                    last.then_inc(tile_done, 1)

            def expert_out(g, i=None):
                pe.wait_ge(split_lo, nth((8 * g + SPLIT_U[3] + 1 if g < 31 else 256, 16), i))
                pe.wait_ge(w_done, nth((4 * g + 4, 8), i))
                for d in range(KT):
                    pe.wait_ge(acc_done, nth((8 * g + d + 5, 16), i))
                    dd = slice(d * P, (d + 1) * P)
                    for e in range(GROUP):
                        last = three(ps[:, 2 + d % 4, :], UH[:, e, dd], UL[:, e, dd], WH[:, g % 2, e, :],
                                     WL[:, g % 2, e, :], e == 0, e == GROUP - 1)
                        if d == KT - 1:
                            last.then_inc(tile_done, 1)
                    if d < KT - 1:
                        last.then_inc(y_done, 1)

            hidden(0)
            with pe.Fori(0, 15) as i:
                for g in range(2):
                    hidden(g + 1, i)
                    expert_out(g, i)
            hidden(31)
            expert_out(30)
            expert_out(31)
            for j in (2, 3):
                sum_squares(j, XN)
            pe.wait_ge(norm_done, 4)
            n0 = STREAM["w_in_2"]
            for u in range(16):
                project(n0 + u, 92 + u, XN)
            with pe.Fori(0, 2) as i:
                for u in range(8):
                    project(n0 + 16 + u, 108 + u, XN, i)
            for u in range(5):
                project(n0 + 32 + u, 124 + u, XN)
            for j in range(4):
                w = weights(STREAM["v_tok"] + j)
                for c in range(TT):
                    for k in range(2):
                        last = mm(ps[:, 4 + c, 0:408], XN[:, 2 * j + k, c * P:(c + 1) * P],
                                  w[:, k * 512:k * 512 + 408], j == 0 and k == 0, j == 3 and k == 1)
                last.then_inc(tile_done, 1)
            for kv in range(2):
                pe.wait_ge(cb_ready, kv + 1)
                pe.wait_ge(v_ready, 4)
                for m in range(16):
                    w = weights(STREAM["cmp_k1" if kv == 0 else "cmp_v1"] + m // 4)
                    for a in range(2):
                        last = mm(ps[:, 4 + 2 * kv + a, 0:62], w[:, (m % 4) * 256 + a * P:(m % 4) * 256 + (a + 1) * P],
                                  CB[:, kv, m, :], m == 0, m == 15)
                    if m % 4 == 3:
                        last.then_inc(tile_done, 1)
            pe.wait_ge(hid_ready, 2)
            for b in range(4):
                pe.wait_ge(bank_free[b], (129 - b + 3) // 4)
            for half in range(2):
                for a in range(2):
                    mm(ps[half * 64:(half + 1) * 64, 0, 0:62], param("w_cmp_k2")[:, a * 64:(a + 1) * 64],
                       HID[:, 0, a, :], a == 0, a == 1)
            for g in range(2):
                for a in range(2):
                    last = mm(ps[0:NC_CMP, 1, g * 64:(g + 1) * 64], HID[:, 1, a, g * NC_CMP:(g + 1) * NC_CMP],
                              param("w_cmp_v2")[:, a * 64:(a + 1) * 64], a == 0, a == 1)
            last.then_inc(kv_done, 1)
            pe.wait_ge(kc_ready, 1)
            pe.wait_ge(dup_done, 64)

            def scores(u):
                kind, h = UNITS[u]
                if u:
                    pe.wait_ge(at_read, u)
                p0, t = 64 * (h % 2), h // 2 + (4 if kind == "swa" else 0)
                for i in range(TT):
                    q = QA[p0:p0 + 64, t, i * P:(i + 1) * P]
                    w, k0 = key_cols(kind, i)
                    if kind == "cmp":
                        k = KC[p0:p0 + 64, (h // 4) * NC_CMP:(h // 4 + 1) * NC_CMP]
                    else:
                        k = KD[p0:p0 + 64, ("slc", "win", "swa").index(kind), h // 4, k0:k0 + w]
                    last = mm(ps[:, i, 0:w], q, k)
                last.then_inc(at_scored, 1)

            def turn_probs(u):
                kind, h = UNITS[u]
                pe.wait_ge(at_weighted, u + 1)
                for x, (kt, tiles) in enumerate(turns(kind)):
                    chunk = CHUNKS[u] + x
                    if chunk >= 2:
                        pe.wait_ge(at_copied, chunk - 1)
                    for i in tiles:
                        w, k0 = key_cols(kind, i)
                        a = kt * P - k0
                        m = NC_CMP if kind == "cmp" else P
                        last = nc.tensor.transpose(ps[0:m, 4 + chunk % 2, i * P:(i + 1) * P],
                                                   SS[:, u % 3, i, a:a + m], ident)
                    last.then_inc(at_turned, 1)

            def values(u):
                kind, h = UNITS[u]
                par, p0, t = u % 2, 64 * (h % 2), h // 2 + (4 if kind == "swa" else 0)
                pe.wait_ge(at_copied, CHUNKS[u + 1])
                if h % 2 == 0 and kind in ("cmp", "swa") and t >= 2:
                    pe.wait_ge(o_ready, t - 1)
                o = ps[p0:p0 + 64, 6 + t % 2, :]
                if kind == "cmp":
                    last = mm(o, VC[0:NC_CMP, h // 4, :], PT[0:NC_CMP, par, 0, :], True, False)
                elif kind == "swa":
                    for i in range(TT):
                        for kt in range(max(0, i - 1), i + 1):
                            v = VT[:, kt, 256 + (h // 4) * 64:256 + (h // 4 + 1) * 64]
                            last = mm(o[:, i * P:(i + 1) * P], v, PT[:, par, kt, i * P:(i + 1) * P],
                                      kt == max(0, i - 1), kt == i)
                else:
                    b = 0 if kind == "slc" else 128
                    for kt in range(TT):
                        v = VT[:, kt, b + (h // 4) * 64:b + (h // 4 + 1) * 64]
                        last = mm(o[:, kt * P:], v, PT[:, par, kt, kt * P:], False, kind == "win" and kt == TT - 1)
                last.then_inc(at_out, 1)

            scores(0)
            scores(1)
            for u in range(len(UNITS)):
                if u + 2 < len(UNITS):
                    scores(u + 2)
                turn_probs(u)
                if u:
                    values(u - 1)
            values(len(UNITS) - 1)
            pe.wait_ge(o_ready, 8)
            for u in range(4):
                project_half(STREAM["o_nsa"] + u, 129 + 2 * u, QA[:, 0:4, :])
            for u in range(4):
                project_half(STREAM["o_swa"] + u, 137 + 2 * u, QA[:, 4:8, :])
            pe.wait_ge(merged, 2)
            for u in range(8):
                project(STREAM["w_out"] + u, 145 + u, XN)
            sum_squares(4, XN)


def shape_constants():
    p, j = np.arange(P)[:, None], np.arange(P)[None, :]
    parts = {
        "ident": p == j,
        "ones": np.ones((P, P)),
        "upper": p <= j,
        "iota": np.broadcast_to(j, (P, P)),
        "strict": j < p,
        "block": np.concatenate([(j >> l & 1 == 1) & (p >> l & 1 == 0) & (j >> l + 1 == p >> l + 1)
                                 for l in range(LEVELS)], axis=1),
    }
    x = np.arange(S)[None, :]
    dist = p + S - P - x
    parts["alibi"] = np.where(dist >= 0, -dist, -1e30)
    dist = P + p - np.arange(2 * P)[None, :]
    parts["window"] = np.where((dist >= 0) & (dist < P), -dist, -1e30)
    t = np.arange(TT)[None, :, None] * P + p[:, :, None]
    dist = t - (np.arange(NC_CMP)[None, None, :] * 16 + 31)
    parts["cmp"] = np.where(dist >= 0, -dist, -1e30).reshape(P, -1)
    parts["seen"] = (t[:, :, 0] >= 31)
    n = np.arange(16)[None, :] + 1
    first = 1.0 / np.minimum(n, 2.0 ** (np.arange(4)[:, None] + 1))
    parts["eps"] = np.broadcast_to([[EPS, D * EPS]], (P, 2))
    parts["first"] = np.broadcast_to(first.reshape(1, 64), (P, 64))
    return np.concatenate([np.asarray(parts[k], np.float32) for k in CONST], axis=1)


def by_feature(v):
    return v.reshape(-1, P).T


def tiles(w):
    return w.reshape(KT, P, -1, P).transpose(2, 1, 0, 3).reshape(-1, P, 1024)


def half_tiles(w):
    return w.reshape(4, P, 8, P).transpose(2, 1, 0, 3).reshape(4, 2, P, 512).transpose(0, 2, 1, 3).reshape(4, P, 1024)


def lay_out(inputs):
    a = {k: np.asarray(v) for k, v in inputs.items()}
    one = {k: v[0] for k, v in a.items()}
    w, w2 = one["w_in"], one["w_in_2"]
    down = one["peer_down"].reshape(P, P, KT, P).transpose(0, 3, 2, 1).reshape(32, GROUP, P, 1024)
    up = one["peer_up"].reshape(32, GROUP, P, 1024)
    experts = [down[0]]
    for g in range(31):
        experts += [down[g + 1], up[g]]
    experts.append(up[31])
    v_tok = np.concatenate([w2[:, 896:1024], w2[:, 1152:1280], w2[:, 2456:2584], w2[:, 1280:1304],
                            np.zeros((1024, 104), np.float32)], axis=1)
    cmp_tiles = lambda m: m.reshape(4, 4, P, 256).transpose(0, 2, 1, 3).reshape(4, P, 1024)
    stream = np.concatenate([
        tiles(w[:, 0:4608]), tiles(w[:, 4624:6672]), half_tiles(one["w_pool_up"]), tiles(one["w_dn_up"]),
        tiles(one["w_mix_out"]), tiles(one["peer_w_query"]), tiles(one["w_ada_2"]), *experts,
        tiles(w2[:, 0:512]), tiles(w2[:, 1816:2328]), tiles(w2[:, 1304:1816]), tiles(w2[:, 2584:3096]),
        tiles(w2[:, 3096:5144]), tiles(w2[:, 512:768]), tiles(w2[:, 768:896]), tiles(w2[:, 1024:1152]),
        tiles(w2[:, 2328:2456]),
        v_tok.reshape(4, 2, P, 512).transpose(0, 2, 1, 3).reshape(4, P, 1024),
        cmp_tiles(one["w_cmp_k1_2"]), cmp_tiles(one["w_cmp_v1_2"]),
        half_tiles(one["w_o_nsa_2"]), half_tiles(one["w_o_swa_2"]), tiles(one["w_out_2"])])
    rows = lambda v: np.broadcast_to(v.reshape(1, -1), (P, v.size))
    params = {
        "mix_norm_w": by_feature(one["mix_norm_w"]),
        "conv_w": one["conv_w"].reshape(4, 24, P).transpose(2, 1, 0).reshape(P, 96),
        "pool_scale": by_feature(one["pool_scale"]),
        "a_log": rows(one["a_log"]), "dt_bias": rows(one["dt_bias"]),
        "dn_norm_w": one["dn_norm_w"].reshape(P, 1),
        "ffn_norm_w": by_feature(one["ffn_norm_w"]), "final_norm_w": by_feature(a["final_norm_w"]),
        "c": by_feature(one["c_2"]), "b_ada": by_feature(one["b_ada_2"]),
        "g_pre": by_feature(one["g_pre_2"]), "g_post": by_feature(one["g_post_2"]),
        "sinks": rows(one["sinks_2"]),
        "pe_k": one["pe_cmp_k_2"].reshape(16, P).T, "pe_v": one["pe_cmp_v_2"].reshape(16, P).T,
        "pool_w": one["pool_w"].transpose(1, 0, 2).reshape(P, 512),
        "w_ba": w[:, 4608:4624].reshape(KT, P, 16).transpose(1, 0, 2).reshape(P, 128),
        "w_cmp_k2": one["w_cmp_k2_2"].reshape(2, P, 64).transpose(1, 0, 2).reshape(P, 128),
        "w_cmp_v2": one["w_cmp_v2_2"].reshape(2, P, 64).transpose(1, 0, 2).reshape(P, 128),
    }
    both = np.stack([one["peer_keys_1"], one["peer_keys_2"]], axis=1)
    return {
        "x_in": one["x"].T.reshape(KT, P, S).transpose(1, 0, 2).reshape(P, KT * S),
        "stream": stream,
        "params": np.concatenate([params[k] for k in PARAM], axis=1),
        "consts": shape_constants(),
        "keys": both.transpose(3, 0, 1, 2).reshape(P, 2048),
    }


def kernel(**inputs):
    import concourse.bacc as bacc
    from concourse.bass_utils import run_bass_kernel_spmd

    nc = bacc.Bacc("TRN2", target_bir_lowering=False, num_devices=1)
    arrays = {k: np.ascontiguousarray(v) for k, v in lay_out(inputs).items()}
    aps = [nc.dram_tensor("dram_" + k, v.shape, mybir.dt.float32, kind="ExternalInput").ap() for k, v in arrays.items()]
    out = nc.dram_tensor("dram_out", [P, KT * S], mybir.dt.float32, kind="ExternalOutput").ap()
    program(nc, *aps, out)
    got = run_bass_kernel_spmd(nc, [{"dram_" + k: v for k, v in arrays.items()}], core_ids=[0]).results[0]["dram_out"]
    return got.reshape(P, KT, S).transpose(2, 1, 0).reshape(1, S, D)
```

```python
import numpy as np
import concourse.bass as bass
from concourse import mybir
from contextlib import ExitStack

D = 1024
S = 512
P = 128
KT = D // P
TT = S // P
HEADS = 8
HD = 128
TOPK = 16
RING = 8
EPS = 1e-6
EXPERTS_A = 128
GROUP = 4
BLOCK_T = 64
NC_CMP = 31
NSA_SCALE = 0.125
LEVELS = 7

CONST = {}
_at = 0
for _n, _w in (("ident", P), ("ones", P), ("upper", P), ("iota", P), ("strict", P), ("block", LEVELS * P),
               ("alibi", S), ("window", 2 * P), ("cmp", TT * NC_CMP), ("seen", TT), ("first", 64), ("eps", 2)):
    CONST[_n] = (_at, _w)
    _at += _w
N_CONST = _at

PARAM = {}
_at = 0
for _n, _w in (("mix_norm_w", KT), ("conv_w", 96), ("pool_scale", 4), ("a_log", 8), ("dt_bias", 8),
               ("dn_norm_w", 1), ("ffn_norm_w", KT), ("final_norm_w", KT), ("c", KT), ("b_ada", 24),
               ("g_pre", KT), ("g_post", KT), ("sinks", 8), ("pe_k", 16), ("pe_v", 16), ("pool_w", 512),
               ("w_ba", KT * 16), ("w_cmp_k2", 128), ("w_cmp_v2", 128)):
    PARAM[_n] = (_at, _w)
    _at += _w
N_PARAM = _at

STREAM = {}
_at = 0
for _n, _w in (("w_in", 52), ("pool_up", 4), ("dn_up", 8), ("mix_out", 8), ("query", 16),
               ("ada", 24), ("experts", 256), ("w_in_2", 37), ("v_tok", 4), ("cmp_k1", 4), ("cmp_v1", 4),
               ("o_nsa", 4), ("o_swa", 4), ("w_out", 8)):
    STREAM[_n] = _at
    _at += _w
N_STREAM = _at


class Steps:

    def __init__(self, sem, names):
        self.sem, self.names = sem, names

    def done(self, rnd, name):
        return rnd * len(self.names) + self.names.index(name) + 1


def program(nc, x_in, stream, params_in, consts_in, keys_in, out):
    f32, u32 = mybir.dt.float32, mybir.dt.uint32
    ALU, ACT, AX = mybir.AluOpType, mybir.ActivationFunctionType, mybir.AxisListType
    ds = bass.ds
    gate_dram = nc.dram_tensor("gate_matrix", [S // BLOCK_T, P, EXPERTS_A, BLOCK_T], f32).ap()

    with ExitStack() as ctx:
        def sb(name, cols, dt=f32):
            return ctx.enter_context(nc.sbuf_tensor(name, [P, cols], dt))

        def sem(name):
            return ctx.enter_context(nc.semaphore(name))

        consts = sb("consts", N_CONST)
        params = sb("params", N_PARAM)
        acts_at = -(-nc.sbuf_base // 32) * 32
        acts = sb("acts", 2 * KT * S)
        ring_at = -(-nc.sbuf_base // 32) * 32
        ring = sb("ring", RING * 1024)[:, :].rearrange("p (s n) -> p s n", s=RING)
        RS = sb("rstd", S)
        small = sb("small", 1024)
        work_at = -(-nc.sbuf_base // 32) * 32
        work = sb("work", 31600)
        ps = ctx.enter_context(nc.psum_tensor("ps", [P, 8, 512], f32))

        def const(name):
            a, w = CONST[name]
            return consts[:, a:a + w]

        def param(name):
            a, w = PARAM[name]
            return params[:, a:a + w]

        ident, ones, upper, iota = (const(n) for n in ("ident", "ones", "upper", "iota"))

        def view(base, at, *dims):
            n = int(np.prod(dims))
            assert at + n <= base.shape[1], (at, dims)
            v = base[:, at:at + n]
            if len(dims) == 1:
                return v
            names = "abcd"[:len(dims)]
            return v.rearrange(f"p ({' '.join(names)}) -> p {' '.join(names)}", **dict(zip(names, dims)))

        def over(ap, axis, n):
            v = ap.unsqueeze(axis)
            shape = list(v.shape)
            shape[axis] = n
            return v.broadcast_to(shape)

        XT = view(acts, 0, KT, S)
        XN = view(acts, KT * S, KT, S)

        class Region:

            def __init__(self, base, at=0):
                self.base, self.at = base, at

            def take(self, *dims):
                v = view(self.base, self.at, *dims)
                self.at += int(np.prod(dims))
                return v

        sm = Region(small)
        w32 = sm.take(KT)
        ea, beta, a_in, sp_a, sp_b = sm.take(8), sm.take(TT, 8), sm.take(TT, 8), sm.take(TT, 8), sm.take(TT, 8)
        g_log, gc, egc, nbeg = sm.take(TT, 8), sm.take(TT, 8), sm.take(TT, 8), sm.take(TT, 8)
        mod, g_eff = sm.take(24), sm.take(KT)
        mx, nm, den, fac = sm.take(3, TT), sm.take(3, TT), sm.take(3, TT), sm.take(3, TT)
        esink, gn = sm.take(3, TT), sm.take(TT, 24)
        KC, VC = sm.take(64), sm.take(2, 64)
        zero_exp, zero_v, zero_w, rtok, RS16 = sm.take(8), sm.take(8), sm.take(8), sm.take(TT), sm.take(16)

        r1 = Region(work)
        QKV, Z, GT = r1.take(24, S), r1.take(KT, S), r1.take(16, S)
        SIDE = r1.at
        XA = r1.take(4, 16 + S)
        pool_tmp = Region(work, SIDE - 2 * (16 + S)).take(2, 16 + S)
        RAW, CONV = r1.take(2, 3 + S), r1.take(2, S)

        class Slot:

            def __init__(self, region):
                t = region.take
                self.sq, self.ed, self.et, self.df = t(2, S), t(TT, HD), t(TT, HD), t(TT, HD)
                self.lk, self.t, self.tt, self.vb = t(TT, HD), t(TT, HD), t(TT, HD), t(TT, HD)
                self.kt, self.state, self.r, self.vn = t(TT, HD), t(HD), t(HD), t(HD)
                self.rqk = t(8)
                self.egl, self.edl, self.oss, self.ors = t(TT), t(TT), t(TT), t(TT)
                self.gu = self.sq[:, 0, :].rearrange("p (c t) -> p c t", c=TT)
                self.x = self.sq[:, 1, :].rearrange("p (c t) -> p c t", c=TT)

        slots = [Slot(Region(acts)), Slot(Region(work, SIDE))]
        IN_HI = -(-r1.at // 8) * 8

        r2 = Region(work)
        QP, keys = r2.take(16, S), r2.take(16, P)
        SC, SC2, CAND, CAND2 = r2.take(2, TT, P), r2.take(TT, P), r2.take(TT, 128), r2.take(TT, 128)
        BITS = r2.take(4, 512)
        CAND_FLAT = CAND.rearrange("p c n -> p (c n)")
        V1, I1, I1F = r2.take(TT, 16, TOPK), r2.take(TT, 16, TOPK), r2.take(TT, 16, TOPK)
        TOP, POS, PF = r2.take(TT, 8, TOPK), r2.take(TT, 8, TOPK), r2.take(2, TT, 8, TOPK)
        SEL, EQ = r2.take(2, TT, 128), r2.take(2, 2048)
        GSUM = r2.take(TT, 8)
        TR = Region(work, 31600 - 1536)
        I1T, I2T, GTT = TR.take(S), TR.take(S), TR.take(S)
        r3 = Region(work)
        ONE_A, ONE_B = r3.take(16, P), r3.take(16, P)
        ADA_PART = (0, 32)
        ADA_ROWS = view(work, 0, 16 * P)
        GB = r3.take(2, EXPERTS_A, BLOCK_T)
        def split_at(name, base, at, *dims):
            t = nc.alloc_sbuf_tensor_at(name, [P, int(np.prod(dims))], mybir.dt.float32r, offset=base + 4 * at)
            return view(t, 0, *dims)

        UH, UL = split_at("up_hi", work_at, 0, GROUP, 1024), split_at("up_lo", work_at, 4096, GROUP, 1024)
        WH, WL = (split_at("act_hi", work_at, 8192, 2, GROUP, S), split_at("act_lo", work_at, 12288, 2, GROUP, S))
        GG = view(work, 16384, 2, 8, GROUP, BLOCK_T)
        XH, XL = split_at("x_hi", work_at, 20480, KT, S), split_at("x_lo", work_at, 24576, KT, S)
        GE = view(work, 28672, 2, S)
        DH, DL = split_at("down_hi", acts_at, KT * S, 2, 1024), split_at("down_lo", acts_at, KT * S + 2048, 2, 1024)
        assert SIDE == 48 * S
        assert max(r2.at, r3.at) <= 31600 - 1536
        X_LO, RING_LO = split_at("xn_lo", acts_at, KT * S, KT, S), split_at("ring_lo", ring_at, 0, RING, 1024)
        X_HI1, W_HI1 = split_at("xn_hi_1", acts_at, 0, KT, S), split_at("w_hi_1", work_at, IN_HI, 2, 1024)
        BA_HI, BA_LO = split_at("ba_hi", work_at, IN_HI + 2048, KT * 16), split_at("ba_lo", work_at, IN_HI + 2176, KT * 16)

        r5 = Region(work)
        QA, ZZ, GT2, KD = r5.take(8, S), r5.take(8, S), r5.take(16, S), r5.take(3, 2, S)
        at2 = r5.at
        SQ1 = view(work, 0, KT, S)
        Z_HI, Z_LO = split_at("delta_hi", work_at, 0, KT, S), split_at("delta_lo", work_at, 24 * S, KT, S)
        M_HI1, W_HID = split_at("merged_hi_1", work_at, 8 * S, KT, S), split_at("w_hi_d", work_at, 16 * S, 2, 1024)
        O_HI, O_LO = split_at("attn_hi", work_at, 8 * S, 8, S), split_at("attn_lo", work_at, 0, 8, S)
        M_HI2 = split_at("merged_hi_2", work_at, at2, KT, S)
        W_HI3 = split_at("w_hi_3", work_at, at2 + 3 * TT * S, 2, 1024)
        KK, XC = r5.take(5, S), r5.take(2, 2, S)
        X_HI2, W_HI2 = split_at("xn_hi_2", work_at, r5.at, KT, S), split_at("w_hi_2", work_at, r5.at + KT * S, 2, 1024)
        VT = Region(work, r5.at + KT * S).take(TT, 384)
        CB, HID = r5.take(2, 16, 62), r5.take(2, 2, 62)
        r6 = Region(work, at2)
        SS, PT = r6.take(3, TT, S), view(acts, KT * S, 2, TT, S)

        w_loaded = [sem(f"w_loaded_{s}") for s in range(RING)]
        tile_done = sem("tile_done")
        bank_free = [sem(f"bank_free_{b}") for b in range(4)]
        x_loaded, par_loaded, keys_loaded = sem("x_loaded"), sem("par_loaded"), sem("keys_loaded")
        v_chain, a_chain, g_chain = sem("v_chain"), sem("a_chain"), sem("g_chain")
        rs_out = sem("rs_out")
        norm_diag, norm_bc = sem("norm_diag"), sem("norm_bc")
        norm_sq, norm_ss, norm_done = sem("norm_sq"), sem("norm_ss"), sem("norm_done")
        x_part, final_part = [sem(f"x_part_{q}") for q in range(4)], sem("final_part")
        pads, conv_part, conv_done, silu_done = sem("pads"), sem("conv_part"), sem("conv_done"), sem("silu_done")
        pool_ready, pooly_done, yt_ready = sem("pool_ready"), sem("pooly_done"), sem("yt_ready")
        ba_done, ba_v, ba_a, gc_done, gc_ready = sem("ba_done"), sem("ba_v"), sem("ba_a"), sem("gc_done"), sem("gc_ready")
        T_STEPS = ["sumsq", "spread", "turn", "gram", "decay", "lt", "t1"]
        A_STEPS = ["sq", "root", "ktok", "e", "eg", "lts"]
        V_STEPS = ["rd", "norm", "vb", "gu", "bkk", "diff", "l", "tt", "at", "t"]
        for l in range(1, LEVELS):
            T_STEPS += [f"x{l}", f"tx{l}"]
            A_STEPS += [f"x{l}"]
            V_STEPS += [f"u{l}"]
        for c in range(TT):
            T_STEPS += [f"pq{c}"] * (c > 0) + [f"v{c}", f"os{c}"]
            A_STEPS += [f"vn{c}"]
            V_STEPS += [f"r{c}"] * (c > 0) + [f"s{c}"] * (c < TT - 1) + [f"o{c}"]
        dT = [Steps(sem(f"delta_pe_{p}"), T_STEPS + ["turn_o"]) for p in range(2)]
        dA = [Steps(sem(f"delta_act_{p}"), A_STEPS + ["oroot"]) for p in range(2)]
        dV = [Steps(sem(f"delta_dve_{p}"), V_STEPS + ["dg", "fin"]) for p in range(2)]
        dG = [Steps(sem(f"delta_pool_{p}"), ["mask", "etm", "lk1", "kdec"] + [f"lk{l}" for l in range(2, LEVELS)])
              for p in range(2)]
        merged = sem("merged")
        sc_done, sc_ready, topk_done, cand_ready = (sem(n) for n in (
            "sc_done", "sc_ready", "topk_done", "cand_ready"))
        cand_used, eq_ready, eq_mul, sel_ready = sem("cand_used"), sem("eq_ready"), sem("eq_mul"), sem("sel_ready")
        i1f_ready = sem("i1f_ready")
        gd_ready, ge_ready, gate_ready = sem("gd_ready"), sem("ge_ready"), sem("gate_ready")
        turned, turned_read = sem("turned"), sem("turned_read")
        onehot_a, onehot_b, gated_a = sem("onehot_a"), sem("onehot_b"), sem("gated_a")
        ada_rows, ada_turned = sem("ada_rows"), sem("ada_turned")
        token_mm, gate_out = sem("token_mm"), sem("gate_out")
        gate_written = [sem(f"gate_written_{p}") for p in range(2)]
        gate_loaded = [sem(f"gate_loaded_{p}") for p in range(2)]
        gelu_done, w_done, y_done, acc_done = sem("gelu_done"), sem("w_done"), sem("y_done"), sem("acc_done")
        x_hi, x_lo, split_hi, split_lo, prod_done = (sem(n) for n in ("x_hi", "x_lo", "split_hi", "split_lo", "prod_done"))
        w_hi = sem("w_hi")
        norm_part, xn_hi, xn_lo = sem("norm_part"), sem("xn_hi"), sem("xn_lo")
        tile_hi, tile_lo, ba_hi, ba_lo = sem("tile_hi"), sem("tile_lo"), sem("ba_hi"), sem("ba_lo")
        dup_done, xc_ready, cb_ready = sem("dup_done"), sem("xc_ready"), sem("cb_ready")
        v_ready, hid_ready, kv_done, kc_ready = sem("v_ready"), sem("hid_ready"), sem("kv_done"), sem("kc_ready")
        at_scored, at_scaled, at_exp, at_fac = sem("at_scored"), sem("at_scaled"), sem("at_exp"), sem("at_fac")
        at_read, at_weighted = sem("at_read"), sem("at_weighted")
        at_turned, at_copied, at_out, o_ready = sem("at_turned"), sem("at_copied"), sem("at_out"), sem("o_ready")
        out_ready, out_written = sem("out_ready"), sem("out_written")

        UNITS = [(kind, h) for h in range(8) for kind in ("cmp", "slc", "win")] + [("swa", h) for h in range(8)]

        def turns(kind):
            if kind == "cmp":
                return [(0, range(TT))]
            if kind == "swa":
                return [(k, range(k, min(k + 2, TT))) for k in range(TT)]
            return [(k, range(k, TT)) for k in range(TT)]

        OUT_UNITS = [u for u, (kind, h) in enumerate(UNITS) if h % 2 == 1 and kind in ("win", "swa")]
        CHUNKS = [0]
        for kind, _ in UNITS:
            CHUNKS.append(CHUNKS[-1] + len(turns(kind)))

        def key_cols(kind, i):
            if kind == "cmp":
                return NC_CMP, 0
            if kind == "swa":
                return (2 * P, (i - 1) * P) if i else (P, 0)
            return (i + 1) * P, 0

        SPLIT_U, SPLIT_D = (6, 8, 10, 11), (4, 5, 7, 9)

        def down_tile(g, e):
            return STREAM["experts"] + (e if g == 0 else 8 * g - 4 + e)

        def nth(base, later):
            return base[0] if later is None else later * base[1] + base[0]

        def pair_side(v, level, side):
            return v.rearrange("p (a s n) -> p a s n", s=2, n=2 ** level)[:, :, side, :]

        IN_TILES, DN_TILES, IN2_TILES, OUT_TILES = 52, 16, 41, 16
        SPLIT_BEFORE = {STREAM["w_in"]: 0, STREAM["dn_up"]: IN_TILES, STREAM["w_in_2"]: IN_TILES + DN_TILES,
                        STREAM["o_nsa"]: IN_TILES + DN_TILES + IN2_TILES}
        NORM_BANK = (7, 7, 7, 6, 7)
        X_IN, X_DELTA, X_MERGED, X_IN2, X_ATTN, X_MERGED2 = range(6)

        block = ctx.enter_context(nc.Block())

        @block.sync
        def _(sp):
            sp.wait_ge(x_part[3], 16)
            for s in range(RING):
                sp.dma_start(ring[:, s, :], stream[s, :, :]).then_inc(w_loaded[s], 16)
            loops = (N_STREAM - RING) // RING
            with sp.Fori(0, loops) as i:
                for s in range(RING):
                    sp.wait_ge(tile_done, i * RING + (s + 1))
                    sp.dma_start(ring[:, s, :], stream[ds(i * RING + (RING + s), 1), :, :]
                                 .rearrange("o p n -> p (o n)")).then_inc(w_loaded[s], 16)
            for n in range(RING * (loops + 1), N_STREAM):
                sp.wait_ge(tile_done, n - RING + 1)
                sp.dma_start(ring[:, n % RING, :], stream[n, :, :]).then_inc(w_loaded[n % RING], 16)

        @block.gpsimd
        def _(pool):
            g_ = nc.gpsimd
            count = [0]

            def link(ins):
                count[0] += 1
                ins.then_inc(g_chain, 1)
                pool.wait_ge(g_chain, count[0])

            pool.wait_ge(pads, 1)
            pool.wait_ge(par_loaded, 32)
            first = const("first").rearrange("p (g n) -> p g n", g=4)
            for g in range(4):
                pool.wait_ge(bank_free[g], 1)
                src = XA[:, g, :]
                for x in range(g + 1):
                    dst = pool_tmp[:, x % 2, :]
                    link(g_.tensor_tensor(dst[:, 16:], src[:, 16:], src[:, 16 - 2 ** x:16 + S - 2 ** x], ALU.add))
                    src = dst
                link(g_.tensor_tensor(RS16, src[:, 16:32], first[:, g, :], ALU.mult))
                link(g_.tensor_tensor(RS16, RS16, XA[:, g, 16:32], ALU.subtract))
                link(g_.tensor_scalar(src[:, 16:], src[:, 16:], 1.0 / 2 ** (g + 1), None, ALU.mult))
                link(g_.tensor_tensor(XA[:, g, 16:], src[:, 16:], XA[:, g, 16:], ALU.subtract))
                link(g_.tensor_copy(XA[:, g, 16:32], RS16))
            g_.memset(RS16, 0.0).then_inc(pool_ready, 1)

            own = [0, 0]
            for r in range(HEADS // 2):
                def each(fn, steps=1):
                    for p in range(2):
                        if own[p]:
                            pool.wait_ge(dG[p].sem, own[p])
                        fn(p, 2 * r + p, slots[p])
                        own[p] += steps

                def mask(p, h, s):
                    pool.wait_ge(dA[p].sem, dA[p].done(r, "sq"))
                    if r:
                        pool.wait_ge(dT[p].sem, dT[p].done(r - 1, "turn_o"))
                    g_.tensor_tensor(s.lk, over(const("strict"), 1, TT), over(beta[:, :, h], 2, P), ALU.mult)\
                        .then_inc(dG[p].sem, 1)

                def etm(p, h, s):
                    pool.wait_ge(dA[p].sem, dA[p].done(r, "e"))
                    g_.tensor_tensor(s.et, s.et, over(upper, 1, TT), ALU.mult).then_inc(dG[p].sem, 1)

                def kdec(p, h, s):
                    pool.wait_ge(dA[p].sem, dA[p].done(r, "eg"))
                    g_.tensor_tensor(s.kt, s.kt, over(s.edl, 2, HD), ALU.mult).then_inc(dG[p].sem, 1)

                for fn in (mask, etm):
                    each(fn)
                for l in range(1, LEVELS):
                    def lk(p, h, s):
                        if l == 1:
                            pool.wait_ge(dA[p].sem, dA[p].done(r, "lts"))
                            pool.wait_ge(dV[p].sem, dV[p].done(r, "l"))
                        else:
                            pool.wait_ge(dT[p].sem, dT[p].done(r, f"x{l - 1}"))
                        m = const("block")[:, l * P:(l + 1) * P]
                        g_.tensor_tensor(s.lk, s.df, over(m, 1, TT), ALU.mult).then_inc(dG[p].sem, 1)
                    each(lk)
                    if l == 1:
                        each(kdec)

            for d in range(KT):
                pool.wait_ge(bank_free[d % 4], (60 + d) // 4 + 1)
                g_.tensor_tensor(XN[:, d, :], GT[:, d, :], GT[:, 8 + d, :], ALU.add).then_inc(merged, 1)
            for h in range(8):
                pool.wait_ge(topk_done, 2 * h + 2)
                if h:
                    pool.wait_ge(cand_used, h)
                a, b = V1[:, :, 2 * h, :], V1[:, :, 2 * h + 1, :]
                g_.tensor_tensor(CAND[:, :, 0:64].rearrange("p c (a b) -> p c a b", a=4),
                                 over(a[:, :, 0:4], 3, 16), over(b, 2, 4), ALU.add)
                g_.tensor_tensor(CAND[:, :, 64:112].rearrange("p c (a b) -> p c a b", a=12),
                                 over(a[:, :, 4:16], 3, 4), over(b[:, :, 0:4], 2, 12), ALU.add).then_inc(cand_ready, 1)
            pool.wait_ge(i1f_ready, 1)
            for x in range(8):
                c, z = divmod(x, 2)
                pool.wait_ge(eq_ready, x + 1)
                e = EQ[:, x % 2, :].rearrange("p (h k j) -> p h k j", h=8, k=16)
                idx = I1F[:, c, :, :].rearrange("p (h z) j -> p h z j", z=2)[:, :, z, :]
                g_.tensor_tensor(e, e, over(idx, 2, 16), ALU.mult).then_inc(eq_mul, 1)

            with pool.Fori(0, S // 16) as j:
                for u in range(0, 16, 4):
                    pool.wait_ge(onehot_a, j * 4 + (u // 4 + 1))
                    rows = ONE_A[:, u:u + 4, :]
                    g_.tensor_tensor(rows, rows, over(GTT[:, ds(j * 16 + u, 4)], 2, P), ALU.mult)\
                        .then_inc(gated_a, 1)

            def load(g, par):
                pool.dma_start(GG[:, par, :, :, :].rearrange("p c e t -> p c (e t)"),
                               gate_dram[:, :, ds(g * GROUP, GROUP), :].rearrange("c p e t -> p c (e t)"))\
                    .then_inc(gate_loaded[par], 16)

            for par in range(2):
                pool.wait_ge(gate_written[par], 16 * (S // BLOCK_T // 2) + 16)
            load(0, 0)
            load(1, 1)
            with pool.Fori(0, 15) as i:
                pool.wait_ge(w_done, i * 8 + 4)
                load(i * 2 + 2, 0)
                pool.wait_ge(w_done, i * 8 + 8)
                load(i * 2 + 3, 1)

            for m in range(124, 129):
                pool.wait_ge(bank_free[m % 4], m // 4 + 1)
            for g in range(2):
                src = KK[g * 64:(g + 1) * 64, :, :]
                pool.dma_start(XC[0:64, :, g, :], src[:, 0:2, :]).then_inc(xc_ready, 16)
                pool.dma_start(XC[64:128, :, g, 0:S - 1], src[:, 0:2, 1:S]).then_inc(xc_ready, 16)
            for g in range(2):
                src = KK[g * 64:(g + 1) * 64, :, :]
                for half in range(2):
                    pool.dma_start(KD[half * 64:(half + 1) * 64, :, g, :], src[:, 2:5, :]).then_inc(dup_done, 16)
            for u, (kind, h) in enumerate(UNITS):
                pool.wait_ge(at_fac, u + 1)
                for i in range(TT):
                    w, _ = key_cols(kind, i)
                    p_ = SS[:, u % 3, i, 0:w]
                    last = g_.tensor_tensor(p_, p_, fac[:, u % 3, i:i + 1].broadcast_to([P, w]), ALU.mult)
                last.then_inc(at_weighted, 1)
            for d in range(KT):
                pool.wait_ge(bank_free[(137 + d) % 4], (137 + d) // 4 + 1)
                g_.tensor_tensor(XN[:, d, :], GT2[:, d, :], GT2[:, 8 + d, :], ALU.add).then_inc(merged, 1)
            pool.wait_ge(dup_done, 64)

        @block.scalar
        def _(act):
            def link(ins):
                a_count[0] += 1
                ins.then_inc(a_chain, 1)
                act.wait_ge(a_chain, a_count[0])

            a_count = [0]

            def take(m, dst, func):
                return nc.scalar.activation(dst, ps[:, m % 4, :], func)

            def tile_high(n0, t, dst, i=None):
                n, later = n0 + t, 0 if i is None else i
                act.wait_ge(w_loaded[n % RING], later * 16 + 16 * (n // RING + 1))
                if t >= 2:
                    act.wait_ge(tile_done, later * 8 + (n - 1))
                nc.scalar.activation(dst[:, t % 2, :], ring[:, n % RING, :], ACT.Copy).then_inc(tile_hi, 1)

            def x_high(k, src, dst):
                nc.scalar.activation(dst[:, k, :], src[:, k, :], ACT.Copy).then_inc(xn_hi, 1)

            def square(k, src, dst):
                nc.scalar.activation(dst[:, k, :], src[:, k, :], ACT.Square).then_inc(norm_sq, 1)

            def root(j):
                act.wait_ge(norm_ss, j + 1)
                nc.scalar.activation(rtok, ps[:, NORM_BANK[j], 0:TT], ACT.Sqrt, bias=const("eps")[:, 1:2]).then_inc(rs_out, 1)

            for q in range(4):
                act.dma_start(view(acts, q * 2 * S, 2 * S), x_in[:, q * 2 * S:(q + 1) * 2 * S]).then_inc(x_part[q], 16)
            act.dma_start(params[:, :], params_in).then_inc(par_loaded, 16)
            act.dma_start(consts[:, :], consts_in).then_inc(par_loaded, 16)
            for k in range(KT):
                act.wait_ge(x_part[k // 2], 16)
                square(k, XT, XN)
            act.wait_ge(par_loaded, 32)
            root(0)
            nc.scalar.activation(ea, param("a_log"), ACT.Exp).then_inc(silu_done, 2)
            nc.scalar.activation(BA_HI, param("w_ba"), ACT.Copy).then_inc(ba_hi, 1)
            for t in range(2):
                tile_high(0, t, W_HI1)
            for k in range(KT):
                act.wait_ge(norm_part, k + 1)
                x_high(k, XN, X_HI1)
            for m in range(4):
                act.wait_ge(tile_done, m + 1)
                tile_high(0, m + 2, W_HI1)
                take(m, XA[:, m, 16:], ACT.Copy).then_inc(bank_free[m % 4], 1)
            def raw_of(y, i=None):
                later = 0 if i is None else i * 8
                act.wait_ge(tile_done, later + (y + 5))
                tile_high(0, 6 + y, W_HI1, i)
                act.wait_ge(conv_done, later + (y + 1))
                take(4 + y, RAW[:, y % 2, 3:], ACT.Copy).then_inc(bank_free[y % 4], 1)

            def silu_of(y, i=None):
                later = 0 if i is None else i * 8
                act.wait_ge(conv_done, later + (y + 3))
                nc.scalar.activation(QKV[:, ds(later + y, 1), :].rearrange("p o t -> p (o t)"),
                                     CONV[:, y % 2, :], ACT.Silu).then_inc(silu_done, 1)

            raw_of(0)
            with act.Fori(0, 2) as i:
                for u in range(8):
                    raw_of(u + 1, i)
                    silu_of(u, i)
            for y in range(16, 24):
                if y < 23:
                    raw_of(y + 1)
                silu_of(y)
            for u in range(8):
                act.wait_ge(tile_done, 29 + u)
                tile_high(0, 30 + u, W_HI1)
                take(28 + u, Z[:, u, :], ACT.Silu).then_inc(bank_free[u % 4], 1)
            act.wait_ge(pool_ready, 1)
            for u in range(16):
                act.wait_ge(tile_done, 37 + u)
                if 38 + u < IN_TILES:
                    tile_high(0, 38 + u, W_HI1)
                take(36 + u, GT[:, u, :], ACT.Sigmoid).then_inc(bank_free[u % 4], 1)
            for g in range(4):
                act.wait_ge(pooly_done, g + 1)
                nc.scalar.activation(XA[:, g, 16:], ps[:, 4 + g, :], ACT.Copy,
                                     scale=param("pool_scale")[:, g:g + 1]).then_inc(yt_ready, 1)
            act.wait_ge(ba_v, 1)
            logits = ps[:, 4, 0:64].rearrange("p (c n) -> p c n", c=TT)
            nc.scalar.activation(beta, logits[:, :, 0:8], ACT.Sigmoid).then_inc(ba_a, 1)
            act.wait_ge(ba_v, 1)
            link(nc.scalar.activation(sp_a, sp_a, ACT.Exp, scale=-1.0))
            nc.scalar.activation(sp_b, sp_a, ACT.Ln, bias=1.0).then_inc(ba_a, 1)
            act.wait_ge(ba_v, 3)
            nc.scalar.activation(egc, gc, ACT.Exp).then_inc(ba_a, 1)

            act.wait_ge(silu_done, 26)
            act.wait_ge(tile_done, 56)
            own = [0, 0]

            def z_high(r):
                for p in range(2):
                    act.wait_ge(dV[p].sem, dV[p].done(r, "fin"))
                    x_high(2 * r + p, Z, Z_HI)

            for r in range(HEADS // 2):
                def each(fn, steps=1):
                    for p in range(2):
                        if own[p]:
                            act.wait_ge(dA[p].sem, own[p])
                        fn(p, 2 * r + p, slots[p], 4 * p)
                        own[p] += steps

                def four(v):
                    return v.rearrange("p c t -> p (c t)")

                def sq(p, h, s, b):
                    nc.scalar.activation(s.sq[:, 0, :], QKV[:, h, :], ACT.Square)
                    nc.scalar.activation(s.sq[:, 1, :], QKV[:, 8 + h, :], ACT.Square).then_inc(dA[p].sem, 1)

                def root_qk(p, h, s, b):
                    act.wait_ge(dT[p].sem, dT[p].done(r, "sumsq"))
                    nc.scalar.activation(s.rqk, ps[:, b, 0:8], ACT.Sqrt, bias=const("eps")[:, 0:1])\
                        .then_inc(dA[p].sem, 1)

                def ktok(p, h, s, b):
                    act.wait_ge(dT[p].sem, dT[p].done(r, "turn"))
                    nc.scalar.activation(four(s.kt), ps[:, b, :], ACT.Copy).then_inc(dA[p].sem, 1)

                def e(p, h, s, b):
                    act.wait_ge(dV[p].sem, dV[p].done(r, "diff"))
                    nc.scalar.activation(s.ed, s.ed, ACT.Exp, scale=-1.0)
                    nc.scalar.activation(s.et, s.et, ACT.Exp).then_inc(dA[p].sem, 1)
                    gl = ps[:, b, :].rearrange("p (c t) -> p c t", c=TT)[:, :, P - 1]
                    nc.scalar.activation(s.egl, gl, ACT.Exp)
                    nc.scalar.activation(s.edl, s.df[:, :, P - 1], ACT.Exp).then_inc(dA[p].sem, 1)

                def lts(p, h, s, b):
                    act.wait_ge(dT[p].sem, dT[p].done(r, "lt"))
                    nc.scalar.activation(four(s.df), ps[:, b + 1, :], ACT.Copy).then_inc(dA[p].sem, 1)

                for fn in (sq, root_qk, ktok):
                    each(fn)
                if r:
                    z_high(r - 1)
                each(e, 2)
                each(lts)
                for l in range(1, LEVELS):
                    def x(p, h, s, b):
                        act.wait_ge(dT[p].sem, dT[p].done(r, f"x{l}"))
                        nc.scalar.activation(four(s.x), ps[:, b, :], ACT.Copy).then_inc(dA[p].sem, 1)
                    each(x)
                for c in range(TT):
                    def vn(p, h, s, b):
                        act.wait_ge(dT[p].sem, dT[p].done(r, f"v{c}"))
                        nc.scalar.activation(s.vn, ps[:, b + 1, 0:P], ACT.Copy).then_inc(dA[p].sem, 1)
                    each(vn)

                def osq(p, h, s, b):
                    act.wait_ge(dV[p].sem, dV[p].done(r, f"o{TT - 1}"))
                    for c in range(TT):
                        last = nc.scalar.activation(s.x[:, c, :], s.t[:, c, :], ACT.Square,
                                                    accum_out=s.oss[:, c:c + 1])
                    link(last)
                    nc.scalar.activation(s.ors, s.oss, ACT.Sqrt, scale=1.0 / HD, bias=const("eps")[:, 0:1])\
                        .then_inc(dA[p].sem, 1)
                each(osq)

            for p in range(2):
                act.wait_ge(dV[p].sem, dV[p].done(3, "fin"))
            act.dma_start(view(acts, 0, KT * S), x_in).then_inc(x_loaded, 16)
            z_high(3)
            nd = STREAM["dn_up"]
            for t in range(2):
                tile_high(nd, t, W_HID)
            for t in range(DN_TILES):
                act.wait_ge(tile_done, nd + t + 1)
                if t + 2 < DN_TILES:
                    tile_high(nd, t + 2, W_HID)
                if t < KT:
                    act.wait_ge(merged, t + 1)
                    x_high(t, XN, M_HI1)
                else:
                    d = t - KT
                    act.wait_ge(bank_free[d % 4], (68 + d) // 4 + 1)
                    square(d, XT, SQ1)
            act.dma_start(keys.rearrange("p a b -> p (a b)"), keys_in).then_inc(keys_loaded, 16)
            root(1)
            for hz in range(17):
                if hz < 16:
                    act.wait_ge(tile_done, STREAM["query"] + hz + 1)
                    take(76 + hz, QP[:, hz, :], ACT.Copy).then_inc(bank_free[hz % 4], 1)
                if hz:
                    q = hz - 1
                    act.wait_ge(sc_done, q + 1)
                    if q >= 2:
                        act.wait_ge(topk_done, q - 1)
                    nc.scalar.activation(SC[:, q % 2, :, :].rearrange("p c t -> p (c t)"), ps[:, 4 + q % 4, :],
                                         ACT.Copy).then_inc(sc_ready, 1)
            act.wait_ge(gd_ready, 1)
            nc.scalar.activation(TOP.rearrange("p c h k -> p (c h k)"), view(CAND_FLAT, 0, 512), ACT.Exp)\
                .then_inc(ge_ready, 1)
            nc.scalar.activation(zero_exp[:, 0:1], ea[:, 0:1], ACT.Copy).then_inc(gate_out, 4)
            nc.scalar.activation(zero_exp[:, 1:2], ea[:, 0:1], ACT.Copy).then_inc(gate_written[0], 16)
            nc.scalar.activation(zero_exp[:, 2:3], ea[:, 0:1], ACT.Copy).then_inc(gate_written[1], 16)
            for n, dst in enumerate((I1T, I2T, GTT)):
                act.wait_ge(turned, n + 1)
                nc.scalar.activation(dst, ps[:, 4 + n, :], ACT.Copy).then_inc(turned_read, 1)
            nc.scalar.activation(XH.rearrange("p k t -> p (k t)"), view(acts, KT * S, KT * S), ACT.Copy)\
                .then_inc(x_hi, 1)
            with act.Fori(0, S // BLOCK_T // 2) as cc:
                for par in range(2):
                    act.wait_ge(gate_written[par], cc * 16 + 16)
                    with act.Fori(0, BLOCK_T // 16) as j:
                        for q in range(4):
                            act.wait_ge(token_mm, cc * (32 * 4) + j * 16 + (par * 64 + 4 * (q + 1) + 16))
                            nc.scalar.activation(
                                GB[:, par, :, ds(j * 16 + 4 * q, 4)],
                                ps[:, 4 + q, :].rearrange("p (t i) -> p i t", t=4), ACT.Copy)\
                                .then_inc(gate_out, 1)
                    act.wait_ge(gate_out, cc * 32 + (16 * (par + 1) + 4))
                    act.dma_start(gate_dram[ds(cc * 2 + par, 1), :, :, :].rearrange("o p i t -> p (o i t)"),
                                  GB[:, par, :, :].rearrange("p i t -> p (i t)")).then_inc(gate_written[par], 16)
            act.wait_ge(tile_done, STREAM["ada"] + 24)
            for p0, n in zip(ADA_PART, (16, 8)):
                last = nc.scalar.activation(ADA_ROWS[p0:p0 + 1, 0:n * P],
                                            ps[p0:p0 + 1, 0:n // 4, :].rearrange("p b n -> p (b n)"), ACT.Copy)
            last.then_inc(ada_rows, 1)
            act.wait_ge(x_lo, 1)
            e0 = STREAM["experts"]

            def high(n, dst, freed, i):
                act.wait_ge(w_loaded[n % RING], nth((16 * (n // RING + 1), 32), i))
                if freed is not None:
                    act.wait_ge(tile_done, nth((freed + 1, 16), i))
                nc.scalar.activation(dst, ring[:, n % RING, :], ACT.Copy).then_inc(split_hi, 1)

            def high_down(g, e, i=None):
                n = down_tile(g, e)
                freed = n - 2 if e >= 2 else (down_tile(g - 1, e + 2) if g else None)
                high(n, DH[:, e % 2, :], freed, i)

            def high_up(g, e, i=None):
                n = e0 + 8 * g + 8 + e if g < 31 else e0 + 252 + e
                high(n, UH[:, e, :], n - 8 if 0 < g < 31 else (n - 4 if g == 31 else None), i)

            def acts_of(g, e, i=None):
                act.wait_ge(tile_done, nth((down_tile(g, e) + 1, 16), i))
                if g or e >= 2:
                    act.wait_ge(w_done, nth((4 * g + e - 1, 8), i))
                nc.scalar.activation(GE[:, e % 2, :], ps[:, e % 2, :], ACT.Gelu).then_inc(gelu_done, 1)
                if g == 0 and e == 0:
                    for par in range(2):
                        act.wait_ge(gate_written[par], 16 * (S // BLOCK_T // 2) + 16)
                act.wait_ge(prod_done, nth((4 * g + e + 1, 8), i))
                nc.scalar.activation(WH[:, g % 2, e, :], GE[:, e % 2, :], ACT.Copy).then_inc(w_hi, 1)

            def step(g, i=None):
                for e in range(GROUP):
                    high_up(g, e, i)
                    if e < 2:
                        high_down(g + 1, e + 2, i)
                    acts_of(g + 1, e, i)
                if g < 30:
                    for e in range(2):
                        high_down(g + 2, e, i)

            for e in range(2):
                high_down(0, e)
            for e in range(GROUP):
                if e < 2:
                    high_down(0, e + 2)
                acts_of(0, e)
            for e in range(2):
                high_down(1, e)
            act.wait_ge(ada_turned, 1)
            step(0)
            step(1)
            with act.Fori(1, 15) as i:
                for g in range(2, 4):
                    step(g, i - 1)
            step(30)
            for e in range(GROUP):
                high_up(31, e)
            for d in range(KT):
                act.wait_ge(acc_done, 8 * 32 + d + 1)
                square(d, XT, XN)
            root(2)
            for k in range(KT):
                act.wait_ge(final_part, k + 1)
                square(k, XT, XN)
            root(3)

            n0 = STREAM["w_in_2"]
            for t in range(2):
                tile_high(n0, t, W_HI2)
            for k in range(KT):
                act.wait_ge(norm_part, KT + k + 1)
                x_high(k, XN, X_HI2)
            for u in range(16):
                act.wait_ge(tile_done, n0 + u + 1)
                tile_high(n0, u + 2, W_HI2)
                take(92 + u, QA[:, u, :] if u < 8 else ZZ[:, u - 8, :], ACT.Copy if u < 8 else ACT.Silu)\
                    .then_inc(bank_free[u % 4], 1)
            with act.Fori(0, 2) as i:
                for u in range(8):
                    act.wait_ge(tile_done, i * 8 + (n0 + 17 + u))
                    tile_high(n0, 18 + u, W_HI2, i)
                    take(108 + u, GT2[:, ds(i * 8 + u, 1), :].rearrange("p o t -> p (o t)"), ACT.Sigmoid)\
                        .then_inc(bank_free[u % 4], 1)
            for u in range(5):
                act.wait_ge(tile_done, n0 + 33 + u)
                tile_high(n0, 34 + u, W_HI2)
                take(124 + u, KK[:, u, :], ACT.Copy).then_inc(bank_free[u % 4], 1)
            for t in range(39, IN2_TILES):
                tile_high(n0, t, W_HI2)
            act.wait_ge(tile_done, STREAM["v_tok"] + 4)
            for c in range(TT):
                nc.scalar.activation(VT[:, c, :], ps[:, 4 + c, 0:384], ACT.Copy)
                nc.scalar.activation(gn[:, c, :], ps[:, 4 + c, 384:408], ACT.Sigmoid).then_inc(v_ready, 1)
            for kv in range(2):
                act.wait_ge(tile_done, STREAM["cmp_k1" if kv == 0 else "cmp_v1"] + 4)
                for a in range(2):
                    last = nc.scalar.activation(HID[:, kv, a, :], ps[:, 4 + 2 * kv + a, 0:62], ACT.Silu)
                last.then_inc(hid_ready, 1)
            act.wait_ge(kv_done, 1)
            nc.scalar.activation(KC[:, 0:62], ps[:, 0, 0:62], ACT.Copy)
            nc.scalar.activation(VC[0:NC_CMP, :, :].rearrange("p g d -> p (g d)"), ps[0:NC_CMP, 1, 0:128], ACT.Copy)\
                .then_inc(kc_ready, 1)

            def exps(u):
                kind, h = UNITS[u]
                par = u % 3
                act.wait_ge(at_scaled, u + 1)
                if kind == "swa":
                    nc.scalar.activation(esink[:, par, :], nm[:, par, :], ACT.Exp, bias=param("sinks")[:, h:h + 1])
                for i in range(TT):
                    w, _ = key_cols(kind, i)
                    last = nc.scalar.activation(SS[:, par, i, 0:w], SS[:, par, i, 0:w], ACT.Exp,
                                                bias=nm[:, par, i:i + 1], scale=NSA_SCALE,
                                                accum_out=den[:, par, i:i + 1])
                last.then_inc(at_exp, 1)

            def copies(u):
                kind, h = UNITS[u]
                par = u % 2
                if u >= 2:
                    act.wait_ge(at_out, u - 1)
                for x, (kt, tiles) in enumerate(turns(kind)):
                    chunk = CHUNKS[u] + x
                    act.wait_ge(at_turned, chunk + 1)
                    m = NC_CMP if kind == "cmp" else P
                    a, b = tiles[0] * P, (tiles[-1] + 1) * P
                    nc.scalar.activation(PT[0:m, par, kt, a:b], ps[0:m, 4 + chunk % 2, a:b], ACT.Copy)\
                        .then_inc(at_copied, 1)

            def o_high(t):
                act.wait_ge(o_ready, t + 1)
                x_high(t, QA, O_HI)

            no = STREAM["o_nsa"]
            for t in range(2):
                tile_high(no, t, W_HI3)
            exps(0)
            exps(1)
            for u in range(len(UNITS)):
                copies(u)
                if u + 2 < len(UNITS):
                    exps(u + 2)
                if u - 4 in OUT_UNITS:
                    o_high(OUT_UNITS.index(u - 4))
            for t in range(sum(w + 4 < len(UNITS) for w in OUT_UNITS), 8):
                o_high(t)
            for t in range(OUT_TILES):
                act.wait_ge(tile_done, no + t + 1)
                if t + 2 < OUT_TILES:
                    tile_high(no, t + 2, W_HI3)
                if 4 <= t < 8:
                    for d in range(2 * (t - 4), 2 * (t - 3)):
                        act.wait_ge(merged, KT + d + 1)
                        x_high(d, XN, M_HI2)
                if t >= 8:
                    take(145 + t - 8, ZZ[:, t - 8, :], ACT.Copy).then_inc(bank_free[(145 + t - 8) % 4], 1)
                    act.wait_ge(bank_free[(145 + t - 8) % 4], (145 + t - 8) // 4 + 1)
                    square(t - 8, ZZ, SQ1)
            root(4)
            act.wait_ge(out_ready, 1)
            act.dma_start(out, view(acts, 0, KT * S)).then_inc(out_written, 16)
            act.wait_ge(out_written, 16)

        @block.vector
        def _(dve):
            v = nc.vector
            count = [0]

            def link(ins):
                count[0] += 1
                ins.then_inc(v_chain, 1)
                dve.wait_ge(v_chain, count[0])

            def norm(j, src, dst, weight, part=None):
                link(v.tensor_scalar(w32, weight, float(np.sqrt(D)), None, ALU.mult))
                dve.wait_ge(rs_out, j + 1)
                link(v.reciprocal(rtok, rtok))
                v.tensor_tensor(RS[:, :].rearrange("p (c t) -> p c t", c=TT), over(ident, 1, TT), over(rtok, 2, P),
                                ALU.mult).then_inc(norm_diag, 1)
                dve.wait_ge(norm_bc, j + 1)
                for k in range(KT):
                    last = v.scalar_tensor_tensor(dst[:, k, :], src[:, k, :], w32[:, k:k + 1], ps[:, 7, :],
                                                  ALU.mult, ALU.mult)
                    if part:
                        last.then_inc(part, 1)
                return last

            def tile_low(n0, t, hi, i=None):
                n = n0 + t
                dve.wait_ge(tile_hi, nth((SPLIT_BEFORE[n0] + t + 1, 8), i))
                v.tensor_tensor(RING_LO[:, n % RING, :], ring[:, n % RING, :], hi[:, t % 2, :].bitcast(f32),
                                ALU.subtract).then_inc(tile_lo, 1)

            def x_low(j, k, src, hi, lo):
                dve.wait_ge(xn_hi, 8 * j + k + 1)
                v.tensor_tensor(lo[:, k, :], src[:, k, :], hi[:, k, :].bitcast(f32), ALU.subtract).then_inc(xn_lo, 1)

            v.memset(XA[:, :, 0:16], 0.0)
            v.memset(pool_tmp[:, :, 0:16], 0.0).then_inc(pads, 1)
            v.memset(RAW[:, :, 0:3], 0.0).then_inc(conv_done, 2)
            v.memset(zero_v, 0.0).then_inc(token_mm, 16)
            v.memset(zero_w, 0.0).then_inc(acc_done, 8)
            dve.wait_ge(par_loaded, 32)
            dve.wait_ge(acc_done, 8)
            norm(0, XT, XN, param("mix_norm_w"), norm_part)
            for t in range(2):
                tile_low(0, t, W_HI1)
            for k in range(KT):
                x_low(X_IN, k, XN, X_HI1, X_LO)
            dve.wait_ge(ba_hi, 1)
            v.tensor_tensor(BA_LO, param("w_ba"), BA_HI.bitcast(f32), ALU.subtract).then_inc(ba_lo, 1)
            for m in range(4):
                tile_low(0, m + 2, W_HI1)
            with dve.Fori(0, 3) as i:
                for u in range(8):
                    tile_low(0, 6 + u, W_HI1, i)
                    raw, y = RAW[:, u % 2, :], CONV[:, u % 2, :]
                    dve.wait_ge(bank_free[u % 4], i * 2 + (u // 4 + 2))
                    dve.wait_ge(silu_done, i * 8 + (u + 1))
                    dve.wait_ge(conv_done, i * 8 + (u + 2))

                    def w(tap):
                        return param("conv_w")[:, ds(i * 32 + (u * 4 + tap), 1)]
                    v.tensor_scalar(y, raw[:, 3:3 + S], w(3), None, ALU.mult).then_inc(conv_part, 1)
                    for x in (2, 1, 0):
                        dve.wait_ge(conv_part, i * 24 + (3 * u + 3 - x))
                        v.scalar_tensor_tensor(y, raw[:, x:x + S], w(x), y, ALU.mult, ALU.add)\
                            .then_inc(conv_part if x else conv_done, 1)
            for t in range(30, IN_TILES):
                tile_low(0, t, W_HI1)
            for d in range(KT):
                dve.wait_ge(tile_done, 53 + d // 2)
                v.tensor_tensor(GT[:, d, :], GT[:, d, :], ps[:, d % 4, :], ALU.mult).then_inc(bank_free[d % 4], 1)
            dve.wait_ge(ba_done, 1)
            logits = ps[:, 4, 0:64].rearrange("p (c n) -> p c n", c=TT)
            link(v.tensor_tensor(a_in, logits[:, :, 8:16], over(param("dt_bias"), 1, TT), ALU.add))
            v.scalar_tensor_tensor(sp_a, a_in, -1.0, a_in, ALU.mult, ALU.max).then_inc(ba_v, 1)
            dve.wait_ge(ba_a, 2)
            link(v.scalar_tensor_tensor(sp_b, a_in, 0.0, sp_b, ALU.max, ALU.add))
            v.scalar_tensor_tensor(g_log, sp_b, -1.0, over(ea, 1, TT), ALU.mult, ALU.mult).then_inc(ba_v, 1)
            dve.wait_ge(gc_done, 1)
            v.tensor_copy(gc.rearrange("p c h -> p (c h)"), ps[:, 5, 0:TT * 8]).then_inc(ba_v, 1)
            dve.wait_ge(ba_a, 3)
            v.scalar_tensor_tensor(nbeg, beta, -1.0, egc, ALU.mult, ALU.mult).then_inc(gc_ready, 1)
            dve.wait_ge(gc_ready, 1)

            own = [0, 0]

            def z_low(r):
                for h in (2 * r, 2 * r + 1):
                    x_low(X_DELTA, h, Z, Z_HI, Z_LO)

            for r in range(HEADS // 2):
                def each(fn, steps=1):
                    for p in range(2):
                        if own[p]:
                            dve.wait_ge(dV[p].sem, own[p])
                        fn(p, 2 * r + p, slots[p], 4 * p)
                        own[p] += steps

                def bank(b):
                    return ps[:, b, :].rearrange("p (c t) -> p c t", c=TT)

                def rd(p, h, s, b):
                    dve.wait_ge(dA[p].sem, dA[p].done(r, "root"))
                    link(v.reciprocal(s.rqk, s.rqk))
                    v.tensor_tensor(s.sq.rearrange("p a (c t) -> p (a c) t", c=TT), over(ident, 1, 8),
                                    over(s.rqk, 2, P), ALU.mult).then_inc(dV[p].sem, 1)

                def norm_qk(p, h, s, b):
                    dve.wait_ge(dT[p].sem, dT[p].done(r, "spread"))
                    v.scalar_tensor_tensor(QKV[:, h, :], QKV[:, h, :], HD ** -0.5, ps[:, b, :], ALU.mult, ALU.mult)
                    v.tensor_tensor(QKV[:, 8 + h, :], QKV[:, 8 + h, :], ps[:, b + 1, :], ALU.mult)\
                        .then_inc(dV[p].sem, 1)

                def vb(p, h, s, b):
                    dve.wait_ge(dT[p].sem, dT[p].done(r, "turn"))
                    v.tensor_tensor(s.vb, bank(b + 1), over(beta[:, :, h], 2, HD), ALU.mult).then_inc(dV[p].sem, 1)
                    v.tensor_tensor(s.gu, over(upper, 1, TT), over(g_log[:, :, h], 2, P), ALU.mult)\
                        .then_inc(dV[p].sem, 1)

                def bkk(p, h, s, b):
                    dve.wait_ge(dT[p].sem, dT[p].done(r, "gram"))
                    dve.wait_ge(dG[p].sem, dG[p].done(r, "mask"))
                    v.tensor_tensor(s.lk, bank(b + 2), s.lk, ALU.mult).then_inc(dV[p].sem, 1)

                def diff(p, h, s, b):
                    dve.wait_ge(dT[p].sem, dT[p].done(r, "decay"))
                    link(v.tensor_tensor(s.df, bank(b), over(gc[:, :, h], 2, P), ALU.subtract))
                    v.tensor_scalar(s.ed, s.df, 0.0, None, ALU.max)
                    v.tensor_scalar(s.et, s.df, 0.0, None, ALU.min).then_inc(dV[p].sem, 1)

                def lower(p, h, s, b):
                    dve.wait_ge(dA[p].sem, dA[p].done(r, "e"))
                    v.tensor_tensor(s.ed, s.ed, s.lk, ALU.mult).then_inc(dV[p].sem, 1)

                def upper_kq(p, h, s, b):
                    dve.wait_ge(dG[p].sem, dG[p].done(r, "etm"))
                    v.tensor_tensor(s.et, bank(b + 3), s.et, ALU.mult).then_inc(dV[p].sem, 1)

                def level0(p, h, s, b):
                    dve.wait_ge(dA[p].sem, dA[p].done(r, "lts"))
                    link(v.tensor_tensor(s.tt, s.df, over(const("block")[:, 0:P], 1, TT), ALU.mult))
                    v.tensor_tensor(s.tt, over(ident, 1, TT), s.tt, ALU.subtract).then_inc(dV[p].sem, 1)

                def t1(p, h, s, b):
                    dve.wait_ge(dT[p].sem, dT[p].done(r, "t1"))
                    v.tensor_copy(s.t, bank(b)).then_inc(dV[p].sem, 1)

                for fn, steps in ((rd, 1), (norm_qk, 1), (vb, 2), (bkk, 1), (diff, 1), (lower, 1), (level0, 1),
                                  (upper_kq, 1), (t1, 1)):
                    each(fn, steps)
                    if r and fn is diff:
                        z_low(r - 1)
                for l in range(1, LEVELS):
                    def up(p, h, s, b):
                        dve.wait_ge(dT[p].sem, dT[p].done(r, f"tx{l}"))
                        dve.wait_ge(dV[p].sem, dV[p].done(r, "t" if l == 1 else f"u{l - 1}"))
                        def less(x, side, pb):
                            o = pair_side(x, l, side)
                            return v.tensor_tensor(o, o, ps[:, pb, 0:256].rearrange("p (a n) -> p a n", n=2 ** l),
                                                   ALU.subtract)
                        if l < LEVELS - 1:
                            less(s.t.rearrange("p c t -> p (c t)"), 0, b + 2)
                        less(s.tt.rearrange("p c t -> p (c t)"), 1, b + 3).then_inc(dV[p].sem, 1)
                    each(up)
                for c in range(TT):
                    def r_(p, h, s, b):
                        dve.wait_ge(dT[p].sem, dT[p].done(r, f"pq{c}"))
                        v.scalar_tensor_tensor(s.r, ps[:, b, 0:P], nbeg[:, c, h:h + 1], s.vb[:, c, :],
                                               ALU.mult, ALU.add).then_inc(dV[p].sem, 1)

                    def so(p, h, s, b):
                        dve.wait_ge(dT[p].sem, dT[p].done(r, f"os{c}"))
                        o = ps[:, b + 1, P:2 * P]
                        if c == 0:
                            v.tensor_copy(s.state, ps[:, b + 1, 2 * P:3 * P]).then_inc(dV[p].sem, 1)
                            v.tensor_copy(s.t[:, c, :], o).then_inc(dV[p].sem, 1)
                            return
                        if c < TT - 1:
                            dve.wait_ge(dV[p].sem, dV[p].done(r, f"s{c - 1}"))
                            v.scalar_tensor_tensor(s.state, s.state, s.egl[:, c:c + 1], ps[:, b + 1, 2 * P:3 * P],
                                                   ALU.mult, ALU.add).then_inc(dV[p].sem, 1)
                        link(v.tensor_scalar(s.t[:, c, :], ps[:, b, P:2 * P], egc[:, c, h:h + 1], None, ALU.mult))
                        v.tensor_tensor(s.t[:, c, :], s.t[:, c, :], o, ALU.add).then_inc(dV[p].sem, 1)

                    if c:
                        each(r_)
                    each(so, 2 if c < TT - 1 else 1)

                def dg(p, h, s, b):
                    dve.wait_ge(dA[p].sem, dA[p].done(r, "oroot"))
                    link(v.reciprocal(s.ors, s.ors))
                    v.tensor_tensor(s.lk, over(ident, 1, TT), over(s.ors, 2, P), ALU.mult).then_inc(dV[p].sem, 1)

                def fin(p, h, s, b):
                    dve.wait_ge(dT[p].sem, dT[p].done(r, "turn_o"))
                    v.scalar_tensor_tensor(Z[:, h, :], ps[:, b + 2, :], param("dn_norm_w"), Z[:, h, :],
                                           ALU.mult, ALU.mult).then_inc(dV[p].sem, 1)
                each(dg)
                each(fin)

            nd = STREAM["dn_up"]
            for t in range(2):
                tile_low(nd, t, W_HID)
            z_low(3)
            for d in range(KT):
                dve.wait_ge(tile_done, nd + d + 1)
                v.tensor_tensor(GT[:, 8 + d, :], GT[:, 8 + d, :], ps[:, d % 4, :], ALU.mult)\
                    .then_inc(bank_free[d % 4], 1)
                tile_low(nd, d + 2, W_HID)
                x_low(X_MERGED, d, XN, M_HI1, X_LO)
            dve.wait_ge(x_loaded, 16)
            for d in range(KT):
                if d + 10 < DN_TILES:
                    tile_low(nd, d + 10, W_HID)
                dve.wait_ge(tile_done, STREAM["mix_out"] + d + 1)
                v.tensor_tensor(XT[:, d, :], XT[:, d, :], ps[:, d % 4, :], ALU.add).then_inc(bank_free[d % 4], 1)
            for b in range(4):
                dve.wait_ge(bank_free[b], 19)
            norm(1, XT, XN, param("ffn_norm_w")).then_inc(norm_done, 1)

            i1u, posu = I1.bitcast(u32), POS.bitcast(u32)

            def top16(sources, spare, values, indices, sig):
                for c in range(TT):
                    last = v.max(values[c][:, 0:8], sources[c])
                link(last)
                for c in range(TT):
                    v.max_index(indices[c][:, 0:8], values[c][:, 0:8], sources[c])
                for c in range(TT):
                    last = v.match_replace(spare[c], values[c][:, 0:8], sources[c], -3.0e38)
                link(last)
                for c in range(TT):
                    last = v.max(values[c][:, 8:16], spare[c])
                link(last)
                for c in range(TT):
                    last = v.max_index(indices[c][:, 8:16], values[c][:, 8:16], spare[c])
                last.then_inc(sig, 1)

            def pick(h):
                dve.wait_ge(cand_ready, h + 1)
                top16([CAND[:, c, 0:112] for c in range(TT)], [CAND2[:, c, 0:112] for c in range(TT)],
                      [TOP[:, c, h, :] for c in range(TT)], [posu[:, c, h, :] for c in range(TT)], cand_used)

            for q in range(16):
                dve.wait_ge(sc_ready, q + 1)
                top16([SC[:, q % 2, c, :] for c in range(TT)], [SC2[:, c, :] for c in range(TT)],
                      [V1[:, c, q, :] for c in range(TT)], [i1u[:, c, q, :] for c in range(TT)], topk_done)
                if q % 2 == 0 and q:
                    pick(q // 2 - 1)
            pick(7)
            dve.wait_ge(cand_used, 8)
            dve.wait_ge(topk_done, 16)
            v.tensor_copy(I1F, i1u).then_inc(i1f_ready, 1)
            flat = posu.rearrange("p c h k -> p (c h k)")
            bits = [BITS[:, x, :].bitcast(u32) for x in range(4)]
            for dst, op, n in zip(bits, (ALU.logical_shift_right,) * 2 + (ALU.bitwise_and,) * 2, (4, 2, 12, 3)):
                last = v.tensor_scalar(dst, flat, n, None, op)
            link(last)
            first, second = (PF[:, z, :, :, :].rearrange("p c h k -> p (c h k)") for z in range(2))
            link(v.scalar_tensor_tensor(first, bits[1], 12.0, bits[0], ALU.subtract, ALU.max))
            link(v.scalar_tensor_tensor(second, first, 4.0, bits[2], ALU.is_lt, ALU.mult))
            link(v.tensor_tensor(second, second, bits[3], ALU.add))
            gtmp = view(CAND_FLAT, 0, TT, 8, TOPK)
            v.tensor_tensor(gtmp, TOP, TOP[:, :, :, 0:1].broadcast_to([P, TT, 8, TOPK]), ALU.subtract)\
                .then_inc(gd_ready, 1)

            def eq(x):
                c, z = divmod(x, 2)
                if x >= 2:
                    dve.wait_ge(sel_ready, x - 1)
                v.tensor_tensor(EQ[:, x % 2, :].rearrange("p (h k j) -> p h k j", h=8, k=16),
                                over(PF[:, z, c, :, :], 3, 16), over(over(iota[:, 0:16], 1, 16), 1, 8),
                                ALU.is_equal).then_inc(eq_ready, 1)

            eq(0)
            for x in range(8):
                if x < 7:
                    eq(x + 1)
                c, z = divmod(x, 2)
                dve.wait_ge(eq_mul, x + 1)
                v.tensor_reduce(SEL[:, z, c, :], EQ[:, x % 2, :].rearrange("p (n j) -> p n j", j=16),
                                AX.X, ALU.add).then_inc(sel_ready, 1)
            dve.wait_ge(ge_ready, 1)
            link(v.tensor_reduce(GSUM, TOP, AX.X, ALU.add))
            link(v.reciprocal(GSUM, GSUM))
            v.tensor_tensor(TOP, TOP, over(GSUM, 3, TOPK), ALU.mult).then_inc(gate_ready, 1)
            dve.wait_ge(turned_read, 3)
            with dve.Fori(0, S // 16) as j:
                for u in range(0, 16, 4):
                    dve.wait_ge(token_mm, j * 16 + (u + 4))
                    for one, key, ready in ((ONE_A, I1T, onehot_a), (ONE_B, I2T, onehot_b)):
                        v.tensor_tensor(one[:, u:u + 4, :], over(iota, 1, 4), over(key[:, ds(j * 16 + u, 4)], 2, P),
                                        ALU.is_equal).then_inc(ready, 1)

            e0 = STREAM["experts"]

            def low(index, n, hi, lo, i):
                dve.wait_ge(split_hi, nth((index + 1, 16), i))
                v.tensor_tensor(lo, ring[:, n % RING, :], hi.bitcast(f32), ALU.subtract).then_inc(split_lo, 1)

            def low_down(g, e, i=None):
                n = down_tile(g, e)
                low(e if g == 0 else 8 * (g - 1) + SPLIT_D[e], n, DH[:, e % 2, :], DL[:, e % 2, :], i)

            def low_up(g, e, i=None):
                n = e0 + 8 * g + 8 + e if g < 31 else e0 + 252 + e
                low(8 * g + SPLIT_U[e] if g < 31 else 252 + e, n, UH[:, e, :], UL[:, e, :], i)

            def weigh(g, e, i=None):
                if e == 0:
                    dve.wait_ge(gate_loaded[g % 2], nth((16 * (g // 2 + 1), 16), i))
                dve.wait_ge(gelu_done, nth((4 * g + e + 1, 8), i))
                ge = GE[:, e % 2, :]
                v.tensor_tensor(ge.rearrange("p (c t) -> p c t", t=BLOCK_T), ge.rearrange("p (c t) -> p c t", t=BLOCK_T),
                                GG[:, g % 2, :, e, :], ALU.mult).then_inc(prod_done, 1)
                dve.wait_ge(w_hi, nth((4 * g + e + 1, 8), i))
                v.tensor_tensor(WL[:, g % 2, e, :], ge, WH[:, g % 2, e, :].bitcast(f32), ALU.subtract)\
                    .then_inc(w_done, 1)

            def accumulate(g, i=None):
                n = e0 + 8 * g + 8 if g < 31 else e0 + 252
                for d in range(KT):
                    if d < KT - 1:
                        dve.wait_ge(y_done, nth((7 * g + d + 1, 14), i))
                    else:
                        dve.wait_ge(tile_done, nth((n + 4, 16), i))
                    dve.wait_ge(acc_done, nth((8 * g + d + 1, 16), i))
                    v.tensor_tensor(XT[:, d, :], XT[:, d, :], ps[:, 2 + d % 4, :], ALU.add).then_inc(acc_done, 1)

            def step(g, i=None):
                for e in range(GROUP):
                    low_up(g, e, i)
                    if e < 2:
                        low_down(g + 1, e + 2, i)
                    weigh(g + 1, e, i)
                if g < 30:
                    for e in range(2):
                        low_down(g + 2, e, i)
                accumulate(g, i)

            dve.wait_ge(x_hi, 1)
            v.tensor_tensor(XL, XN, XH.bitcast(f32), ALU.subtract).then_inc(x_lo, 1)
            for e in range(2):
                low_down(0, e)
            for e in range(GROUP):
                if e < 2:
                    low_down(0, e + 2)
                weigh(0, e)
            for e in range(2):
                low_down(1, e)
            dve.wait_ge(ada_turned, 1)
            for bank, a, b in ((6, 0, 16), (7, 16, 24)):
                last = v.tensor_tensor(mod[:, a:b], ps[:, bank, a:b], param("b_ada")[:, a:b], ALU.add)
            link(last)
            link(v.scalar_tensor_tensor(g_eff, mod[:, 8:16], 1.0, param("g_pre"), ALU.add, ALU.mult))
            with dve.Fori(0, 15) as i:
                for g in range(2):
                    step(g, i)
            step(30)
            for e in range(GROUP):
                low_up(31, e)
            accumulate(31)

            dve.wait_ge(acc_done, 8 * 32 + 8)
            norm(2, XT, XT, param("final_norm_w"), final_part)
            dve.wait_ge(final_part, KT)
            link(norm(3, XT, XN, g_eff))
            for k in range(KT):
                v.tensor_scalar(XN[:, k, :], XN[:, k, :], mod[:, k:k + 1], None, ALU.add).then_inc(norm_part, 1)
            n0 = STREAM["w_in_2"]
            for t in range(2):
                tile_low(n0, t, W_HI2)
            for k in range(KT):
                x_low(X_IN2, k, XN, X_HI2, X_LO)
            with dve.Fori(0, 4) as i:
                for u in range(8):
                    tile_low(n0, 2 + u, W_HI2, i)
            for t in range(34, IN2_TILES):
                tile_low(n0, t, W_HI2)

            dve.wait_ge(xc_ready, 64)
            dve.wait_ge(tile_done, STREAM["v_tok"] + 4)
            for kv in range(2):
                for m in range(16):
                    last = v.tensor_scalar(CB[:, kv, m, :].rearrange("p (g n) -> p g n", g=2),
                                           XC[:, kv, :, 2 * m:2 * m + 16 * (NC_CMP - 1) + 1:16],
                                           param("pe_k" if kv == 0 else "pe_v")[:, m:m + 1], None, ALU.add)
                last.then_inc(cb_ready, 1)

            def scale(u):
                kind, h = UNITS[u]
                par = u % 3
                slope = 2.0 ** -(h + 1) / NSA_SCALE
                dve.wait_ge(at_scored, u + 1)
                if u >= 3:
                    dve.wait_ge(at_turned, CHUNKS[u - 2])
                for i in range(TT):
                    w, k0 = key_cols(kind, i)
                    if kind == "cmp":
                        bias = const("cmp")[:, i * NC_CMP:(i + 1) * NC_CMP]
                    elif kind == "swa":
                        bias = const("window")[:, 2 * P - w:2 * P]
                    else:
                        bias = const("alibi")[:, S - w:S]
                    last = v.scalar_tensor_tensor(SS[:, par, i, 0:w], bias, slope, ps[:, i, 0:w], ALU.mult, ALU.add)
                last.then_inc(at_read, 1)
                dve.wait_ge(at_read, u + 1)
                for i in range(TT):
                    w, _ = key_cols(kind, i)
                    last = v.tensor_reduce(mx[:, par, i:i + 1], SS[:, par, i, 0:w], AX.X, ALU.max)
                link(last)
                if kind == "swa":
                    link(v.tensor_scalar(mx[:, par, :], mx[:, par, :], NSA_SCALE, param("sinks")[:, h:h + 1],
                                         ALU.mult, ALU.max))
                    v.tensor_scalar(nm[:, par, :], mx[:, par, :], -1.0, None, ALU.mult).then_inc(at_scaled, 1)
                else:
                    v.tensor_scalar(nm[:, par, :], mx[:, par, :], -NSA_SCALE, None, ALU.mult).then_inc(at_scaled, 1)

            def factors(u):
                kind, h = UNITS[u]
                par = u % 3
                dve.wait_ge(at_exp, u + 1)
                if kind == "swa":
                    link(v.tensor_tensor(den[:, par, :], den[:, par, :], esink[:, par, :], ALU.add))
                    v.reciprocal(fac[:, par, :], den[:, par, :]).then_inc(at_fac, 1)
                    return
                link(v.reciprocal(fac[:, par, :], den[:, par, :]))
                b = ("cmp", "slc", "win").index(kind) * 8 + h
                if kind == "cmp":
                    link(v.tensor_tensor(fac[:, par, :], fac[:, par, :], const("seen"), ALU.mult))
                v.tensor_tensor(fac[:, par, :], fac[:, par, :], gn[:, :, b], ALU.mult).then_inc(at_fac, 1)

            def gate_out_tile(u):
                kind, h = UNITS[u]
                if h % 2 == 1 and kind in ("win", "swa"):
                    t = h // 2 + (4 if kind == "swa" else 0)
                    dve.wait_ge(at_out, u + 1)
                    v.tensor_tensor(QA[:, t, :], ps[:, 6 + t % 2, :], ZZ[:, t, :], ALU.mult).then_inc(o_ready, 1)

            dve.wait_ge(v_ready, 4)
            no = STREAM["o_nsa"]
            for t in range(2):
                tile_low(no, t, W_HI3)
            scale(0)
            scale(1)
            factors(0)
            for u in range(len(UNITS)):
                if u + 2 < len(UNITS):
                    scale(u + 2)
                if u + 1 < len(UNITS):
                    factors(u + 1)
                if u >= 2:
                    gate_out_tile(u - 2)
                if u - 6 in OUT_UNITS:
                    x_low(X_ATTN, OUT_UNITS.index(u - 6), QA, O_HI, O_LO)
            gate_out_tile(len(UNITS) - 2)
            gate_out_tile(len(UNITS) - 1)
            for t in range(sum(w + 6 < len(UNITS) for w in OUT_UNITS), 8):
                x_low(X_ATTN, t, QA, O_HI, O_LO)
            for t in range(8):
                dve.wait_ge(tile_done, no + t + 1)
                for d in (2 * t, 2 * t + 1):
                    v.tensor_tensor(GT2[:, d, :], GT2[:, d, :], ps[:, (129 + d) % 4, :], ALU.mult)\
                        .then_inc(bank_free[(129 + d) % 4], 1)
                tile_low(no, t + 2, W_HI3)
                if t >= 4:
                    for d in range(2 * (t - 4), 2 * (t - 3)):
                        x_low(X_MERGED2, d, XN, M_HI2, X_LO)
            for t in range(10, OUT_TILES):
                tile_low(no, t, W_HI3)
            norm(4, ZZ, ZZ, param("g_post")).then_inc(norm_done, 1)
            dve.wait_ge(norm_done, 2)
            for k in range(KT):
                last = v.scalar_tensor_tensor(XT[:, k, :], ZZ[:, k, :], mod[:, 16 + k:17 + k], XT[:, k, :],
                                              ALU.mult, ALU.add)
            last.then_inc(out_ready, 1)

        @block.tensor
        def _(pe):
            def mm(o, lhsT, rhs, start=True, stop=True):
                return nc.tensor.matmul(o, lhsT, rhs, start=start, stop=stop, skip_group_check=True)

            def weights(n):
                pe.wait_ge(w_loaded[n % RING], 16 * (n // RING + 1))
                return ring[:, n % RING, :]

            def project(n, m, x):
                w = weights(n)
                pe.wait_ge(bank_free[m % 4], m // 4)
                for k in range(KT):
                    last = mm(ps[:, m % 4, :], w[:, k * P:(k + 1) * P], x[:, k, :], k == 0, k == KT - 1)
                last.then_inc(tile_done, 1)

            def three(o, wh, wl, xh, xl, first, last):
                mm(o, wh, xh, first, False)
                mm(o, wh, xl, False, False)
                return mm(o, wl, xh, False, last)

            def project_split(n0, t, m, j, wh, x, i=None):
                s = (n0 + t) % RING
                pe.wait_ge(tile_lo, nth((SPLIT_BEFORE[n0] + t + 1, 8), i))
                if m >= 4:
                    pe.wait_ge(bank_free[m % 4], m // 4 if i is None else i * 2 + m // 4)
                for k in range(KT):
                    if i is None:
                        pe.wait_ge(xn_lo, 8 * j + k + 1)
                    ks = slice(k * P, (k + 1) * P)
                    last = three(ps[:, m % 4, :], wh[:, t % 2, ks], RING_LO[:, s, ks], x[0][:, k, :], x[1][:, k, :],
                                 k == 0, k == KT - 1)
                last.then_inc(tile_done, 1)

            def project_half(n, m, x):
                w = weights(n)
                for o in range(2):
                    pe.wait_ge(bank_free[(m + o) % 4], (m + o) // 4)
                    for k in range(4):
                        last = mm(ps[:, (m + o) % 4, :], w[:, o * 512 + k * P:o * 512 + (k + 1) * P],
                                  x[:, k, :], k == 0, k == 3)
                last.then_inc(tile_done, 1)

            def project_half_split(n0, t, m, k0):
                s = (n0 + t) % RING
                pe.wait_ge(tile_lo, SPLIT_BEFORE[n0] + t + 1)
                for o in range(2):
                    pe.wait_ge(bank_free[(m + o) % 4], (m + o) // 4)
                    for k in range(4):
                        pe.wait_ge(xn_lo, 8 * X_ATTN + k0 + k + 1)
                        ks = slice(o * 512 + k * P, o * 512 + (k + 1) * P)
                        last = three(ps[:, (m + o) % 4, :], W_HI3[:, t % 2, ks], RING_LO[:, s, ks],
                                     O_HI[:, k0 + k, :], O_LO[:, k0 + k, :], k == 0, k == 3)
                last.then_inc(tile_done, 1)

            def sum_squares(j, sq):
                for k in range(KT):
                    pe.wait_ge(norm_sq, 8 * j + k + 1)
                    for c in range(TT):
                        last = mm(ps[:, NORM_BANK[j], c:c + 1], sq[:, k, c * P:(c + 1) * P], ones[:, 0:1],
                                  k == 0 and c == 0, k == KT - 1)
                last.then_inc(norm_ss, 1)
                pe.wait_ge(norm_diag, j + 1)
                mm(ps[:, 7, :], ones, RS[:, :]).then_inc(norm_bc, 1)

            pe.wait_ge(par_loaded, 32)
            sum_squares(0, XN)
            n0 = STREAM["w_in"]
            for m in range(4):
                project_split(n0, m, m, X_IN, W_HI1, (X_HI1, X_LO))
            with pe.Fori(0, 6) as i:
                for u in range(8):
                    project_split(n0, 4 + u, 4 + u, X_IN, W_HI1, (X_HI1, X_LO), i)
            pe.wait_ge(pool_ready, 1)
            for g in range(4):
                mm(ps[:, 4 + g, :], param("pool_w")[:, g * P:(g + 1) * P], XA[:, g, 16:]).then_inc(pooly_done, 1)
            pe.wait_ge(yt_ready, 4)
            for u in range(4):
                project_half(STREAM["pool_up"] + u, 52 + 2 * u, XA[:, :, 16:])
            pe.wait_ge(ba_lo, 1)
            for c in range(TT):
                cs = slice(c * P, (c + 1) * P)
                for k in range(KT):
                    ks = slice(k * 16, (k + 1) * 16)
                    last = three(ps[:, 4, c * 16:(c + 1) * 16], X_HI1[:, k, cs], X_LO[:, k, cs], BA_HI[:, ks],
                                 BA_LO[:, ks], k == 0, k == KT - 1)
            last.then_inc(ba_done, 1)
            pe.wait_ge(ba_v, 2)
            mm(ps[:, 5, 0:TT * 8], upper, g_log.rearrange("p c h -> p (c h)")).then_inc(gc_done, 1)
            pe.wait_ge(gc_ready, 1)

            for r in range(HEADS // 2):
                def each(fn):
                    for p in range(2):
                        fn(p, 2 * r + p, slots[p], 4 * p)

                def sumsq(p, h, s, b):
                    pe.wait_ge(dA[p].sem, dA[p].done(r, "sq"))
                    for x in range(8):
                        last = mm(ps[:, b, x:x + 1], s.sq[:, x // 4, (x % 4) * P:(x % 4 + 1) * P], ones[:, 0:1])
                    last.then_inc(dT[p].sem, 1)

                def spread(p, h, s, b):
                    pe.wait_ge(dV[p].sem, dV[p].done(r, "rd"))
                    mm(ps[:, b, :], ones, s.sq[:, 0, :])
                    mm(ps[:, b + 1, :], ones, s.sq[:, 1, :]).then_inc(dT[p].sem, 1)

                def four(bank, lhsT, rhs=None):
                    for c in range(TT):
                        o = ps[:, bank, c * P:(c + 1) * P]
                        last = mm(o, lhsT(c), rhs(c)) if rhs else nc.tensor.transpose(o, lhsT(c), ident)
                    return last

                def turn(p, h, s, b):
                    pe.wait_ge(dV[p].sem, dV[p].done(r, "norm"))
                    four(b, lambda c: QKV[:, 8 + h, c * P:(c + 1) * P])
                    four(b + 1, lambda c: QKV[:, 16 + h, c * P:(c + 1) * P])\
                        .then_inc(dT[p].sem, 1)
                    four(b + 2, lambda c: QKV[:, 8 + h, c * P:(c + 1) * P], lambda c: QKV[:, 8 + h, c * P:(c + 1) * P])
                    four(b + 3, lambda c: QKV[:, 8 + h, c * P:(c + 1) * P], lambda c: QKV[:, h, c * P:(c + 1) * P])\
                        .then_inc(dT[p].sem, 1)

                def decay(p, h, s, b):
                    pe.wait_ge(dV[p].sem, dV[p].done(r, "gu"))
                    pe.wait_ge(dA[p].sem, dA[p].done(r, "ktok"))
                    mm(ps[:, b, :], ones, s.gu.rearrange("p c t -> p (c t)")).then_inc(dT[p].sem, 1)

                def lt(p, h, s, b):
                    pe.wait_ge(dV[p].sem, dV[p].done(r, "l"))
                    four(b + 1, lambda c: s.ed[:, c, :]).then_inc(dT[p].sem, 1)

                def t1(p, h, s, b):
                    pe.wait_ge(dV[p].sem, dV[p].done(r, "tt"))
                    pe.wait_ge(dA[p].sem, dA[p].done(r, "lts"))
                    four(b, lambda c: s.tt[:, c, :]).then_inc(dT[p].sem, 1)

                for fn in (sumsq, spread, turn, decay, lt, t1):
                    each(fn)
                for l in range(1, LEVELS):
                    def lx(p, h, s, b):
                        pe.wait_ge(dG[p].sem, dG[p].done(r, f"lk{l}"))
                        pe.wait_ge(dV[p].sem, dV[p].done(r, "t" if l == 1 else f"u{l - 1}"))
                        four(b, lambda c: s.lk[:, c, :], lambda c: s.t[:, c, :]).then_inc(dT[p].sem, 1)

                    def tx(p, h, s, b):
                        pe.wait_ge(dA[p].sem, dA[p].done(r, f"x{l}"))
                        for c in range(TT):
                            if l < LEVELS - 1:
                                mm(ps[:, b + 2, c * 64:(c + 1) * 64], s.tt[:, c, :], pair_side(s.x[:, c, :], l, 0))
                        for c in range(TT):
                            last = mm(ps[:, b + 3, c * 64:(c + 1) * 64], s.x[:, c, :], pair_side(s.tt[:, c, :], l, 1))
                        last.then_inc(dT[p].sem, 1)

                    each(lx)
                    each(tx)
                for c in range(TT):
                    def pq(p, h, s, b):
                        pe.wait_ge(dV[p].sem, dV[p].done(r, f"o{c - 1}"))
                        mm(ps[:, b, 0:P], QKV[:, 8 + h, c * P:(c + 1) * P], s.state)
                        mm(ps[:, b, P:2 * P], QKV[:, h, c * P:(c + 1) * P], s.state).then_inc(dT[p].sem, 1)

                    def vnew(p, h, s, b):
                        pe.wait_ge(dV[p].sem, dV[p].done(r, f"r{c}" if c else f"u{LEVELS - 1}"))
                        mm(ps[:, b + 1, 0:P], s.tt[:, c, :], s.r if c else s.vb[:, 0, :]).then_inc(dT[p].sem, 1)

                    def outs(p, h, s, b):
                        pe.wait_ge(dA[p].sem, dA[p].done(r, f"vn{c}"))
                        pe.wait_ge(dG[p].sem, dG[p].done(r, "kdec"))
                        last = mm(ps[:, b + 1, P:2 * P], s.et[:, c, :], s.vn)
                        if c < TT - 1:
                            last = mm(ps[:, b + 1, 2 * P:3 * P], s.kt[:, c, :], s.vn)
                        last.then_inc(dT[p].sem, 1)

                    for fn in ((pq,) if c else ()) + (vnew, outs):
                        each(fn)

                def turn_o(p, h, s, b):
                    pe.wait_ge(dV[p].sem, dV[p].done(r, "dg"))
                    four(b + 2, lambda c: s.t[:, c, :], lambda c: s.lk[:, c, :]).then_inc(dT[p].sem, 1)

                each(turn_o)

            for p in range(2):
                pe.wait_ge(dV[p].sem, dV[p].done(3, "fin"))
            for u in range(8):
                project_split(STREAM["dn_up"], u, 60 + u, X_DELTA, W_HID, (Z_HI, Z_LO))
            for u in range(8, 16):
                project_split(STREAM["dn_up"], u, 60 + u, X_MERGED, W_HID, (M_HI1, X_LO))
            sum_squares(1, SQ1)
            pe.wait_ge(norm_done, 1)
            pe.wait_ge(keys_loaded, 16)
            for hz in range(17):
                if hz < 16:
                    project(STREAM["query"] + hz, 76 + hz, XN)
                if hz:
                    q = hz - 1
                    pe.wait_ge(bank_free[(76 + q) % 4], (76 + q) // 4 + 1)
                    if q >= 4:
                        pe.wait_ge(sc_ready, q - 3)
                    for c in range(TT):
                        last = mm(ps[:, 4 + q % 4, c * P:(c + 1) * P], QP[:, q, c * P:(c + 1) * P], keys[:, q, :])
                    last.then_inc(sc_done, 1)
            for z, bank in ((0, 4), (1, 5)):
                for c in range(TT):
                    pe.wait_ge(sel_ready, 8)
                    last = nc.tensor.transpose(ps[:, bank, c * P:(c + 1) * P], SEL[:, z, c, :], ident)
                last.then_inc(turned, 1)
            pe.wait_ge(gate_ready, 1)
            for c in range(TT):
                last = nc.tensor.transpose(ps[:, 6, c * P:(c + 1) * P], TOP[:, c, :, :].rearrange("p h k -> p (h k)"), ident)
            last.then_inc(turned, 1)
            pe.wait_ge(turned_read, 3)
            def gate_tokens(j):
                for u in range(16):
                    if u % 4 == 0:
                        pe.wait_ge(gate_out, j * 4 + (u // 4 + 1))
                        pe.wait_ge(gated_a, j * 4 + (u // 4 + 1))
                        pe.wait_ge(onehot_b, j * 4 + (u // 4 + 1))
                    mm(ps[:, 4 + u // 4, (u % 4) * P:(u % 4 + 1) * P], ONE_B[:, u, :], ONE_A[:, u, :])\
                        .then_inc(token_mm, 1)

            for b in range(4):
                pe.wait_ge(bank_free[b], 23)
            for t in range(24):
                w = weights(STREAM["ada"] + t)
                p0 = ADA_PART[t // 16]
                for k in range(KT):
                    last = mm(ps[p0:p0 + 1, t // 4 % 4, (t % 4) * P:(t % 4 + 1) * P], param("c")[:, k:k + 1],
                              w[:, k * P:(k + 1) * P], k == 0, k == KT - 1)
                last.then_inc(tile_done, 1)
                gate_tokens(t)
            with pe.Fori(24, S // 16) as j:
                gate_tokens(j)

            def hidden(g, i=None):
                for e in range(GROUP):
                    pe.wait_ge(split_lo, nth((8 * (g - 1) + SPLIT_D[e] + 1 if g else e + 1, 16), i))
                    if g or e >= 2:
                        pe.wait_ge(gelu_done, nth((4 * g + e - 1, 8), i))
                    for k in range(KT):
                        ks = slice(k * P, (k + 1) * P)
                        last = three(ps[:, e % 2, :], DH[:, e % 2, ks], DL[:, e % 2, ks], XH[:, k, :], XL[:, k, :],
                                     k == 0, k == KT - 1)
                    last.then_inc(tile_done, 1)

            def expert_out(g, i=None):
                pe.wait_ge(split_lo, nth((8 * g + SPLIT_U[3] + 1 if g < 31 else 256, 16), i))
                pe.wait_ge(w_done, nth((4 * g + 4, 8), i))
                for d in range(KT):
                    pe.wait_ge(acc_done, nth((8 * g + d + 5, 16), i))
                    dd = slice(d * P, (d + 1) * P)
                    for e in range(GROUP):
                        last = three(ps[:, 2 + d % 4, :], UH[:, e, dd], UL[:, e, dd], WH[:, g % 2, e, :],
                                     WL[:, g % 2, e, :], e == 0, e == GROUP - 1)
                        if d == KT - 1:
                            last.then_inc(tile_done, 1)
                    if d < KT - 1:
                        last.then_inc(y_done, 1)

            hidden(0)
            pe.wait_ge(ada_rows, 1)
            for t in range(24):
                p0 = ADA_PART[t // 16]
                last = mm(ps[:, 6 + t // 16, t:t + 1], ADA_ROWS[p0:p0 + 1, (t % 16) * P:(t % 16 + 1) * P], ones[p0:p0 + 1, 0:1])
            last.then_inc(ada_turned, 1)
            with pe.Fori(0, 15) as i:
                for g in range(2):
                    hidden(g + 1, i)
                    expert_out(g, i)
            hidden(31)
            expert_out(30)
            expert_out(31)
            for j in (2, 3):
                sum_squares(j, XN)
            n0 = STREAM["w_in_2"]
            for t in range(5):
                project_split(n0, t, 92 + t, X_IN2, W_HI2, (X_HI2, X_LO))
            with pe.Fori(0, 4) as i:
                for u in range(8):
                    project_split(n0, 5 + u, 97 + u, X_IN2, W_HI2, (X_HI2, X_LO), i)
            for j in range(4):
                t, n = 37 + j, STREAM["v_tok"] + j
                pe.wait_ge(tile_lo, SPLIT_BEFORE[n0] + t + 1)
                for c in range(TT):
                    cs = slice(c * P, (c + 1) * P)
                    for k in range(2):
                        ws = slice(k * 512, k * 512 + 408)
                        last = three(ps[:, 4 + c, 0:408], X_HI2[:, 2 * j + k, cs], X_LO[:, 2 * j + k, cs],
                                     W_HI2[:, t % 2, ws], RING_LO[:, n % RING, ws], j == 0 and k == 0,
                                     j == 3 and k == 1)
                last.then_inc(tile_done, 1)
            for kv in range(2):
                pe.wait_ge(cb_ready, kv + 1)
                pe.wait_ge(v_ready, 4)
                for m in range(16):
                    w = weights(STREAM["cmp_k1" if kv == 0 else "cmp_v1"] + m // 4)
                    for a in range(2):
                        last = mm(ps[:, 4 + 2 * kv + a, 0:62], w[:, (m % 4) * 256 + a * P:(m % 4) * 256 + (a + 1) * P],
                                  CB[:, kv, m, :], m == 0, m == 15)
                    if m % 4 == 3:
                        last.then_inc(tile_done, 1)
            pe.wait_ge(hid_ready, 2)
            for b in range(4):
                pe.wait_ge(bank_free[b], (129 - b + 3) // 4)
            for half in range(2):
                for a in range(2):
                    mm(ps[half * 64:(half + 1) * 64, 0, 0:62], param("w_cmp_k2")[:, a * 64:(a + 1) * 64],
                       HID[:, 0, a, :], a == 0, a == 1)
            for g in range(2):
                for a in range(2):
                    last = mm(ps[0:NC_CMP, 1, g * 64:(g + 1) * 64], HID[:, 1, a, g * NC_CMP:(g + 1) * NC_CMP],
                              param("w_cmp_v2")[:, a * 64:(a + 1) * 64], a == 0, a == 1)
            last.then_inc(kv_done, 1)
            pe.wait_ge(kc_ready, 1)
            pe.wait_ge(dup_done, 64)

            def scores(u):
                kind, h = UNITS[u]
                if u:
                    pe.wait_ge(at_read, u)
                p0, t = 64 * (h % 2), h // 2 + (4 if kind == "swa" else 0)
                for i in range(TT):
                    q = QA[p0:p0 + 64, t, i * P:(i + 1) * P]
                    w, k0 = key_cols(kind, i)
                    if kind == "cmp":
                        k = KC[p0:p0 + 64, (h // 4) * NC_CMP:(h // 4 + 1) * NC_CMP]
                    else:
                        k = KD[p0:p0 + 64, ("slc", "win", "swa").index(kind), h // 4, k0:k0 + w]
                    last = mm(ps[:, i, 0:w], q, k)
                last.then_inc(at_scored, 1)

            def turn_probs(u):
                kind, h = UNITS[u]
                pe.wait_ge(at_weighted, u + 1)
                for x, (kt, tiles) in enumerate(turns(kind)):
                    chunk = CHUNKS[u] + x
                    if chunk >= 2:
                        pe.wait_ge(at_copied, chunk - 1)
                    for i in tiles:
                        w, k0 = key_cols(kind, i)
                        a = kt * P - k0
                        m = NC_CMP if kind == "cmp" else P
                        last = nc.tensor.transpose(ps[0:m, 4 + chunk % 2, i * P:(i + 1) * P],
                                                   SS[:, u % 3, i, a:a + m], ident)
                    last.then_inc(at_turned, 1)

            def values(u):
                kind, h = UNITS[u]
                par, p0, t = u % 2, 64 * (h % 2), h // 2 + (4 if kind == "swa" else 0)
                pe.wait_ge(at_copied, CHUNKS[u + 1])
                if h % 2 == 0 and kind in ("cmp", "swa") and t >= 2:
                    pe.wait_ge(o_ready, t - 1)
                o = ps[p0:p0 + 64, 6 + t % 2, :]
                if kind == "cmp":
                    last = mm(o, VC[0:NC_CMP, h // 4, :], PT[0:NC_CMP, par, 0, :], True, False)
                elif kind == "swa":
                    for i in range(TT):
                        for kt in range(max(0, i - 1), i + 1):
                            v = VT[:, kt, 256 + (h // 4) * 64:256 + (h // 4 + 1) * 64]
                            last = mm(o[:, i * P:(i + 1) * P], v, PT[:, par, kt, i * P:(i + 1) * P],
                                      kt == max(0, i - 1), kt == i)
                else:
                    b = 0 if kind == "slc" else 128
                    for kt in range(TT):
                        v = VT[:, kt, b + (h // 4) * 64:b + (h // 4 + 1) * 64]
                        last = mm(o[:, kt * P:], v, PT[:, par, kt, kt * P:], False, kind == "win" and kt == TT - 1)
                last.then_inc(at_out, 1)

            scores(0)
            scores(1)
            for u in range(len(UNITS)):
                if u + 2 < len(UNITS):
                    scores(u + 2)
                turn_probs(u)
                if u:
                    values(u - 1)
            values(len(UNITS) - 1)
            pe.wait_ge(o_ready, 8)
            no = STREAM["o_nsa"]
            for u in range(8):
                project_half_split(no, u, 129 + 2 * u, 0 if u < 4 else 4)
            for u in range(8):
                project_split(no, 8 + u, 145 + u, X_MERGED2, W_HI3, (M_HI2, X_LO))
            sum_squares(4, SQ1)


def shape_constants():
    p, j = np.arange(P)[:, None], np.arange(P)[None, :]
    parts = {
        "ident": p == j,
        "ones": np.ones((P, P)),
        "upper": p <= j,
        "iota": np.broadcast_to(j, (P, P)),
        "strict": j < p,
        "block": np.concatenate([(j >> l & 1 == 1) & (p >> l & 1 == 0) & (j >> l + 1 == p >> l + 1)
                                 for l in range(LEVELS)], axis=1),
    }
    x = np.arange(S)[None, :]
    dist = p + S - P - x
    parts["alibi"] = np.where(dist >= 0, -dist, -1e30)
    dist = P + p - np.arange(2 * P)[None, :]
    parts["window"] = np.where((dist >= 0) & (dist < P), -dist, -1e30)
    t = np.arange(TT)[None, :, None] * P + p[:, :, None]
    dist = t - (np.arange(NC_CMP)[None, None, :] * 16 + 31)
    parts["cmp"] = np.where(dist >= 0, -dist, -1e30).reshape(P, -1)
    parts["seen"] = (t[:, :, 0] >= 31)
    n = np.arange(16)[None, :] + 1
    first = 1.0 / np.minimum(n, 2.0 ** (np.arange(4)[:, None] + 1))
    parts["eps"] = np.broadcast_to([[EPS, D * EPS]], (P, 2))
    parts["first"] = np.broadcast_to(first.reshape(1, 64), (P, 64))
    return np.concatenate([np.asarray(parts[k], np.float32) for k in CONST], axis=1)


def by_feature(v):
    return v.reshape(-1, P).T


def tiles(w):
    return w.reshape(KT, P, -1, P).transpose(2, 1, 0, 3).reshape(-1, P, 1024)


def half_tiles(w):
    return w.reshape(4, P, 8, P).transpose(2, 1, 0, 3).reshape(4, 2, P, 512).transpose(0, 2, 1, 3).reshape(4, P, 1024)


def lay_out(inputs):
    a = {k: np.asarray(v) for k, v in inputs.items()}
    one = {k: v[0] for k, v in a.items()}
    w, w2 = one["w_in"], one["w_in_2"]
    down = one["peer_down"].reshape(P, P, KT, P).transpose(0, 3, 2, 1).reshape(32, GROUP, P, 1024)
    up = one["peer_up"].reshape(32, GROUP, P, 1024)
    experts = [down[0]]
    for g in range(31):
        experts += [down[g + 1], up[g]]
    experts.append(up[31])
    v_tok = np.concatenate([w2[:, 896:1024], w2[:, 1152:1280], w2[:, 2456:2584], w2[:, 1280:1304],
                            np.zeros((1024, 104), np.float32)], axis=1)
    cmp_tiles = lambda m: m.reshape(4, 4, P, 256).transpose(0, 2, 1, 3).reshape(4, P, 1024)
    stream = np.concatenate([
        tiles(w[:, 0:4608]), tiles(w[:, 4624:6672]), half_tiles(one["w_pool_up"]), tiles(one["w_dn_up"]),
        tiles(one["w_mix_out"]), tiles(one["peer_w_query"]), tiles(one["w_ada_2"]), *experts,
        tiles(w2[:, 0:512]), tiles(w2[:, 1816:2328]), tiles(w2[:, 1304:1816]), tiles(w2[:, 2584:3096]),
        tiles(w2[:, 3096:5144]), tiles(w2[:, 512:768]), tiles(w2[:, 768:896]), tiles(w2[:, 1024:1152]),
        tiles(w2[:, 2328:2456]),
        v_tok.reshape(4, 2, P, 512).transpose(0, 2, 1, 3).reshape(4, P, 1024),
        cmp_tiles(one["w_cmp_k1_2"]), cmp_tiles(one["w_cmp_v1_2"]),
        half_tiles(one["w_o_nsa_2"]), half_tiles(one["w_o_swa_2"]), tiles(one["w_out_2"])])
    rows = lambda v: np.broadcast_to(v.reshape(1, -1), (P, v.size))
    params = {
        "mix_norm_w": by_feature(one["mix_norm_w"]),
        "conv_w": one["conv_w"].reshape(4, 24, P).transpose(2, 1, 0).reshape(P, 96),
        "pool_scale": by_feature(one["pool_scale"]),
        "a_log": rows(one["a_log"]), "dt_bias": rows(one["dt_bias"]),
        "dn_norm_w": one["dn_norm_w"].reshape(P, 1),
        "ffn_norm_w": by_feature(one["ffn_norm_w"]), "final_norm_w": by_feature(a["final_norm_w"]),
        "c": by_feature(one["c_2"]), "b_ada": by_feature(one["b_ada_2"]),
        "g_pre": by_feature(one["g_pre_2"]), "g_post": by_feature(one["g_post_2"]),
        "sinks": rows(one["sinks_2"]),
        "pe_k": one["pe_cmp_k_2"].reshape(16, P).T, "pe_v": one["pe_cmp_v_2"].reshape(16, P).T,
        "pool_w": one["pool_w"].transpose(1, 0, 2).reshape(P, 512),
        "w_ba": w[:, 4608:4624].reshape(KT, P, 16).transpose(1, 0, 2).reshape(P, 128),
        "w_cmp_k2": one["w_cmp_k2_2"].reshape(2, P, 64).transpose(1, 0, 2).reshape(P, 128),
        "w_cmp_v2": one["w_cmp_v2_2"].reshape(2, P, 64).transpose(1, 0, 2).reshape(P, 128),
    }
    both = np.stack([one["peer_keys_1"], one["peer_keys_2"]], axis=1)
    return {
        "x_in": one["x"].T.reshape(KT, P, S).transpose(1, 0, 2).reshape(P, KT * S),
        "stream": stream,
        "params": np.concatenate([params[k] for k in PARAM], axis=1),
        "consts": shape_constants(),
        "keys": both.transpose(3, 0, 1, 2).reshape(P, 2048),
    }


def kernel(**inputs):
    import concourse.bacc as bacc
    from concourse.bass_utils import run_bass_kernel_spmd

    nc = bacc.Bacc("TRN2", target_bir_lowering=False, num_devices=1)
    arrays = {k: np.ascontiguousarray(v) for k, v in lay_out(inputs).items()}
    aps = [nc.dram_tensor("dram_" + k, v.shape, mybir.dt.float32, kind="ExternalInput").ap() for k, v in arrays.items()]
    out = nc.dram_tensor("dram_out", [P, KT * S], mybir.dt.float32, kind="ExternalOutput").ap()
    program(nc, *aps, out)
    got = run_bass_kernel_spmd(nc, [{"dram_" + k: v for k, v in arrays.items()}], core_ids=[0]).results[0]["dram_out"]
    return got.reshape(P, KT, S).transpose(2, 1, 0).reshape(1, S, D)
```
